# Optimizing a Trainium2 kernel written in Bass

```python
import math
import jax, jax.numpy as jnp
from jax import lax
import numpy as np

D_MODEL = 1024
BATCH = 1
SEQ = 256
DEPTH = 2

CHUNK = 64
Q_BLOCK = 128
PLE_DIM = 256
ROPE_THETA = 10000.0
EPS = 1e-6

MLA_HEADS = 8
MLA_NOPE_DIM = 64
MLA_ROPE_DIM = 32
MLA_QK_DIM = MLA_NOPE_DIM + MLA_ROPE_DIM
MLA_V_DIM = 64
MLA_Q_RANK = 256
MLA_KV_RANK = 128

DIFF_HEADS = 4
DIFF_HEAD_DIM = 64
DIFF_V_DIM = 2 * DIFF_HEAD_DIM

MIX_WIDTH = MLA_HEADS * MLA_V_DIM + DIFF_HEADS * DIFF_V_DIM

IN_SPLITS = (MLA_Q_RANK, MLA_KV_RANK, MLA_ROPE_DIM,
             DIFF_HEADS * 2 * DIFF_HEAD_DIM, DIFF_HEADS * 2 * DIFF_HEAD_DIM,
             DIFF_HEADS * DIFF_V_DIM)
IN_WIDTH = sum(IN_SPLITS)

N_GROUPS = 4
EXPERTS_PER_GROUP = 8
TOP_K_IN_GROUP = 2
EXPERT_FF = 256

kernel_name = "hymba_mla_diffattn_hier_moe_ple"

def rms_norm(x, g):
    xf = x.astype(jnp.float32)
    y = xf * lax.rsqrt(jnp.mean(xf * xf, axis=-1, keepdims=True) + EPS)
    return (y * g.astype(jnp.float32)).astype(x.dtype)

def rope_tables(positions, dim):
    inv_freq = ROPE_THETA ** (-jnp.arange(0, dim, 2, dtype=jnp.float32) / dim)
    ang = positions.astype(jnp.float32)[..., None] * inv_freq
    return jnp.cos(ang)[:, :, None, :], jnp.sin(ang)[:, :, None, :]

def apply_rope(x, cos, sin):
    xf = x.astype(jnp.float32)
    x1, x2 = jnp.split(xf, 2, axis=-1)
    out = jnp.concatenate([x1 * cos - x2 * sin, x2 * cos + x1 * sin], axis=-1)
    return out.astype(x.dtype)

def chunk_causal_attention(q, k, v, scale):
    B, H, S, dk = q.shape
    dv = v.shape[-1]
    nb = S // Q_BLOCK
    qb = q.reshape(B, H, nb, Q_BLOCK, dk).transpose(2, 0, 1, 3, 4)
    k_chunk = jnp.arange(S) // CHUNK

    def block(args):
        qi, bi = args
        q_chunk = (bi * Q_BLOCK + jnp.arange(Q_BLOCK)) // CHUNK
        s = jnp.einsum('bhqd,bhkd->bhqk', qi, k).astype(jnp.float32) * scale
        s = jnp.where(k_chunk[None, :] <= q_chunk[:, None], s, jnp.float32(-1e30))
        pr = jax.nn.softmax(s, axis=-1).astype(v.dtype)
        return jnp.einsum('bhqk,bhkd->bhqd', pr, v)

    out = lax.map(block, (qb, jnp.arange(nb)))
    return out.transpose(1, 2, 0, 3, 4).reshape(B, H, S, dv)

def mla_group(c_q, c_kv, k_rope, cos, sin, q_a_norm, w_uq, kv_a_norm, w_ukv, q_norm, k_norm):
    B, S, _ = c_q.shape
    q = (rms_norm(c_q, q_a_norm) @ w_uq).reshape(B, S, MLA_HEADS, MLA_QK_DIM)
    kv = (rms_norm(c_kv, kv_a_norm) @ w_ukv).reshape(B, S, MLA_HEADS, MLA_NOPE_DIM + MLA_V_DIM)
    k_nope, v = kv[..., :MLA_NOPE_DIM], kv[..., MLA_NOPE_DIM:]
    k_pe = jnp.broadcast_to(k_rope[:, :, None, :], (B, S, MLA_HEADS, MLA_ROPE_DIM))
    k = jnp.concatenate([k_nope, k_pe], axis=-1)
    q = rms_norm(q, q_norm)
    k = rms_norm(k, k_norm)
    q = jnp.concatenate([q[..., :MLA_NOPE_DIM], apply_rope(q[..., MLA_NOPE_DIM:], cos, sin)], axis=-1)
    k = jnp.concatenate([k[..., :MLA_NOPE_DIM], apply_rope(k[..., MLA_NOPE_DIM:], cos, sin)], axis=-1)
    o = chunk_causal_attention(q.transpose(0, 2, 1, 3), k.transpose(0, 2, 1, 3),
                               v.transpose(0, 2, 1, 3), MLA_QK_DIM ** -0.5)
    return o.transpose(0, 2, 1, 3).reshape(B, S, MLA_HEADS * MLA_V_DIM)

def diff_group(q, k, v, cos, sin, q_norm, k_norm, lq1, lk1, lq2, lk2, subln, lambda_init):
    B, S, _ = q.shape
    q = apply_rope(rms_norm(q.reshape(B, S, 2 * DIFF_HEADS, DIFF_HEAD_DIM), q_norm), cos, sin)
    k = apply_rope(rms_norm(k.reshape(B, S, 2 * DIFF_HEADS, DIFF_HEAD_DIM), k_norm), cos, sin)
    v = v.reshape(B, S, DIFF_HEADS, DIFF_V_DIM).transpose(0, 2, 1, 3)
    v = jnp.repeat(v, 2, axis=1)
    o = chunk_causal_attention(q.transpose(0, 2, 1, 3), k.transpose(0, 2, 1, 3), v,
                               DIFF_HEAD_DIM ** -0.5)
    o = o.reshape(B, DIFF_HEADS, 2, S, DIFF_V_DIM)
    lam = (jnp.exp(jnp.sum(lq1.astype(jnp.float32) * lk1.astype(jnp.float32)))
           - jnp.exp(jnp.sum(lq2.astype(jnp.float32) * lk2.astype(jnp.float32)))
           + lambda_init)
    o = o[:, :, 0] - lam.astype(o.dtype) * o[:, :, 1]
    o = rms_norm(o, subln) * (1.0 - lambda_init)
    return o.transpose(0, 2, 1, 3).reshape(B, S, DIFF_HEADS * DIFF_V_DIM)

def hierarchical_moe(m, w_group, b_group, w_router, b_router, w_gate, w_up, w_down):
    B, S, D = m.shape
    t = m.reshape(-1, D)
    g_logits = (t @ w_group).astype(jnp.float32) + b_group.astype(jnp.float32)
    g_prob = jax.nn.softmax(g_logits, axis=-1)
    g_sel = jnp.argmax(g_logits, axis=-1)
    g_w = jnp.take_along_axis(g_prob, g_sel[:, None], axis=1)[:, 0]
    e_logits = ((t @ w_router).astype(jnp.float32) + b_router.astype(jnp.float32)).reshape(
        -1, N_GROUPS, EXPERTS_PER_GROUP)
    e_logits = jnp.take_along_axis(e_logits, g_sel[:, None, None], axis=1)[:, 0]
    top_v, top_i = lax.top_k(e_logits, TOP_K_IN_GROUP)
    e_w = jax.nn.softmax(top_v, axis=-1)
    in_group = jnp.einsum('tk,tke->te', e_w, jax.nn.one_hot(top_i, EXPERTS_PER_GROUP, dtype=jnp.float32))
    combine = (jax.nn.one_hot(g_sel, N_GROUPS, dtype=jnp.float32)[:, :, None]
               * (g_w[:, None] * in_group)[:, None, :]).astype(t.dtype)
    y = jnp.zeros_like(t)
    for g in range(N_GROUPS):
        h = jax.nn.silu(jnp.einsum('td,edf->tef', t, w_gate[g])) * jnp.einsum('td,edf->tef', t, w_up[g])
        y = y + jnp.einsum('tef,efd->td', h * combine[:, g, :, None], w_down[g])
    return y.reshape(B, S, D)

def setup_inputs(seed: int = 0) -> dict:
    key = jax.random.key(seed)
    ks = iter(jax.random.split(key, 40))
    f32 = jnp.float32

    def nrm(shape, scale):
        return jax.random.normal(next(ks), shape, f32) * scale

    def gain(shape):
        return 1.0 + 0.02 * jax.random.normal(next(ks), shape, f32)

    L, D = DEPTH, D_MODEL
    x = nrm((BATCH, SEQ, D), 1.0)
    p = nrm((DEPTH, BATCH, SEQ, PLE_DIM), 1.0)
    offset = jax.random.randint(next(ks), (BATCH, 1), 0, 64, dtype=jnp.int32) * CHUNK
    positions = (offset + jnp.arange(SEQ, dtype=jnp.int32)[None, :]).astype(jnp.int32)
    G, EP, F = N_GROUPS, EXPERTS_PER_GROUP, EXPERT_FF
    return {
        "x": x,
        "p": p,
        "positions": positions,
        "attn_norm": gain((L, D)),
        "w_in": nrm((L, D, IN_WIDTH), D ** -0.5),
        "q_a_norm": gain((L, MLA_Q_RANK)),
        "w_uq": nrm((L, MLA_Q_RANK, MLA_HEADS * MLA_QK_DIM), MLA_Q_RANK ** -0.5),
        "kv_a_norm": gain((L, MLA_KV_RANK)),
        "w_ukv": nrm((L, MLA_KV_RANK, MLA_HEADS * (MLA_NOPE_DIM + MLA_V_DIM)), MLA_KV_RANK ** -0.5),
        "mla_q_norm": gain((L, MLA_QK_DIM)),
        "mla_k_norm": gain((L, MLA_QK_DIM)),
        "diff_q_norm": gain((L, DIFF_HEAD_DIM)),
        "diff_k_norm": gain((L, DIFF_HEAD_DIM)),
        "lambda_q1": nrm((L, DIFF_HEAD_DIM), 0.1),
        "lambda_k1": nrm((L, DIFF_HEAD_DIM), 0.1),
        "lambda_q2": nrm((L, DIFF_HEAD_DIM), 0.1),
        "lambda_k2": nrm((L, DIFF_HEAD_DIM), 0.1),
        "diff_subln": gain((L, DIFF_V_DIM)),
        "w_out": nrm((L, MIX_WIDTH, D), MIX_WIDTH ** -0.5),
        "ffn_norm": gain((L, D)),
        "w_group": nrm((L, D, G), D ** -0.5),
        "b_group": nrm((L, G), 0.01),
        "w_router": nrm((L, D, G * EP), D ** -0.5),
        "b_router": nrm((L, G * EP), 0.01),
        "w_gate": nrm((L, G, EP, D, F), D ** -0.5),
        "w_up": nrm((L, G, EP, D, F), D ** -0.5),
        "w_down": nrm((L, G, EP, F, D), F ** -0.5),
        "ple_norm": gain((L, D)),
        "w_ple_gate": nrm((L, D, D), D ** -0.5),
        "w_ple_proj": nrm((L, PLE_DIM, D), PLE_DIM ** -0.5),
    }

def reference(x, p, positions, attn_norm, w_in, q_a_norm, w_uq, kv_a_norm, w_ukv,
              mla_q_norm, mla_k_norm, diff_q_norm, diff_k_norm,
              lambda_q1, lambda_k1, lambda_q2, lambda_k2, diff_subln, w_out,
              ffn_norm, w_group, b_group, w_router, b_router, w_gate, w_up, w_down,
              ple_norm, w_ple_gate, w_ple_proj):
    cos_mla, sin_mla = rope_tables(positions, MLA_ROPE_DIM)
    cos_diff, sin_diff = rope_tables(positions, DIFF_HEAD_DIM)
    offsets = [int(o) for o in np.cumsum(IN_SPLITS)[:-1]]
    h = x
    for i in range(DEPTH):
        lambda_init = 0.8 - 0.6 * math.exp(-0.3 * i)
        a = rms_norm(h, attn_norm[i])
        z = a @ w_in[i]
        c_q, c_kv, k_rope, dq, dk, dv = jnp.split(z, offsets, axis=-1)
        o_mla = mla_group(c_q, c_kv, k_rope, cos_mla, sin_mla, q_a_norm[i], w_uq[i],
                          kv_a_norm[i], w_ukv[i], mla_q_norm[i], mla_k_norm[i])
        o_diff = diff_group(dq, dk, dv, cos_diff, sin_diff, diff_q_norm[i], diff_k_norm[i],
                            lambda_q1[i], lambda_k1[i], lambda_q2[i], lambda_k2[i],
                            diff_subln[i], lambda_init)
        h = h + jnp.concatenate([o_mla, o_diff], axis=-1) @ w_out[i]
        m = rms_norm(h, ffn_norm[i])
        h = h + hierarchical_moe(m, w_group[i], b_group[i], w_router[i], b_router[i],
                                 w_gate[i], w_up[i], w_down[i])
        gate = jax.nn.sigmoid((rms_norm(h, ple_norm[i]) @ w_ple_gate[i]).astype(jnp.float32)).astype(h.dtype)
        h = h + gate * (p[i] @ w_ple_proj[i])
    return h


_drawn_inputs = setup_inputs


def setup_inputs(seed=0):
    import zlib

    import numpy as np

    out = dict(_drawn_inputs(seed))
    spreads = {}
    factors = {'q_a_norm': 5.594,
     'kv_a_norm': 3.321,
     'mla_q_norm': 3.603,
     'mla_k_norm': 5.144,
     'b_group': 4.369,
     'b_router': 3.794,
     'ple_norm': 8.0}
    for name, (base, spread) in spreads.items():
        noise = np.random.default_rng([zlib.crc32(name.encode()), seed]).standard_normal(out[name].shape)
        drawn = base * np.exp(spread * noise) if base else spread * noise
        out[name] = __import__('jax').numpy.asarray(drawn.astype(out[name].dtype))
    for name, factor in factors.items():
        out[name] = (out[name] * factor).astype(out[name].dtype)
    return out
```

```python
import math
from contextlib import ExitStack

import concourse.bass as bass
from concourse import mybir

F32 = mybir.dt.float32
I32 = mybir.dt.int32
ALU = mybir.AluOpType
ACT = mybir.ActivationFunctionType
AX = mybir.AxisListType
ds = bass.ds

P = 128
D = 1024
SEQ = 256
DEPTH = 2
TT = SEQ // P
KD = D // P
CHUNK = 64
EPS = 1e-6
PLE = 256
MH, NOPE, ROPE, MV = 8, 64, 32, 64
MQK = NOPE + ROPE
QR, KVR = 256, 128
DH, DHD = 4, 64
DV = 2 * DHD
MAPS = 2 * DH
SPLITS = [(0, 416), (416, 928), (928, 1440), (1440, 1952)]
NG, NEG, FF = 4, 8, 256
NE = NG * NEG
KF = FF // P
BLK = 128
NSLOT = 2 * SEQ
MAXB = -(-SEQ // BLK)
CB = 512

SLOT = 2048
EPI = 4
RING = 3 * EPI
EXPERT_ITERS = NE // EPI

HB = ROPE // 2
HD = DHD // 2
C_ID, C_TRI, C_ONE, C_MU, C_MV = 0, 128, 256, 384, 512
C_IOTA = C_MV + CHUNK
C_FM = C_IOTA + NSLOT
C_FD = C_FM + HB
C_E32 = C_FD + HD
C_G4 = C_E32 + NE
NCONST = C_G4 + NG

INV_2PI = 1.0 / (2.0 * math.pi)
TWO_PI_1 = 6.28125
TWO_PI_2 = 2029 / 2.0 ** 20
TWO_PI_3 = 2.0 * math.pi - TWO_PI_1 - TWO_PI_2
ROUND = 12582912.0
PI = 3.1415925


def constants():
    import numpy as np
    c = np.zeros((P, NCONST), np.float32)
    c[:, C_ID:C_ID + P] = np.eye(P)
    c[:, C_TRI:C_TRI + P] = np.triu(np.ones((P, P)), 1)
    c[:, C_ONE:C_ONE + P] = 1.0
    c[0, C_MU:C_MU + CHUNK] = 1.0
    c[CHUNK, C_MU:C_MU + CHUNK] = 1.0
    c[0, C_MV:C_MV + CHUNK] = -1e30
    c[CHUNK, C_MV:C_MV + CHUNK] = -1e30
    c[:, C_IOTA:C_IOTA + NSLOT] = np.arange(NSLOT)
    c[:, C_FM:C_FM + HB] = np.float32(10000.0) ** (-np.arange(0, ROPE, 2, dtype=np.float32) / ROPE)
    c[:, C_FD:C_FD + HD] = np.float32(10000.0) ** (-np.arange(0, DHD, 2, dtype=np.float32) / DHD)
    c[:, C_E32:C_E32 + NE] = np.arange(NE)
    c[:, C_G4:C_G4 + NG] = np.arange(NG)
    return c


def stream_plan():
    items, pos, used = [], 0, 0
    owner = [0] * RING
    fills = [0] * RING
    for layer in range(DEPTH):
        kinds = [("z0", 2), ("z1", 2), ("z2", 2), ("z3", 2), ("uq", 1), ("ukv", 1), ("out0", 2), ("out1", 2)]
        kinds += [(("expert", e), 3) for e in range(NE)]
        kinds += [("proj", 1), ("gate0", 2), ("gate1", 2)]
        for kind, n in kinds:
            expert = isinstance(kind, tuple)
            if not expert and pos % RING + n > RING:
                pos += RING - pos % RING
            slots = [(pos + j) % RING for j in range(n)]
            need = max(owner[s] for s in slots)
            used += 1
            for j, s in enumerate(slots):
                owner[s] = used
                if expert or j == 0:
                    fills[s] += 1
            items.append((layer, kind, slots, need, [fills[s] for s in slots], used))
            pos += n
    return items


ITEMS = stream_plan()
ITEM = {(i[0], i[1]): i for i in ITEMS}


N_SMALL = DEPTH * (3 + DH + 4 + 12 + 4 + 4)
HT_BANK = (6, 7, 0, 1, 2, 3, 4, 5, 6, 7, 0, 1)
S_BANK = (5, 6, 7, 0)
T_BANK = (3, 4)
O_BANK = (1, 2)
DISP_BANK = (6, 7, 0, 1, 2, 3, 6, 7)
YT_BANK = (0, 1, 2, 3, 6, 7, 0, 1)


class Stage:

    def __init__(self, sem, n):
        self.sem, self.n = sem, n

    def at(self, layer, k=None):
        return self.sem, layer * self.n + (self.n if k is None else k)


def trunk_kernel(nc, x, p, positions, attn_norm, w_in, q_a_norm, w_uq, kv_a_norm, w_ukv, mla_q_norm,
                 mla_k_norm, diff_q_norm, diff_k_norm, lambda_q1, lambda_k1, lambda_q2, lambda_k2,
                 diff_subln, w_out, ffn_norm, w_group, b_group, w_router, b_router, w_gate, w_up,
                 w_down, ple_norm, w_ple_gate, w_ple_proj, const, out):
    with ExitStack() as ctx:
        def sb(name, shape, dt=F32):
            return ctx.enter_context(nc.sbuf_tensor(name, shape, dt))

        def sem(name):
            return ctx.enter_context(nc.semaphore(name))

        def stage(name, n):
            return Stage(sem(name), n)

        ctx.enter_context(nc.allow_non_contiguous_dma(reason="gains with one value per partition"))

        PS = ctx.enter_context(nc.psum_tensor("PS", [P, 8, CB], F32))

        ring = sb("ring", [P, RING * SLOT])
        cst = sb("cst", [P, NCONST])
        ident = cst[:, C_ID:C_ID + P]
        tri = cst[:, C_TRI:C_TRI + P]
        ones = cst[:, C_ONE:C_ONE + P]
        iota_slot = cst[:, C_IOTA:C_IOTA + NSLOT]
        h = sb("h", [P, TT, D])
        hn = sb("hn", [P, TT, D])
        aT = sb("aT", [P, KD, SEQ])
        g_in = sb("g_in", [P, DEPTH, 4, KD])
        g_cq = sb("g_cq", [P, DEPTH, 2])
        g_ckv = sb("g_ckv", [P, DEPTH, 1])
        g_nope = sb("g_nope", [MQK, DEPTH, 2])
        g_k = sb("g_k", [MQK, DEPTH])
        g_rope = sb("g_rope", [P, DEPTH, 2, 2, ROPE])
        g_diff = sb("g_diff", [P, DEPTH, 2, 2, DHD])
        bias = sb("bias", [P, DEPTH, NG + NE])
        w_rt = sb("w_rt", [P, DEPTH, KD, NG + NE])
        lams = sb("lams", [P, DEPTH, 2])
        lame = sb("lame", [P, DEPTH, 2])
        neglam = sb("neglam", [P, DEPTH])
        pT = sb("pT", [P, DEPTH, 2, SEQ])
        posi = sb("posi", [P, TT], I32)
        posf = sb("posf", [P, TT])
        NF = HB + HD
        trig_m = sb("trig_m", [P, 2, TT, 2, HB])
        trig_d = sb("trig_d", [P, 2, TT, 2, HD])
        rope_m = sb("rope_m", [P, 2, 2, TT, ROPE])
        rope_d = sb("rope_d", [P, 2, 2, TT, DHD])
        lss = sb("lss", [P, 2 * TT])
        lms = sb("lms", [P, 2 * TT])
        lrs = sb("lrs", [P, 2 * TT])
        ssh = sb("ssh", [P, TT])
        krs = sb("krs", [P, TT, ROPE])
        krr2 = sb("krr2", [P, TT, ROPE])
        ods = sb("ods", [P, TT * DH])
        odr = sb("odr", [P, TT * DH])
        mstat = sb("mstat", [P, TT])
        rstd = sb("rstd", [P, TT])
        expo = sb("expo", [P, 32])
        AREA = 12288
        area = sb("area", [P, AREA])
        used = [0]

        def part(n, **dims):
            v = area[:, used[0]:used[0] + n]
            used[0] += n
            assert used[0] <= AREA, used[0]
            return v

        lat = part(TT * 384).rearrange("p (t n) -> p t n", t=TT)
        kr = part(TT * ROPE).rearrange("p (t n) -> p t n", t=TT)
        krr = part(TT * ROPE).rearrange("p (t n) -> p t n", t=TT)
        cqT = part(2 * SEQ).rearrange("p (k t) -> p k t", k=2)
        ckvT = part(SEQ)
        junk = part(1024)
        rtmp = part(1024)
        dqr = part(TT * 512).rearrange("p (t n) -> p t n", t=TT)
        dkr = part(TT * 512).rearrange("p (t n) -> p t n", t=TT)
        vd = part(TT * 512).rearrange("p (t n) -> p t n", t=TT)
        vm = part(TT * 512).rearrange("p (t n) -> p t n", t=TT)
        qTm = part(MH * SEQ).rearrange("p (h t) -> p h t", h=MH)
        kTm = part(MH * SEQ).rearrange("p (h t) -> p h t", h=MH)
        vmf = vm.rearrange("p t n -> p (t n)")
        lamv = vmf[:, 0:DEPTH * 4 * DHD].rearrange("p (l j n) -> p l j n", l=DEPTH, j=4)
        lamp = vmf[:, DEPTH * 4 * DHD:DEPTH * 4 * DHD + 2 * DHD].rearrange("p (j n) -> p j n", j=2)
        kTf = kTm.rearrange("p h t -> p (h t)")
        nang = TT * 2 * NF
        ang, turns, red, trig_raw = (kTf[:, i * nang:(i + 1) * nang].rearrange("p (t c n) -> p t c n", t=TT, c=2)
                                     for i in range(4))
        hnf = hn[:, :, :].rearrange("p t n -> p (t n)")
        qm = hnf[:, 0:TT * MH * MQK].rearrange("p (t n) -> p t n", t=TT)
        ocat = sb("ocat", [P, TT, D])
        ocf = ocat[:, :, :].rearrange("p t n -> p (t n)")
        km = ocf[:, 0:TT * MH * MQK].rearrange("p (t n) -> p t n", t=TT)
        actjunk = ocf[:, 0:TT * D].rearrange("p (t n) -> p t n", t=TT)
        aTf = aT[:, :, :].rearrange("p k t -> p (k t)")
        qTd = aTf[:, 0:DH * SEQ].rearrange("p (h t) -> p h t", h=DH)
        kTd = aTf[:, DH * SEQ:2 * DH * SEQ].rearrange("p (h t) -> p h t", h=DH)
        prb = sb("prb", [P, 2, 384])
        prT = rtmp[:, 256:1024].rearrange("p (b n) -> p b n", b=2)
        ssq = sb("ssq", [P, 4, TT, 8])
        rsq = sb("rsq", [P, 4, TT, 8])
        sskr = sb("sskr", [P, TT])
        qsc = sb("qsc", [P, 2, 2, TT, 8])
        mx = sb("mx", [P, 16, TT])
        nbias = sb("nbias", [P, 16, TT])
        sums = sb("sums", [P, 16, TT])
        rinv = sb("rinv", [P, 16, TT])
        used[0] = 0
        mTs = part(KD * (NSLOT + BLK)).rearrange("p (k s) -> p k s", k=KD)
        yTs = part(KD * (NSLOT + BLK)).rearrange("p (k s) -> p k s", k=KD)
        ys = area[:, 0:4 * D].rearrange("p (s d) -> p s d", s=4)
        pdis = part(TT * NSLOT).rearrange("p (t s) -> p t s", t=TT)
        GT = part(TT * NSLOT).rearrange("p (t s) -> p t s", t=TT)
        G = pdis.rearrange("p t s -> p (t s)").rearrange("p (s t) -> p s t", s=4)
        gtmp = ocat[:, :, 0:NSLOT]
        sg = ocat[:, 0, 0:KF * BLK]
        hb = ocat[:, 0, KF * BLK:2 * KF * BLK]
        xb = ocat[:, 1, :].rearrange("p (k s) -> p k s", k=KD)
        rt = {}
        for name, shape in dict(lg=NG + NE, gmax=1, geq=NG, gc=NG, gi=1, goh=NG, gd=NG, ge=NG, gs=1, gw=1, pen=NG,
                                ml=NE, m1=1, eq=NE, c1=NE, i1=1, oh1=NE, ml2=NE, m2=1, c2=NE, i2=1, oh2=NE,
                                dm=1, e2=1, w2=1, w1=1, den=1, M=NE, Mpre=NE, s1=1, s2=1, t1=NE, t2=NE).items():
            rt[name] = sb("rt_" + name, [P, TT, shape])
        Mp = sb("Mp", [P, NE])
        cnt = sb("cnt", [1, 6, NE])
        pfx = sb("pfx", [1, 8, NE])
        carry = sb("carry", [1, 1])
        ctlf = sb("ctlf", [1, NE, 4])
        ctl = sb("ctl", [1, NE * 4], I32)
        sig = area[:, 4 * D:4 * D + 4 * CB].rearrange("p (j n) -> p j n", j=4)
        prod = area[:, 6 * D:6 * D + 4 * CB].rearrange("p (j n) -> p j n", j=4)
        pin = rtmp.rearrange("p (l t n) -> p l t n", l=DEPTH, t=TT)

        arrived = [sem(f"arrived{s}") for s in range(RING)]
        weights_used = sem("weights_used")
        loaded = {k: sem("loaded_" + k) for k in ("x", "const", "p", "small")}
        sem_pool, sem_dve = sem("pool_order"), sem("dve_order")
        one = {k: sem("one_" + k) for k in ("pow", "posf", "pTc0", "lamp", "lame", "ang", "sin", "trig", "gains")}
        s_sq = stage("sq", 3 * TT)
        s_ms = stage("ms", 3)
        s_rs = stage("rs", 3)
        s_hn0 = stage("hn0", 3)
        s_hn1 = stage("hn1", 3)
        s_tr = stage("tr", 4 * 4)
        s_aTv = stage("aTv", 4 * 2)
        s_aTs = stage("aTs", 4 * 2)
        s_z = stage("z", 4)
        s_lsq = stage("lsq", 1)
        s_lms = stage("lms", 1)
        s_lrs = stage("lrs", 1)
        s_lat = stage("lat", 1)
        s_lT = stage("lT", 1)
        s_lTc = stage("lTc", 1)
        s_junk = stage("junk", 6)
        s_sum = stage("sum", 6)
        s_vd = stage("vd", 1)
        s_uq = stage("uq", TT)
        s_ukv = stage("ukv", TT)
        s_qn = stage("qn", TT)
        s_vm = stage("vm", TT)
        s_kn = stage("kn", TT)
        s_hms = stage("hms", 5)
        s_hrs = stage("hrs", 5)
        s_kr = stage("kr", 1)
        s_krr = stage("krr", 1)
        s_kpe = stage("kpe", TT)
        s_tab = stage("tab", 1)
        s_dq = stage("dq", 1)
        s_dk = stage("dk", 1)
        s_qr = stage("qr", TT)
        s_hT = stage("hT", 12)
        s_hTv = stage("hTv", 6)
        s_hTs = stage("hTs", 6)
        s_S = stage("S", 16)
        s_nb = stage("nb", 16)
        s_exp = stage("exp", 16)
        s_T = stage("T", 16)
        s_Tv = stage("Tv", 8)
        s_Ts = stage("Ts", 8)
        s_O = stage("O", 16)
        s_Oe = stage("Oe", 16)
        s_od = stage("od", 1)
        s_oc = stage("oc", 1)
        s_out = stage("out", 4)
        s_h = stage("hready", 3)
        s_rl = stage("rl", 1)
        s_ra = stage("ra", 2)
        s_re = stage("re", 2)
        s_M = stage("M", 1)
        s_pos = stage("pos", 1)
        s_ctl = stage("ctl", 1)
        s_P = stage("P", 1)
        s_GT = stage("GT", 1)
        s_GTt = stage("GTt", 1)
        s_Gc = stage("Gc", 1)
        s_disp = stage("disp", KD)
        s_dv = stage("dv", KD // 2)
        s_da = stage("da", KD // 2)
        s_pad = stage("pad", 1)
        s_xb = sem("xb")
        s_gu = sem("gu")
        s_silu = sem("silu")
        s_hid = sem("hid")
        s_y = sem("y")
        s_yc = sem("yc")
        s_yT = stage("yT", 8)
        s_yv = stage("yv", 4)
        s_ya = stage("ya", 4)
        s_cmb = stage("cmb", 4)
        s_pp = stage("pp", 4)
        s_gt = stage("gt", 4)
        s_sg = stage("sg", 4)
        s_fin = stage("fin", 4)
        stored = sem("stored")

        def bank(b, n=1):
            return PS[:, b, :] if n == 1 else PS[:, b:b + n, :]

        def slots(item, k, n):
            s = item[2][0]
            return ring[:, s * SLOT:s * SLOT + k * n].rearrange("p (k n) -> p k n", k=k)

        def arrival(eng, item):
            eng.wait_ge(arrived[item[2][0]], 16 * item[4][0])

        def s_sq_at(l, k):
            return s_sq.at(l, TT * (k + 1))

        def hT_dest(l, idx):
            if idx < 4:
                a = 2 * (idx % 2)
                return P, (qTd if idx < 2 else kTd)[:, a:a + 2, :], None
            a = 2 * ((idx - 4) % 4)
            return MQK, (qTm if idx < 8 else kTm)[0:MQK, a:a + 2, :], None if idx < 8 else g_k[:, l:l + 1]

        def column(first, b):
            return nc.s_assert_within(first + b * BLK, 0, NSLOT, skip_runtime_bounds_check_because=
                                      "a block starts at or before the last of the expert's slots")

        block = ctx.enter_context(nc.Block())

        @block.sync
        def _(sp):
            for t in range(TT):
                sp.dma_start(h[:, t, :], x[0, t * P:(t + 1) * P, :]).then_inc(loaded["x"], 16)
            sp.dma_start(cst[:, :], const).then_inc(loaded["const"], 16)

            def load(item):
                layer, kind, slot, need, _, _ = item
                if need:
                    sp.wait_ge(weights_used, need)
                s = slot[0]
                if kind[0] == "z":
                    a, b = SPLITS[int(kind[1])]
                    src = w_in[layer].rearrange("(p k) n -> p k n", k=KD)[:, :, a:b]
                    dst = slots(item, KD, b - a)
                elif kind == "uq":
                    src = w_uq[layer].rearrange("(p k) n -> p k n", k=2)
                    dst = slots(item, 2, MH * MQK)
                elif kind == "ukv":
                    src = w_ukv[layer]
                    dst = ring[:, s * SLOT:s * SLOT + 1024]
                elif kind[:3] == "out" or kind[:4] == "gate":
                    c = int(kind[-1])
                    w = w_out if kind[:3] == "out" else w_ple_gate
                    src = w[layer].rearrange("(p k) n -> p k n", k=KD)[:, :, c * CB:(c + 1) * CB]
                    dst = slots(item, KD, CB)
                else:
                    src = w_ple_proj[layer].rearrange("(p k) n -> p k n", k=2)
                    dst = slots(item, 2, D)
                sp.dma_start(dst, src).then_inc(arrived[s], 16)

            def load_expert(layer, e, slot):
                for part_, w in enumerate((w_gate, w_up, w_down)):
                    s = slot[part_]
                    if part_ < 2:
                        src = w[layer].rearrange("g e (p k) f -> (g e) p (k f)", k=KD)[ds(e, 1)]
                        src = src.rearrange("o p n -> (o p) n")
                        dst = ring[:, s * SLOT:(s + 1) * SLOT]
                    else:
                        src = w[layer].rearrange("g e (k p) d -> (g e) p k d", p=P)[ds(e, 1)]
                        src = src.rearrange("o p k d -> (o p) k d")
                        dst = ring[:, s * SLOT:(s + 1) * SLOT].rearrange("p (k d) -> p k d", k=KF)
                    sp.dma_start(dst, src).then_inc(arrived[s], 16)

            for layer in range(DEPTH):
                for kind in ("z0", "z1", "z2", "z3", "uq", "ukv", "out0", "out1"):
                    load(ITEM[layer, kind])
                first = [ITEM[layer, ("expert", e)] for e in range(EPI)]
                for e, item in enumerate(first):
                    if item[3]:
                        sp.wait_ge(weights_used, item[3])
                    load_expert(layer, e, item[2])
                with sp.Fori(1, EXPERT_ITERS) as i:
                    for u, item in enumerate(first):
                        sp.wait_ge(weights_used, i * EPI + (item[5] - EPI))
                        load_expert(layer, i * EPI + u, item[2])
                for kind in ("proj", "gate0", "gate1"):
                    load(ITEM[layer, kind])
            for t in range(TT):
                for c in range(2):
                    sp.wait_ge(*s_fin.at(DEPTH - 1, 2 * t + c + 1))
                    sp.dma_start(out[0, t * P:(t + 1) * P, c * CB:(c + 1) * CB],
                                 h[:, t, c * CB:(c + 1) * CB]).then_inc(stored, 16)
            sp.wait_ge(stored, 16 * 2 * TT)

        @block.gpsimd
        def _(pool):
            chain = [0]
            s_chain = sem_pool

            def link(ins):
                chain[0] += 1
                ins.then_inc(s_chain, 1)
                pool.wait_ge(s_chain, chain[0])

            nc.gpsimd.memset(expo[:, :], -0.5).then_inc(one["pow"], 1)
            pool.wait_ge(one["pow"], 1)
            def root(dst, src, n, wait, done):
                pool.wait_ge(*wait)
                nc.gpsimd.tensor_tensor(dst, src, expo[:, 0:n], ALU.pow).then_inc(done.sem, 1)

            for l in range(DEPTH):
                root(rstd[:, :], mstat[:, :], TT, s_ms.at(l, 1), s_rs)
                pool.wait_ge(one["trig"], 6)
                pool.wait_ge(loaded["small"], 16 * N_SMALL)
                if l:
                    pool.wait_ge(*s_qr.at(l - 1))
                    pool.wait_ge(*s_krr.at(l - 1))
                for qk in range(2):
                    for cs in range(2):
                        g = g_rope[:, l, qk, cs, :].unsqueeze(1).broadcast_to([P, TT, ROPE])
                        link(nc.gpsimd.tensor_tensor(rope_m[:, qk, cs], trig_m[:, cs].rearrange("p t a n -> p t (a n)"),
                                                     g, ALU.mult))
                        g = g_diff[:, l, qk, cs, :].unsqueeze(1).broadcast_to([P, TT, DHD])
                        ins = nc.gpsimd.tensor_tensor(rope_d[:, qk, cs], trig_d[:, cs].rearrange("p t a n -> p t (a n)"),
                                                      g, ALU.mult)
                        if qk == 1 and cs == 1:
                            ins.then_inc(s_tab.sem, 1)
                        else:
                            link(ins)

                root(lrs[:, :], lms[:, :], 4, s_lms.at(l), s_lrs)

                def head_root(w):
                    root(rsq[:, w].rearrange("p t h -> p (t h)"), ssq[:, w].rearrange("p t h -> p (t h)"), 16,
                         s_hms.at(l, w + 1), s_hrs)

                head_root(0)
                pool.wait_ge(*s_kr.at(l))
                pool.wait_ge(*s_tab.at(l))
                c_, s_ = rope_m[:, 1, 0], rope_m[:, 1, 1]
                t_ = krs[:, :, :]
                link(nc.gpsimd.tensor_tensor(krr, kr, c_, ALU.mult))
                link(nc.gpsimd.tensor_tensor(t_[:, :, 0:HB], kr[:, :, HB:ROPE], s_[:, :, 0:HB], ALU.mult))
                link(nc.gpsimd.tensor_tensor(t_[:, :, HB:ROPE], kr[:, :, 0:HB], s_[:, :, HB:ROPE], ALU.mult))
                link(nc.gpsimd.tensor_tensor(krr, krr, t_, ALU.add))
                nc.gpsimd.tensor_copy(krr2[:, :, :], krr).then_inc(s_krr.sem, 1)
                head_root(1)
                head_root(2)
                head_root(3)
                pool.wait_ge(*s_hrs.at(l, 4))
                pool.wait_ge(*s_krr.at(l))
                for t in range(TT):
                    kv = km[:, t, :].rearrange("p (h n) -> p h n", h=MH)[:, :, NOPE:MQK]
                    nc.gpsimd.tensor_tensor(kv, krr2[:, t, :].unsqueeze(1).broadcast_to([P, MH, ROPE]),
                                            rsq[:, 3, t, :].unsqueeze(2).broadcast_to([P, MH, ROPE]),
                                            ALU.mult).then_inc(s_kpe.sem, 1)
                pool.wait_ge(*s_hms.at(l, 5))
                nc.gpsimd.tensor_tensor(odr[:, :], ods[:, :], expo[:, 0:TT * DH], ALU.pow).then_inc(s_hrs.sem, 1)
                root(rstd[:, :], mstat[:, :], TT, s_ms.at(l, 2), s_rs)
                nc.gpsimd.memset(mTs[:, :, NSLOT:NSLOT + BLK], 0.0).then_inc(s_pad.sem, 1)
                pool.wait_ge(*s_pad.at(l))
                pool.wait_ge(*s_dv.at(l))
                pool.wait_ge(*s_da.at(l))
                pool.wait_ge(*s_ctl.at(l))
                pool.wait_ge(*s_GT.at(l))
                with pool.Fori(0, NE) as e:
                    first = pool.value_load(ctl[0:1, ds(e * 4, 1)], min_val=0, max_val=NSLOT)
                    nb = pool.value_load(ctl[0:1, ds(e * 4 + 1, 1)], min_val=1, max_val=MAXB)
                    base = pool.value_load(ctl[0:1, ds(e * 4 + 2, 1)], min_val=0, max_val=2 * (NE + NSLOT // BLK))
                    with pool.Fori(0, nb) as b:
                        pool.wait_ge(s_gu, base + b + 1)
                        nc.gpsimd.tensor_copy(xb, mTs[:, :, ds(column(first, b), BLK)]).then_inc(s_xb, 1)
                root(rstd[:, :], mstat[:, :], TT, s_ms.at(l, 3), s_rs)

        @block.scalar
        def _(act):
            act.dma_start(posi[:, :], positions.rearrange("b (t p) -> p (b t)", p=P)).then_inc(loaded["p"], 16)
            for l in range(DEPTH):
                act.dma_start(pin[:, l], p[l, 0].rearrange("(t p) n -> p t n", p=P)).then_inc(loaded["p"], 16)
            n = [0]

            def small_load(dst, src):
                n[0] += 1
                act.dma_start(dst, src).then_inc(loaded["small"], 16)

            for l in range(DEPTH):
                small_load(g_in[:, l, 0, :], attn_norm[l].rearrange("(p k) -> p k", k=KD))
                small_load(g_in[:, l, 2, :], ffn_norm[l].rearrange("(p k) -> p k", k=KD))
                small_load(g_in[:, l, 3, :], ple_norm[l].rearrange("(p k) -> p k", k=KD))
                for hd in range(DH):
                    small_load(g_in[64 + 16 * hd:80 + 16 * hd, l, 1, :], diff_subln[l].rearrange("(p k) -> p k", k=KD))
                small_load(g_cq[:, l, :], q_a_norm[l].rearrange("(p k) -> p k", k=2))
                small_load(g_ckv[:, l, :], kv_a_norm[l].rearrange("(p k) -> p k", k=1))
                small_load(g_nope[0:NOPE, l, 0:1], mla_q_norm[l, 0:NOPE].rearrange("(p k) -> p k", k=1))
                small_load(g_nope[0:NOPE, l, 1:2], mla_k_norm[l, 0:NOPE].rearrange("(p k) -> p k", k=1))
                for qk, (gm, gd) in enumerate(((mla_q_norm, diff_q_norm), (mla_k_norm, diff_k_norm))):
                    small_load(g_rope[:, l, qk, 0, :], gm[l, NOPE:MQK].partition_broadcast(P))
                    small_load(g_rope[:, l, qk, 1, 0:HB], gm[l, NOPE + HB:MQK].partition_broadcast(P))
                    small_load(g_rope[:, l, qk, 1, HB:ROPE], gm[l, NOPE:NOPE + HB].partition_broadcast(P))
                    small_load(g_diff[:, l, qk, 0, :], gd[l].partition_broadcast(P))
                    small_load(g_diff[:, l, qk, 1, 0:HD], gd[l, HD:DHD].partition_broadcast(P))
                    small_load(g_diff[:, l, qk, 1, HD:DHD], gd[l, 0:HD].partition_broadcast(P))
                small_load(bias[:, l, 0:NG], b_group[l].partition_broadcast(P))
                small_load(bias[:, l, NG:NG + NE], b_router[l].partition_broadcast(P))
                small_load(w_rt[:, l, :, 0:NG], w_group[l].rearrange("(p k) n -> p k n", k=KD))
                small_load(w_rt[:, l, :, NG:NG + NE], w_router[l].rearrange("(p k) n -> p k n", k=KD))
                for j, v in enumerate((lambda_q1, lambda_k1, lambda_q2, lambda_k2)):
                    small_load(lamv[:, l, j, :], v[l].partition_broadcast(P))
            assert n[0] == N_SMALL
            def square_tiles(l, k):
                for t in range(TT):
                    if t == 0:
                        if k == 0 and l == 0:
                            act.wait_ge(loaded["x"], 32)
                        elif k == 0:
                            act.wait_ge(*s_h.at(l - 1, 3))
                        else:
                            act.wait_ge(*s_h.at(l, k))
                    act.activation(actjunk[:, t, :], h[:, t, :], ACT.Square, accum_out=ssh[:, t:t + 1]).then_inc(s_sq.sem, 1)

            def norm_tile(l, k):
                act.wait_ge(*s_rs.at(l, k + 1))
                act.activation(hn[:, 0, :], h[:, 0, :], ACT.Copy, scale=rstd[:, 0:1]).then_inc(s_hn0.sem, 1)

            def evac_pass(l, n_):
                for b in (2, 3):
                    act.wait_ge(*s_tr.at(l, 4 * n_ + b + 1))
                    for k in (2 * b, 2 * b + 1):
                        ins = act.activation(aT[:, k, :], PS[:, b, (k % 2) * SEQ:(k % 2 + 1) * SEQ], ACT.Copy,
                                             scale=g_in[:, l, n_, k:k + 1])
                    ins.then_inc(s_aTs.sem, 1)

            for l in range(DEPTH):
                square_tiles(l, 0)
                norm_tile(l, 0)
                if l == 0:
                    act.wait_ge(one["ang"], 1)
                    for cs in range(2):
                        act.activation(trig_raw[:, :, cs, :], red[:, :, cs, :], ACT.Sin).then_inc(one["sin"], 1)
                    act.wait_ge(one["lamp"], 2 * DEPTH)
                    act.activation(lame[:, :, :], lams[:, :, :], ACT.Exp).then_inc(one["lame"], 1)
                    act.wait_ge(one["gains"], 1)
                evac_pass(l, 0)
                act.wait_ge(*s_z.at(l, 1))
                for t in range(TT):
                    act.activation(actjunk[:, t, 0:QR], PS[:, 4 + t, 0:QR], ACT.Square, accum_out=lss[:, t:t + 1])
                    ins = act.activation(actjunk[:, t, QR:QR + KVR], PS[:, 4 + t, QR:QR + KVR], ACT.Square,
                                         accum_out=lss[:, 2 + t:3 + t])
                ins.then_inc(s_lsq.sem, 1)
                act.wait_ge(*s_z.at(l, 2))
                act.activation(junk, bank(6, 2).rearrange("p t n -> p (t n)"), ACT.Square).then_inc(s_junk.sem, 1)
                act.wait_ge(*s_z.at(l, 3))
                act.wait_ge(*s_sum.at(l, 1))
                act.activation(junk, bank(0, 2).rearrange("p t n -> p (t n)"), ACT.Square).then_inc(s_junk.sem, 1)
                act.wait_ge(*s_z.at(l, 4))
                act.activation(vd.rearrange("p t n -> p (t n)"), bank(2, 2).rearrange("p t n -> p (t n)"),
                               ACT.Copy).then_inc(s_vd.sem, 1)
                for t, b in enumerate((6, 0)):
                    act.wait_ge(*s_uq.at(l, t + 1))
                    act.wait_ge(*s_sum.at(l, 2 + t))
                    src = bank(b, 2)[:, :, 0:4 * MQK]
                    act.activation(junk[:, 0:MH * MQK].rearrange("p (b n) -> p b n", b=2), src,
                                   ACT.Square).then_inc(s_junk.sem, 1)
                    dst = qm[:, t, :].rearrange("p (b h n) -> p b h n", b=2, h=4)[:, :, :, 0:NOPE]
                    srcn = src.rearrange("p b (h n) -> p b h n", h=4)[:, :, :, 0:NOPE]
                    act.activation(dst, srcn, ACT.Copy).then_inc(s_qn.sem, 1)
                for t, b in enumerate((2, 4)):
                    act.wait_ge(*s_ukv.at(l, t + 1))
                    src = bank(b, 2).rearrange("p b (h n) -> p b h n", h=4)
                    if t == 0:
                        act.wait_ge(*s_sum.at(l, 4))
                    dst = junk.rearrange("p (t b h n) -> p t b h n", t=2, b=2, h=4)[:, t]
                    ins = act.activation(dst, src[:, :, :, 0:NOPE], ACT.Square)
                    if t == 1:
                        ins.then_inc(s_junk.sem, 1)
                    act.activation(vm[:, t, :].rearrange("p (b h n) -> p b h n", b=2, h=4), src[:, :, :, NOPE:],
                                   ACT.Copy).then_inc(s_vm.sem, 1)
                for j in range(6):
                    idx = 2 * j + 1
                    act.wait_ge(*s_hT.at(l, idx + 1))
                    rows, dst, gain = hT_dest(l, idx)
                    src = PS[0:rows, HT_BANK[idx], :].rearrange("p (h t) -> p h t", h=2)
                    if gain is None:
                        act.activation(dst, src, ACT.Copy).then_inc(s_hTs.sem, 1)
                    else:
                        act.activation(dst, src, ACT.Copy, scale=gain).then_inc(s_hTs.sem, 1)
                for m in range(16 + 1):
                    if m < 16:
                        act.wait_ge(*s_nb.at(l, m + 1))
                        if m >= 2:
                            act.wait_ge(*s_T.at(l, m - 1))
                        kind, hd = (0, m) if m < MAPS else (1, m - MAPS)
                        b = S_BANK[m % 4]
                        act.activation(prb[:, m % 2, 0:P], PS[:, b, 0:P], ACT.Exp, bias=nbias[:, m, 0:1],
                                       scale=qsc[:, kind, 0, 0, hd:hd + 1], accum_out=sums[:, m, 0:1])
                        act.activation(prb[:, m % 2, P:3 * P], PS[:, b, P:3 * P], ACT.Exp, bias=nbias[:, m, 1:2],
                                       scale=qsc[:, kind, 0, 1, hd:hd + 1],
                                       accum_out=sums[:, m, 1:2]).then_inc(s_exp.sem, 1)
                    if m >= 1 and (m - 1) % 2 == 1:
                        j = m - 1
                        act.wait_ge(*s_T.at(l, j + 1))
                        if j >= 2:
                            act.wait_ge(*s_O.at(l, j - 1))
                        act.activation(prT[:, 1, :], PS[:, 4, 0:384], ACT.Copy).then_inc(s_Ts.sem, 1)
                    if m == MAPS + 3:
                        act.wait_ge(*s_od.at(l))
                        act.activation(junk.rearrange("p (t n) -> p t n", t=TT), ocat[:, :, 512:1024],
                                       ACT.Square).then_inc(s_junk.sem, 1)
                evac_pass(l, 1)
                square_tiles(l, 1)
                norm_tile(l, 1)
                evac_pass(l, 2)
                act.wait_ge(*s_ra.at(l, 1))
                act.activation(rt["ge"][:, :, :], rt["gd"][:, :, :], ACT.Exp).then_inc(s_re.sem, 1)
                act.wait_ge(*s_ra.at(l, 2))
                act.activation(rt["e2"][:, :, :], rt["dm"][:, :, :], ACT.Exp).then_inc(s_re.sem, 1)
                for k in range(1, KD, 2):
                    act.wait_ge(*s_disp.at(l, k + 1))
                    act.activation(mTs[:, k, 0:NSLOT], PS[:, DISP_BANK[k], :], ACT.Copy,
                                   scale=g_in[:, l, 2, k:k + 1]).then_inc(s_da.sem, 1)
                act.wait_ge(*s_ctl.at(l))
                with act.Fori(0, NE) as e:
                    nb = act.value_load(ctl[0:1, ds(e * 4 + 1, 1)], min_val=1, max_val=MAXB)
                    base = act.value_load(ctl[0:1, ds(e * 4 + 2, 1)], min_val=0, max_val=2 * (NE + NSLOT // BLK))
                    with act.Fori(0, nb) as b:
                        act.wait_ge(s_gu, base + b + 2)
                        act.wait_ge(s_hid, base + b + 1)
                        act.activation(sg, PS[:, 4, 0:KF * BLK], ACT.Silu).then_inc(s_silu, 1)
                for j in range(4):
                    act.wait_ge(*s_yT.at(l, 2 * j + 2))
                    act.activation(ys[:, j, CB:2 * CB], PS[:, YT_BANK[2 * j + 1], :], ACT.Copy).then_inc(s_ya.sem, 1)
                square_tiles(l, 2)
                norm_tile(l, 2)
                evac_pass(l, 3)
                for j in range(4):
                    act.wait_ge(*s_gt.at(l, j + 1))
                    act.activation(sig[:, j, :], PS[:, j, :], ACT.Sigmoid).then_inc(s_sg.sem, 1)

        @block.vector
        def _(dve):
            chain = [0]

            def link(ins):
                chain[0] += 1
                ins.then_inc(sem_dve, 1)
                dve.wait_ge(sem_dve, chain[0])

            tt, ts, stt = nc.vector.tensor_tensor, nc.vector.tensor_scalar, nc.vector.scalar_tensor_tensor
            cp, red_ = nc.vector.tensor_copy, nc.vector.tensor_reduce

            dve.sem_inc(s_gu, 1)
            dve.sem_inc(s_hid, 1)
            dve.sem_inc(s_yc, 1)
            nc.vector.memset(g_in[0:64, :, 1, :], 1.0)
            nc.vector.memset(g_k[:, :], 1.0)
            link(nc.vector.memset(carry[:, :], 0.0))

            def rotary_angles():
                dve.wait_ge(loaded["const"], 16)
                dve.wait_ge(loaded["p"], 16 * (1 + DEPTH))
                link(cp(posf[:, :], posi[:, :]))
                freq = cst[:, C_FM:C_FM + NF]
                for t in range(TT):
                    for cs in range(2):
                        ins = ts(ang[:, t, cs, :], freq, posf[:, t:t + 1], None, ALU.mult)
                link(ins)
                for cs in range(2):
                    ins = ts(turns[:, :, cs, :], ang[:, :, cs, :], INV_2PI, 0.25 * (1 - cs), ALU.mult, ALU.add)
                link(ins)
                link(ts(turns[:, :, :, :], turns[:, :, :, :], ROUND, None, ALU.add))
                link(ts(turns[:, :, :, :], turns[:, :, :, :], -ROUND, None, ALU.add))
                link(stt(out=red[:, :, :, :], in0=turns[:, :, :, :], scalar=-TWO_PI_1, in1=ang[:, :, :, :],
                         op0=ALU.mult, op1=ALU.add))
                link(stt(out=red[:, :, :, :], in0=turns[:, :, :, :], scalar=-TWO_PI_2, in1=red[:, :, :, :],
                         op0=ALU.mult, op1=ALU.add))
                link(stt(out=red[:, :, :, :], in0=turns[:, :, :, :], scalar=-TWO_PI_3, in1=red[:, :, :, :],
                         op0=ALU.mult, op1=ALU.add))
                link(ts(red[:, :, 0, :], red[:, :, 0, :], math.pi / 2, None, ALU.add))
                ts(red[:, :, :, :], red[:, :, :, :], PI, -PI, ALU.min, ALU.max).then_inc(one["ang"], 1)

            def rotary_tables():
                dve.wait_ge(one["sin"], 2)
                for dst, a, n in ((trig_m, 0, HB), (trig_d, HB, HD)):
                    cos, sin = trig_raw[:, :, 0, a:a + n], trig_raw[:, :, 1, a:a + n]
                    cp(dst[:, 0], cos.unsqueeze(2).broadcast_to([P, TT, 2, n])).then_inc(one["trig"], 1)
                    ts(dst[:, 1, :, 0, :], sin, -1.0, None, ALU.mult).then_inc(one["trig"], 1)
                    cp(dst[:, 1, :, 1, :], sin).then_inc(one["trig"], 1)

            def gains():
                dve.wait_ge(loaded["small"], 16 * N_SMALL)
                for l in range(DEPTH):
                    init = 0.8 - 0.6 * math.exp(-0.3 * l)
                    ts(g_in[64:P, l, 1, :], g_in[64:P, l, 1, :], 1.0 - init, None, ALU.mult)
                    tt(g_k[0:NOPE, l:l + 1], g_nope[0:NOPE, l, 0:1], g_nope[0:NOPE, l, 1:2], ALU.mult)
                    for j in range(2):
                        link(tt(lamp[:, j, :], lamv[:, l, 2 * j, :], lamv[:, l, 2 * j + 1, :], ALU.mult))
                        red_(lams[:, l, j:j + 1], lamp[:, j, :], AX.X, ALU.add).then_inc(one["lamp"], 1)
                dve.wait_ge(one["lame"], 1)
                for l in range(DEPTH):
                    init = 0.8 - 0.6 * math.exp(-0.3 * l)
                    link(tt(neglam[:, l:l + 1], lame[:, l, 1:2], lame[:, l, 0:1], ALU.subtract))
                    link(ts(neglam[:, l:l + 1], neglam[:, l:l + 1], -init, None, ALU.add))

            def norm(l, k):
                dve.wait_ge(*s_sq_at(l, k))
                ts(mstat[:, :], ssh[:, :], 1.0 / D, EPS, ALU.mult, ALU.add).then_inc(s_ms.sem, 1)
                dve.wait_ge(*s_rs.at(l, k + 1))
                ts(hn[:, 1, :], h[:, 1, :], rstd[:, 1:2], None, ALU.mult).then_inc(s_hn1.sem, 1)

            def evac_pass(l, n_):
                for b in (0, 1):
                    dve.wait_ge(*s_tr.at(l, 4 * n_ + b + 1))
                    g = g_in[:, l, n_, 2 * b:2 * b + 2].unsqueeze(2).broadcast_to([P, 2, SEQ])
                    tt(aT[:, 2 * b:2 * b + 2, :], bank(b).rearrange("p (k t) -> p k t", k=2), g,
                       ALU.mult).then_inc(s_aTv.sem, 1)

            def head_ms(w, n):
                ts(ssq[:, w], ssq[:, w], 1.0 / n, EPS, ALU.mult, ALU.add).then_inc(s_hms.sem, 1)

            def rotate(dst, src, tab, scratch, half):
                c, s = tab
                link(tt(dst, src, c, ALU.mult))
                tt(scratch[:, :, :, 0:half], src[:, :, :, half:2 * half], s[:, :, :, 0:half], ALU.mult)
                link(tt(scratch[:, :, :, half:2 * half], src[:, :, :, 0:half], s[:, :, :, half:2 * half], ALU.mult))
                return tt(dst, dst, scratch, ALU.add)

            def table(t, n, heads, token=None):
                v = t if token is None else t[:, token:token + 1].broadcast_to([P, 2, n])
                return v.unsqueeze(2).broadcast_to([P, 2, heads, n])

            rotary_angles()
            for l in range(DEPTH):
                norm(l, 0)
                if l == 0:
                    rotary_tables()
                    gains()
                    dve.wait_ge(one["pTc0"], 1)
                    cp(pT[:, :, :, :].rearrange("p l k t -> p (l k t)"),
                       bank(6, 2).rearrange("p b n -> p (b n)")).then_inc(one["gains"], 1)
                evac_pass(l, 0)
                dve.wait_ge(*s_lsq.at(l))
                ts(lms[:, 0:TT], lss[:, 0:TT], 1.0 / QR, EPS, ALU.mult, ALU.add)
                ts(lms[:, TT:2 * TT], lss[:, TT:2 * TT], 1.0 / KVR, EPS, ALU.mult, ALU.add).then_inc(s_lms.sem, 1)
                link(cp(kr, bank(4, 2)[:, :, QR + KVR:QR + KVR + ROPE]))
                link(tt(krs[:, :, :], kr, kr, ALU.mult))
                red_(sskr[:, :], krs[:, :, :], AX.X, ALU.add).then_inc(s_kr.sem, 1)
                dve.wait_ge(*s_lrs.at(l))
                for t in range(TT):
                    ts(lat[:, t, 0:QR], PS[:, 4 + t, 0:QR], lrs[:, t:t + 1], None, ALU.mult)
                    ins = ts(lat[:, t, QR:QR + KVR], PS[:, 4 + t, QR:QR + KVR], lrs[:, TT + t:TT + t + 1], None, ALU.mult)
                ins.then_inc(s_lat.sem, 1)
                dve.wait_ge(*s_junk.at(l, 1))
                red_(ssq[:, 0].rearrange("p t h -> p (t h)"), junk.rearrange("p (h n) -> p h n", n=DHD), AX.X,
                     ALU.add).then_inc(s_sum.sem, 1)
                dve.wait_ge(*s_sum.at(l, 1))
                head_ms(0, DHD)
                dve.wait_ge(*s_tab.at(l))
                src = bank(6, 2).rearrange("p t (h n) -> p t h n", h=8)
                scratch = rtmp.rearrange("p (t h n) -> p t h n", t=TT, h=8)
                rotate(dqr.rearrange("p t (h n) -> p t h n", h=8), src,
                       [table(rope_d[:, 0, cs], DHD, 8) for cs in range(2)], scratch, HD).then_inc(s_dq.sem, 1)
                dve.wait_ge(*s_lT.at(l))
                tt(cqT, bank(4).rearrange("p (k t) -> p k t", k=2), g_cq[:, l, :].unsqueeze(2).broadcast_to([P, 2, SEQ]),
                   ALU.mult)
                ts(ckvT, PS[:, 5, 0:SEQ], g_ckv[:, l, 0:1], None, ALU.mult).then_inc(s_lTc.sem, 1)
                dve.wait_ge(*s_junk.at(l, 2))
                red_(ssq[:, 1].rearrange("p t h -> p (t h)"), junk.rearrange("p (h n) -> p h n", n=DHD), AX.X,
                     ALU.add).then_inc(s_sum.sem, 1)
                dve.wait_ge(*s_sum.at(l, 2))
                head_ms(1, DHD)
                dk4 = dkr.rearrange("p t (h n) -> p t h n", h=8)
                dve.wait_ge(*s_dq.at(l))
                link(rotate(dk4, bank(0, 2).rearrange("p t (h n) -> p t h n", h=8),
                            [table(rope_d[:, 1, cs], DHD, 8) for cs in range(2)], scratch, HD))
                dve.wait_ge(*s_hrs.at(l, 2))
                tt(dk4, dk4, rsq[:, 1].unsqueeze(3).broadcast_to([P, TT, 8, DHD]), ALU.mult).then_inc(s_dk.sem, 1)
                for sign in range(2):
                    ts(qsc[:, 0, sign], rsq[:, 0], (1 - 2 * sign) * DHD ** -0.5, None, ALU.mult)
                dve.wait_ge(*s_dk.at(l))
                for t, b in enumerate((6, 0)):
                    dve.wait_ge(*s_junk.at(l, 3 + t))
                    red_(ssq[:, 2, t], junk[:, 0:MH * MQK].rearrange("p (h n) -> p h n", n=MQK), AX.X,
                         ALU.add).then_inc(s_sum.sem, 1)
                    dve.wait_ge(*s_qn.at(l, t + 1))
                    src = bank(b, 2)[:, :, 0:4 * MQK].rearrange("p b (h n) -> p b h n", h=4)[:, :, :, NOPE:MQK]
                    dst = qm[:, t, :].rearrange("p (b h n) -> p b h n", b=2, h=4)[:, :, :, NOPE:MQK]
                    scr = rtmp[:, 256 * t:256 * t + 256].rearrange("p (b h n) -> p b h n", b=2, h=4)
                    rotate(dst, src, [table(rope_m[:, 0, cs], ROPE, 4, t) for cs in range(2)], scr,
                           HB).then_inc(s_qr.sem, 1)
                dve.wait_ge(*s_sum.at(l, 4))
                head_ms(2, MQK)
                dve.wait_ge(*s_junk.at(l, 5))
                red_(ssq[:, 3].rearrange("p t h -> p (t h)"), junk.rearrange("p (h n) -> p h n", n=NOPE), AX.X,
                     ALU.add).then_inc(s_sum.sem, 1)
                dve.wait_ge(*s_sum.at(l, 5))
                link(tt(ssq[:, 3], ssq[:, 3], sskr[:, :].unsqueeze(2).broadcast_to([P, TT, 8]), ALU.add))
                head_ms(3, MQK)
                dve.wait_ge(*s_hrs.at(l, 4))
                dve.wait_ge(*s_vm.at(l))
                for t, b in enumerate((2, 4)):
                    src = bank(b, 2).rearrange("p b (h n) -> p b h n", h=4)[:, :, :, 0:NOPE]
                    dst = km[:, t, :].rearrange("p (b h n) -> p b h n", b=2, h=4)[:, :, :, 0:NOPE]
                    r = rsq[:, 3, t, :].rearrange("p (b h) -> p b h", b=2).unsqueeze(3).broadcast_to([P, 2, 4, NOPE])
                    tt(dst, src, r, ALU.mult).then_inc(s_kn.sem, 1)
                for sign in range(2):
                    ins = ts(qsc[:, 1, sign], rsq[:, 2], (1 - 2 * sign) * MQK ** -0.5, None, ALU.mult)
                link(ins)
                for j in range(6):
                    idx = 2 * j
                    dve.wait_ge(*s_hT.at(l, idx + 1))
                    rows, dst, gain = hT_dest(l, idx)
                    src = PS[0:rows, HT_BANK[idx], :].rearrange("p (h t) -> p h t", h=2)
                    if gain is None:
                        cp(dst, src).then_inc(s_hTv.sem, 1)
                    else:
                        ts(dst, src, gain, None, ALU.mult).then_inc(s_hTv.sem, 1)

                def maximum(m):
                    kind, hd = (0, m) if m < MAPS else (1, m - MAPS)
                    dve.wait_ge(*s_S.at(l, m + 1))
                    b = S_BANK[m % 4]
                    red_(mx[:, m, 0:1], PS[:, b, 0:P], AX.X, ALU.max)
                    link(red_(mx[:, m, 1:2], PS[:, b, P:3 * P], AX.X, ALU.max))
                    tt(nbias[:, m, :], mx[:, m, :], qsc[:, kind, 1, :, hd], ALU.mult).then_inc(s_nb.sem, 1)

                def output(m):
                    dve.wait_ge(*s_O.at(l, m + 1))
                    link(nc.vector.reciprocal(rinv[:, m, :], sums[:, m, :]))
                    b = O_BANK[m % 2]
                    if m < MAPS:
                        src = bank(b).rearrange("p (t n) -> p t n", t=TT)[:, :, 0:DV]
                        dst = ocat[:, :, 512 + DV * (m // 2):512 + DV * (m // 2 + 1)]
                        w = rinv[:, m, :].unsqueeze(2).broadcast_to([P, TT, DV])
                        if m % 2 == 0:
                            tt(dst, src, w, ALU.mult).then_inc(s_Oe.sem, 1)
                        else:
                            link(ts(rinv[:, m, :], rinv[:, m, :], neglam[:, l:l + 1], None, ALU.mult))
                            tmp = rtmp[:, 0:TT * DV].rearrange("p (t n) -> p t n", t=TT)
                            tt(tmp, src, w, ALU.mult).then_inc(s_Oe.sem, 1)
                            dve.wait_ge(*s_Oe.at(l, m + 1))
                            ins = tt(dst, dst, tmp, ALU.add)
                            if m == MAPS - 1:
                                ins.then_inc(s_od.sem, 1)
                            else:
                                link(ins)
                    else:
                        hd = m - MAPS
                        src = bank(b).rearrange("p (t n) -> p t n", t=TT)[:, :, 0:MV]
                        tt(ocat[:, :, MV * hd:MV * (hd + 1)], src, rinv[:, m, :].unsqueeze(2).broadcast_to([P, TT, MV]),
                           ALU.mult).then_inc(s_Oe.sem, 1)

                def sub_norm():
                    dve.wait_ge(*s_junk.at(l, 6))
                    red_(ods[:, :], junk.rearrange("p (h n) -> p h n", n=DV), AX.X, ALU.add).then_inc(s_sum.sem, 1)
                    dve.wait_ge(*s_sum.at(l, 6))
                    ts(ods[:, :], ods[:, :], 1.0 / DV, EPS, ALU.mult, ALU.add).then_inc(s_hms.sem, 1)

                def sub_scale():
                    dve.wait_ge(*s_hrs.at(l, 5))
                    o4 = ocat[:, :, 512:1024].rearrange("p t (h n) -> p t h n", h=DH)
                    r = odr[:, :].rearrange("p (t h) -> p t h", t=TT).unsqueeze(3).broadcast_to([P, TT, DH, DV])
                    return tt(o4, o4, r, ALU.mult)

                for i in range(16 + 2):
                    if i < 16:
                        maximum(i)
                    if 1 <= i <= 16 and (i - 1) % 2 == 0:
                        j = i - 1
                        dve.wait_ge(*s_T.at(l, j + 1))
                        if j >= 2:
                            dve.wait_ge(*s_O.at(l, j - 1))
                        cp(prT[:, 0, :], PS[:, 3, 0:384]).then_inc(s_Tv.sem, 1)
                    if i >= 2:
                        output(i - 2)
                    if i == MAPS + 5:
                        sub_norm()
                sub_scale().then_inc(s_oc.sem, 1)
                evac_pass(l, 1)
                for c in range(2):
                    for t in range(TT):
                        j = 2 * c + t
                        dve.wait_ge(*s_out.at(l, j + 1))
                        v = h[:, t, c * CB:(c + 1) * CB]
                        ins = tt(v, v, bank(4 + j), ALU.add)
                ins.then_inc(s_h.sem, 1)
                norm(l, 1)
                evac_pass(l, 2)

                R = {k: v[:, :, :] for k, v in rt.items()}
                g4 = cst[:, C_G4:C_G4 + NG].unsqueeze(1).broadcast_to([P, TT, NG])
                e32 = cst[:, C_E32:C_E32 + NE].unsqueeze(1).broadcast_to([P, TT, NE])

                def wide(v, n):
                    return v.broadcast_to([P, TT, n])

                dve.wait_ge(*s_rl.at(l))
                link(tt(R["lg"], PS[:, 4, 0:TT * (NG + NE)].rearrange("p (t n) -> p t n", t=TT),
                        bias[:, l, :].unsqueeze(1).broadcast_to([P, TT, NG + NE]), ALU.add))
                lgg, lge = rt["lg"][:, :, 0:NG], rt["lg"][:, :, NG:NG + NE]
                link(red_(R["gmax"], lgg, AX.X, ALU.max))
                tt(R["gd"], lgg, wide(R["gmax"], NG), ALU.subtract).then_inc(s_ra.sem, 1)
                link(tt(R["geq"], lgg, wide(R["gmax"], NG), ALU.is_equal))
                link(stt(out=R["gc"], in0=R["geq"], scalar=-1000.0, in1=g4, op0=ALU.mult, op1=ALU.add))
                link(red_(R["gi"], R["gc"], AX.X, ALU.min))
                link(tt(R["goh"], R["gc"], wide(R["gi"], NG), ALU.is_equal))
                link(ts(R["pen"], R["goh"], 1e30, -1e30, ALU.mult, ALU.add))
                ml4 = R["ml"].rearrange("p t (g e) -> p t g e", g=NG)
                link(tt(ml4, lge.rearrange("p t (g e) -> p t g e", g=NG),
                        rt["pen"][:, :, :].unsqueeze(3).broadcast_to([P, TT, NG, NEG]), ALU.add))

                def top(src, m, eq, c, i, oh):
                    link(red_(R[m], src, AX.X, ALU.max))
                    link(tt(R[eq], src, wide(R[m], NE), ALU.is_equal))
                    link(stt(out=R[c], in0=R[eq], scalar=-1000.0, in1=e32, op0=ALU.mult, op1=ALU.add))
                    link(red_(R[i], R[c], AX.X, ALU.min))
                    link(tt(R[oh], R[c], wide(R[i], NE), ALU.is_equal))

                top(R["ml"], "m1", "eq", "c1", "i1", "oh1")
                link(stt(out=R["ml2"], in0=R["oh1"], scalar=-2e30, in1=R["ml"], op0=ALU.mult, op1=ALU.add))
                top(R["ml2"], "m2", "eq", "c2", "i2", "oh2")
                tt(R["dm"], R["m2"], R["m1"], ALU.subtract).then_inc(s_ra.sem, 1)
                for i, a in (("i1", "t1"), ("i2", "t2")):
                    link(ts(R[i], R[i], 1000.0, None, ALU.add))
                    link(tt(R[a], e32, wide(R[i], NE), ALU.is_gt))
                link(tt(R["Mpre"], R["t1"], R["t2"], ALU.add))
                tt(Mp[:, :], rt["Mpre"][:, 0, :], rt["Mpre"][:, 1, :], ALU.add)
                tt(R["M"], R["oh1"], R["oh2"], ALU.add).then_inc(s_M.sem, 1)
                dve.wait_ge(*s_re.at(l, 2))
                link(red_(R["gs"], R["ge"], AX.X, ALU.add))
                link(ts(R["den"], R["e2"], 1.0, None, ALU.add))
                link(tt(R["den"], R["den"], R["gs"], ALU.mult))
                link(nc.vector.reciprocal(R["w1"], R["den"]))
                link(tt(R["w2"], R["w1"], R["e2"], ALU.mult))
                dve.wait_ge(*s_pos.at(l))
                pos = PS[:, 5, 0:TT * NE].rearrange("p (t n) -> p t n", t=TT)
                for oh, t_, s in (("oh1", "t1", "s1"), ("oh2", "t2", "s2")):
                    link(tt(R[t_], R[oh], pos, ALU.mult))
                    link(red_(R[s], R[t_], AX.X, ALU.add))
                for t in range(TT):
                    link(ts(pdis[:, t, :], iota_slot, rt["s1"][:, t, :], None, ALU.is_equal))
                    ins = stt(out=pdis[:, t, :], in0=iota_slot, scalar=rt["s2"][:, t, :], in1=pdis[:, t, :],
                              op0=ALU.is_equal, op1=ALU.add)
                ins.then_inc(s_P.sem, 1)
                off = PS[0:1, 5, 2 * NE:3 * NE]
                link(cp(cnt[:, 0, :], PS[0:1, 5, 3 * NE:4 * NE]))
                link(ts(cnt[:, 1, :], cnt[:, 0, :], BLK + 0.5, 1.0, ALU.is_gt, ALU.add))
                blocks = cnt[:, 1, :]
                link(nc.vector.memset(pfx[:, :, :], 0.0))
                link(cp(pfx[:, 1, :], blocks))
                flat = pfx[:, :, :].rearrange("p a n -> p (a n)")
                at = NE
                for j in range(5):
                    to = NE + 2 * NE * ((j + 1) % 2)
                    link(tt(flat[:, to:to + NE], flat[:, at:at + NE], flat[:, at - 2 ** j:at + NE - 2 ** j], ALU.add))
                    at = to
                run = flat[:, at:at + NE]
                cp(ctlf[:, :, 0], off)
                cp(ctlf[:, :, 1], blocks)
                nc.vector.memset(ctlf[:, :, 3], 0.0)
                link(stt(out=ctlf[:, :, 2], in0=run, scalar=carry[:, 0:1], in1=blocks, op0=ALU.add, op1=ALU.subtract))
                link(ts(carry[:, :], flat[:, at + NE - 1:at + NE], carry[:, 0:1], None, ALU.add))
                cp(ctl[:, :], ctlf[:, :, :].rearrange("p e c -> p (e c)")).then_inc(s_ctl.sem, 1)
                for k in range(0, KD, 2):
                    dve.wait_ge(*s_disp.at(l, k + 1))
                    ts(mTs[:, k, 0:NSLOT], PS[:, DISP_BANK[k], :], g_in[:, l, 2, k:k + 1], None,
                       ALU.mult).then_inc(s_dv.sem, 1)
                for t in range(TT):
                    ts(GT[:, t, :], iota_slot, rt["s1"][:, t, :], rt["w1"][:, t, :], ALU.is_equal, ALU.mult)
                    link(ts(gtmp[:, t, :], iota_slot, rt["s2"][:, t, :], rt["w2"][:, t, :], ALU.is_equal, ALU.mult))
                tt(GT, GT, gtmp, ALU.add).then_inc(s_GT.sem, 1)
                dve.wait_ge(*s_GTt.at(l))
                cp(G.rearrange("p s t -> p (s t)"), bank(0, 2).rearrange("p b n -> p (b n)")).then_inc(s_Gc.sem, 1)
                dve.wait_ge(*s_ctl.at(l))
                with dve.Fori(0, NE) as e:
                    first = dve.value_load(ctl[0:1, ds(e * 4, 1)], min_val=0, max_val=NSLOT)
                    nb = dve.value_load(ctl[0:1, ds(e * 4 + 1, 1)], min_val=1, max_val=MAXB)
                    base = dve.value_load(ctl[0:1, ds(e * 4 + 2, 1)], min_val=0, max_val=2 * (NE + NSLOT // BLK))
                    with dve.Fori(0, nb) as b:
                        dve.wait_ge(s_silu, base + b + 1)
                        tt(hb, sg, PS[:, 4, KF * BLK:2 * KF * BLK], ALU.mult).then_inc(s_hid, 1)
                        dve.wait_ge(s_y, base + b + 1)
                        cp(yTs[:, :, ds(column(first, b), BLK)],
                           bank(5, 2).rearrange("p b (k s) -> p (b k) s", s=BLK)).then_inc(s_yc, 1)
                for j in range(4):
                    dve.wait_ge(*s_yT.at(l, 2 * j + 1))
                    cp(ys[:, j, 0:CB], PS[:, YT_BANK[2 * j], :]).then_inc(s_yv.sem, 1)
                for c in range(2):
                    for t in range(TT):
                        j = 2 * c + t
                        dve.wait_ge(*s_cmb.at(l, j + 1))
                        v = h[:, t, c * CB:(c + 1) * CB]
                        ins = tt(v, v, bank(4 + j), ALU.add)
                ins.then_inc(s_h.sem, 1)
                norm(l, 2)
                evac_pass(l, 3)
                for t in range(TT):
                    for c in range(2):
                        j = 2 * t + c
                        dve.wait_ge(*s_sg.at(l, j + 1))
                        link(tt(prod[:, j, :], sig[:, j, :], bank(4 + j), ALU.mult))
                        v = h[:, t, c * CB:(c + 1) * CB]
                        tt(v, v, prod[:, j, :], ALU.add).then_inc(s_fin.sem, 1)
                dve.wait_ge(*s_fin.at(l))
                dve.sem_inc(s_h.sem, 1)

        @block.tensor
        def _(pe):
            mm = nc.tensor.matmul

            def used():
                pe.drain().then_inc(weights_used, 1)

            def tr(dst, src, rows=P):
                return pe.transpose(dst, src, ident[0:rows, 0:rows] if rows < P else ident)

            def transposed_pass(l, n_, src):
                for t in range(TT):
                    for k in range(KD):
                        b = k // 2
                        c = (k % 2) * SEQ + t * P
                        ins = tr(PS[:, b, c:c + P], src[:, t, k::KD])
                        if t == TT - 1 and k % 2 == 1:
                            ins.then_inc(s_tr.sem, 1)

            def aT_ready(l, n_):
                pe.wait_ge(*s_aTv.at(l, 2 * n_ + 2))
                pe.wait_ge(*s_aTs.at(l, 2 * n_ + 2))

            pe.wait_ge(loaded["const"], 16)
            pe.wait_ge(loaded["p"], 16 * (1 + DEPTH))
            for l in range(DEPTH):
                for k in range(2):
                    for t in range(TT):
                        ins = tr(PS[:, 6 + l, k * SEQ + t * P:k * SEQ + (t + 1) * P], pin[:, l, t, k::2])
            ins.then_inc(one["pTc0"], 1)

            for l in range(DEPTH):
                pe.wait_ge(*s_hn0.at(l, 1))
                pe.wait_ge(*s_hn1.at(l, 1))
                transposed_pass(l, 0, hn)
                aT_ready(l, 0)
                for c, b in enumerate((4, 6, 0, 2)):
                    item = ITEM[l, f"z{c}"]
                    n = SPLITS[c][1] - SPLITS[c][0]
                    w = slots(item, KD, n)
                    arrival(pe, item)
                    if c == 1 and l == 0:
                        pe.wait_ge(one["gains"], 1)
                    for t in range(TT):
                        for k in range(KD):
                            ins = mm(PS[:, b + t, 0:n], aT[:, k, t * P:(t + 1) * P], w[:, k, :], start=(k == 0),
                                     stop=(k == KD - 1))
                    ins.then_inc(s_z.sem, 1)
                    used()
                    if c == 2:
                        pe.wait_ge(*s_lat.at(l))
                        pe.wait_ge(*s_kr.at(l))
                        for t in range(TT):
                            for k in range(2):
                                tr(PS[:, 4, k * SEQ + t * P:k * SEQ + (t + 1) * P], lat[:, t, k:QR:2])
                            ins = tr(PS[:, 5, t * P:(t + 1) * P], lat[:, t, QR:QR + KVR])
                        ins.then_inc(s_lT.sem, 1)
                item = ITEM[l, "uq"]
                w = slots(item, 2, MH * MQK)
                arrival(pe, item)
                pe.wait_ge(*s_lTc.at(l))
                for t, b in enumerate((6, 0)):
                    pe.wait_ge(*(s_dq if t == 0 else s_dk).at(l))
                    for half in range(2):
                        for k in range(2):
                            ins = mm(PS[:, b + half, 0:4 * MQK], cqT[:, k, t * P:(t + 1) * P],
                                     w[:, k, half * 4 * MQK:(half + 1) * 4 * MQK], start=(k == 0), stop=(k == 1))
                    ins.then_inc(s_uq.sem, 1)
                used()
                item = ITEM[l, "ukv"]
                w = slots(item, 2, CB)
                arrival(pe, item)
                for t, b in enumerate((2, 4)):
                    if t == 0:
                        pe.wait_ge(*s_vd.at(l))
                    for half in range(2):
                        ins = mm(PS[:, b + half, :], ckvT[:, t * P:(t + 1) * P], w[:, half, :], start=True, stop=True)
                    ins.then_inc(s_ukv.sem, 1)
                used()
                for idx in range(12):
                    b = HT_BANK[idx]
                    if idx == 0:
                        pe.wait_ge(*s_qr.at(l, 1))
                        pe.wait_ge(*s_qn.at(l, 1))
                    if idx == 2:
                        pe.wait_ge(*s_qr.at(l, 2))
                        pe.wait_ge(*s_qn.at(l, 2))
                    if idx == 4:
                        pe.wait_ge(*s_kn.at(l, 2))
                        pe.wait_ge(*s_vm.at(l, 2))
                    if idx == 8:
                        pe.wait_ge(*s_kpe.at(l, 2))
                        pe.wait_ge(*s_hTv.at(l, 2))
                        pe.wait_ge(*s_hTs.at(l, 2))
                    for j in range(2):
                        for t in range(TT):
                            c = j * SEQ + t * P
                            if idx < 4:
                                hd = 2 * (idx % 2) + j
                                src = (dqr if idx < 2 else dkr)[:, t, hd * P:(hd + 1) * P]
                                ins = tr(PS[:, b, c:c + P], src)
                            else:
                                hd = 2 * ((idx - 4) % 4) + j
                                src = (qm if idx < 8 else km)[:, t, hd * MQK:(hd + 1) * MQK]
                                ins = tr(PS[0:MQK, b, c:c + P], src)
                    ins.then_inc(s_hT.sem, 1)
                pe.wait_ge(*s_hTv.at(l))
                pe.wait_ge(*s_hTs.at(l))

                def scores(m):
                    if m >= 4:
                        pe.wait_ge(*s_exp.at(l, m - 3))
                    b = S_BANK[m % 4]
                    if m < MAPS:
                        r = slice((m % 2) * DHD, (m % 2 + 1) * DHD)
                        q, k = qTd[r, m // 2, :], kTd[r, m // 2, :]
                        rows = r
                    else:
                        rows = slice(0, MQK)
                        q, k = qTm[rows, m - MAPS, :], kTm[rows, m - MAPS, :]
                    mu, mv = cst[rows, C_MU:C_MU + P], cst[rows, C_MV:C_MV + CHUNK]
                    for t in range(TT):
                        a = t * P
                        n = (t + 1) * P
                        mm(PS[:, b, a:a + n], q[:, t * P:(t + 1) * P], k[:, 0:n], start=True, stop=False)
                        ins = mm(PS[:, b, a + n - CHUNK:a + n], mu, mv, start=False, stop=True)
                    ins.then_inc(s_S.sem, 1)

                def turn(m):
                    pe.wait_ge(*s_exp.at(l, m + 1))
                    if m >= 2:
                        pe.wait_ge(*(s_Tv if m % 2 == 0 else s_Ts).at(l, m // 2))
                    for j in range(3):
                        ins = tr(PS[:, T_BANK[m % 2], j * P:(j + 1) * P], prb[:, m % 2, j * P:(j + 1) * P])
                    ins.then_inc(s_T.sem, 1)

                def values(m):
                    pe.wait_ge(*(s_Tv if m % 2 == 0 else s_Ts).at(l, m // 2 + 1))
                    if m >= 2:
                        pe.wait_ge(*s_Oe.at(l, m - 1))
                    b = O_BANK[m % 2]
                    if m < MAPS:
                        n = DV
                        v = [vd[:, t, (m // 2) * DV:(m // 2 + 1) * DV] for t in range(TT)]
                    else:
                        n = MV
                        v = [vm[:, t, (m - MAPS) * MV:(m - MAPS + 1) * MV] for t in range(TT)]
                    w = prT[:, m % 2, :]
                    mm(PS[:, b, 0:n], w[:, 0:P], v[0], start=True, stop=True)
                    mm(PS[:, b, SEQ:SEQ + n], w[:, P:2 * P], v[0], start=True, stop=False)
                    mm(PS[:, b, SEQ:SEQ + n], w[:, 2 * P:3 * P], v[1], start=False, stop=True).then_inc(s_O.sem, 1)

                for i in range(16 + 2):
                    if i < 16:
                        scores(i)
                    if 1 <= i <= 16:
                        turn(i - 1)
                    if i >= 2:
                        values(i - 2)
                pe.wait_ge(*s_oc.at(l))
                transposed_pass(l, 1, ocat)
                aT_ready(l, 1)
                for c in range(2):
                    item = ITEM[l, f"out{c}"]
                    w = slots(item, KD, CB)
                    arrival(pe, item)
                    for t in range(TT):
                        for k in range(KD):
                            ins = mm(bank(4 + 2 * c + t), aT[:, k, t * P:(t + 1) * P], w[:, k, :], start=(k == 0),
                                     stop=(k == KD - 1))
                        ins.then_inc(s_out.sem, 1)
                    used()
                pe.wait_ge(*s_hn0.at(l, 2))
                pe.wait_ge(*s_hn1.at(l, 2))
                transposed_pass(l, 2, hn)
                aT_ready(l, 2)
                for t in range(TT):
                    for k in range(KD):
                        ins = mm(PS[:, 4, t * (NG + NE):(t + 1) * (NG + NE)], aT[:, k, t * P:(t + 1) * P], w_rt[:, l, k, :],
                                 start=(k == 0), stop=(k == KD - 1))
                ins.then_inc(s_rl.sem, 1)
                pe.wait_ge(*s_M.at(l))
                M0, M1 = rt["M"][:, 0, :], rt["M"][:, 1, :]
                mm(PS[:, 5, 0:NE], ones, Mp[:, :], start=True, stop=False)
                mm(PS[:, 5, 0:NE], tri, M0, start=False, stop=True)
                mm(PS[:, 5, NE:2 * NE], ones, Mp[:, :], start=True, stop=False)
                mm(PS[:, 5, NE:2 * NE], ones, M0, start=False, stop=False)
                mm(PS[:, 5, NE:2 * NE], tri, M1, start=False, stop=True)
                mm(PS[:, 5, 2 * NE:3 * NE], ones, Mp[:, :], start=True, stop=True)
                mm(PS[:, 5, 3 * NE:4 * NE], ones, M0, start=True, stop=False)
                mm(PS[:, 5, 3 * NE:4 * NE], ones, M1, start=False, stop=True).then_inc(s_pos.sem, 1)
                pe.wait_ge(*s_P.at(l))
                for k in range(KD):
                    if k >= 6:
                        pe.wait_ge(*(s_dv if k == 6 else s_da).at(l, 1))
                    for t in range(TT):
                        ins = mm(bank(DISP_BANK[k]), hn[:, t, k::KD], pdis[:, t, :], start=(t == 0), stop=(t == TT - 1))
                    ins.then_inc(s_disp.sem, 1)
                pe.wait_ge(*s_GT.at(l))
                pe.wait_ge(*s_dv.at(l))
                pe.wait_ge(*s_da.at(l))
                for s in range(4):
                    for t in range(TT):
                        c = (s % 2) * SEQ + t * P
                        ins = tr(PS[:, s // 2, c:c + P], GT[:, t, s * P:(s + 1) * P])
                ins.then_inc(s_GTt.sem, 1)
                pe.wait_ge(*s_pad.at(l))
                pe.wait_ge(*s_ctl.at(l))
                first = [ITEM[l, ("expert", e)] for e in range(EPI)]
                with pe.Fori(0, EXPERT_ITERS) as i:
                    for u, item in enumerate(first):
                        s0, s1, s2 = item[2]
                        wg = ring[:, s0 * SLOT:(s0 + 1) * SLOT].rearrange("p (k f) -> p k f", k=KD)
                        wu = ring[:, s1 * SLOT:(s1 + 1) * SLOT].rearrange("p (k f) -> p k f", k=KD)
                        wd = ring[:, s2 * SLOT:(s2 + 1) * SLOT].rearrange("p (k d) -> p k d", k=KF)
                        at = (i * EPI + u) * 4
                        nb = pe.value_load(ctl[0:1, ds(at + 1, 1)], min_val=1, max_val=MAXB)
                        base = pe.value_load(ctl[0:1, ds(at + 2, 1)], min_val=0, max_val=2 * (NE + NSLOT // BLK))
                        with pe.Fori(0, nb) as b:
                            pe.wait_ge(s_xb, base + b + 1)
                            for part_ in range(2):
                                pe.wait_ge(arrived[item[2][part_]], i * 16 + 16 * item[4][part_])
                            for q in range(2 * KF):
                                w = (wg, wu)[q // KF]
                                for k in range(KD):
                                    ins = mm(PS[:, 4, q * BLK:(q + 1) * BLK], w[:, k, (q % KF) * P:(q % KF + 1) * P],
                                             xb[:, k, :], start=(k == 0), stop=(k == KD - 1))
                            ins.then_inc(s_gu, 1)
                            pe.wait_ge(s_hid, base + b + 2)
                            pe.wait_ge(s_yc, base + b + 1)
                            pe.wait_ge(arrived[item[2][2]], i * 16 + 16 * item[4][2])
                            for d in range(KD):
                                for k in range(KF):
                                    ins = mm(PS[:, 5 + d // 4, d % 4 * BLK:(d % 4 + 1) * BLK], wd[:, k, d * P:(d + 1) * P],
                                             hb[:, k * BLK:(k + 1) * BLK], start=(k == 0), stop=(k == KF - 1))
                            ins.then_inc(s_y, 1)
                        used()
                pe.wait_ge(*s_Gc.at(l))
                last = pe.value_load(ctl[0:1, 4 * NE - 2:4 * NE - 1], min_val=0, max_val=2 * (NE + NSLOT // BLK))
                nlast = pe.value_load(ctl[0:1, 4 * NE - 3:4 * NE - 2], min_val=1, max_val=MAXB)
                pe.wait_ge(s_yc, last + nlast + 1)
                for j in range(8):
                    if j >= 6:
                        pe.wait_ge(*(s_yv if j == 6 else s_ya).at(l, 1))
                    s, half = j // 2, j % 2
                    for d in range(4):
                        ins = tr(PS[:, YT_BANK[j], d * P:(d + 1) * P], yTs[:, half * 4 + d, s * P:(s + 1) * P])
                    ins.then_inc(s_yT.sem, 1)
                pe.wait_ge(*s_yv.at(l))
                pe.wait_ge(*s_ya.at(l))
                for c in range(2):
                    for t in range(TT):
                        for s in range(4):
                            ins = mm(bank(4 + 2 * c + t), G[:, s, t * P:(t + 1) * P], ys[:, s, c * CB:(c + 1) * CB],
                                     start=(s == 0), stop=(s == 3))
                        ins.then_inc(s_cmb.sem, 1)
                pe.wait_ge(*s_hn0.at(l, 3))
                pe.wait_ge(*s_hn1.at(l, 3))
                transposed_pass(l, 3, hn)
                item = ITEM[l, "proj"]
                w = slots(item, 2, D)
                arrival(pe, item)
                for t in range(TT):
                    for c in range(2):
                        for k in range(2):
                            ins = mm(bank(4 + 2 * t + c), pT[:, l, k, t * P:(t + 1) * P], w[:, k, c * CB:(c + 1) * CB],
                                     start=(k == 0), stop=(k == 1))
                        ins.then_inc(s_pp.sem, 1)
                used()
                aT_ready(l, 3)
                for c in range(2):
                    arrival(pe, ITEM[l, f"gate{c}"])
                for t in range(TT):
                    for c in range(2):
                        w = slots(ITEM[l, f"gate{c}"], KD, CB)
                        for k in range(KD):
                            ins = mm(bank(2 * t + c), aT[:, k, t * P:(t + 1) * P], w[:, k, :], start=(k == 0),
                                     stop=(k == KD - 1))
                        ins.then_inc(s_gt.sem, 1)
                used()
                used()


_INS = ["x", "p", "positions", "attn_norm", "w_in", "q_a_norm", "w_uq", "kv_a_norm", "w_ukv", "mla_q_norm",
        "mla_k_norm", "diff_q_norm", "diff_k_norm", "lambda_q1", "lambda_k1", "lambda_q2", "lambda_k2", "diff_subln",
        "w_out", "ffn_norm", "w_group", "b_group", "w_router", "b_router", "w_gate", "w_up", "w_down", "ple_norm",
        "w_ple_gate", "w_ple_proj"]


def kernel(**inputs):
    import numpy as _np
    import concourse.bacc as _bacc
    from concourse import mybir as _mybir
    from concourse.bass_utils import run_bass_kernel_spmd as _run

    nc = _bacc.Bacc("TRN2", target_bir_lowering=False, num_devices=1)
    arrays, args = {}, []
    for name in _INS:
        a = _np.ascontiguousarray(inputs[name])
        arrays[f"in_{name}"] = a
        args.append(nc.dram_tensor(f"in_{name}", a.shape, _mybir.dt.from_np(a.dtype), kind="ExternalInput").ap())
    const = constants()
    arrays["in_const"] = const
    args.append(nc.dram_tensor("in_const", const.shape, _mybir.dt.float32, kind="ExternalInput").ap())
    args.append(nc.dram_tensor("out_0", (1, SEQ, D), _mybir.dt.float32, kind="ExternalOutput").ap())
    trunk_kernel(nc, *args)
    r = _run(nc, [arrays], core_ids=[0])
    return r.results[0]["out_0"]
```

```python
import math
from contextlib import ExitStack

import concourse.bass as bass
from concourse import mybir

F32 = mybir.dt.float32
F32R = mybir.dt.float32r
I32 = mybir.dt.int32
ALU = mybir.AluOpType
ACT = mybir.ActivationFunctionType
AX = mybir.AxisListType
ds = bass.ds

P = 128
D = 1024
SEQ = 256
DEPTH = 2
TT = SEQ // P
KD = D // P
CHUNK = 64
EPS = 1e-6
PLE = 256
MH, NOPE, ROPE, MV = 8, 64, 32, 64
MQK = NOPE + ROPE
QR, KVR = 256, 128
DH, DHD = 4, 64
DV = 2 * DHD
MAPS = 2 * DH
SPLITS = [(0, 416), (416, 928), (928, 1440), (1440, 1952)]
NG, NEG, FF = 4, 8, 256
NE = NG * NEG
KF = FF // P
BLK = 64
NSLOT = 2 * SEQ
CB = 512

SLOT = 2048
REGIONS = 3
RING = 3 * REGIONS
CHUNKS = 6
CH = 3 * SLOT // CHUNKS
NBUF = 3
POOL_CHUNKS = (2, 5)
DVE_CHUNKS = tuple(c for c in range(CHUNKS) if c not in POOL_CHUNKS)
MAXBLK = NE + NSLOT // BLK

HB = ROPE // 2
HD = DHD // 2
C_ID, C_TRI, C_ONE, C_MU, C_MV = 0, 128, 256, 384, 512
C_IOTA = C_MV + CHUNK
C_FM = C_IOTA + NSLOT
C_FD = C_FM + HB
C_E32 = C_FD + HD
C_G4 = C_E32 + NE
C_MOD = C_G4 + NG
C_J = C_MOD + NE
C_II = C_J + 1
NCONST = C_II + P

INV_2PI = 1.0 / (2.0 * math.pi)
TWO_PI_1 = 6.28125
TWO_PI_2 = 2029 / 2.0 ** 20
TWO_PI_3 = 2.0 * math.pi - TWO_PI_1 - TWO_PI_2
ROUND = 12582912.0
PI = 3.1415925


def constants():
    import numpy as np
    c = np.zeros((P, NCONST), np.float32)
    c[:, C_ID:C_ID + P] = np.eye(P)
    c[:, C_TRI:C_TRI + P] = np.triu(np.ones((P, P)), 1)
    c[:, C_ONE:C_ONE + P] = 1.0
    c[0, C_MU:C_MU + CHUNK] = 1.0
    c[CHUNK, C_MU:C_MU + CHUNK] = 1.0
    c[0, C_MV:C_MV + CHUNK] = -1e30
    c[CHUNK, C_MV:C_MV + CHUNK] = -1e30
    c[:, C_IOTA:C_IOTA + NSLOT] = np.arange(NSLOT)
    c[:, C_FM:C_FM + HB] = np.float32(10000.0) ** (-np.arange(0, ROPE, 2, dtype=np.float32) / ROPE)
    c[:, C_FD:C_FD + HD] = np.float32(10000.0) ** (-np.arange(0, DHD, 2, dtype=np.float32) / DHD)
    c[:, C_E32:C_E32 + NE] = np.arange(NE)
    c[:, C_G4:C_G4 + NG] = np.arange(NG)
    c[:, C_MOD:C_MOD + NE] = np.arange(NE) % REGIONS
    c[:, C_J] = np.arange(P)
    c[:, C_II:C_II + P] = np.tile(np.eye(BLK), (2, 2))
    return c


def stream_plan():
    items, pos, used = {}, 0, 0
    owner = [0] * RING
    fills = [0] * RING
    for layer in range(DEPTH):
        kinds = [("z0", 2), ("z1", 2), ("z2", 2), ("z3", 2), ("uq", 1), ("ukv", 1), ("out0", 2), ("out1", 2)]
        kinds += [(("expert", e), 3) for e in range(NE)]
        kinds += [("proj", 1), ("gate0", 2), ("gate1", 2)]
        for kind, n in kinds:
            expert = isinstance(kind, tuple)
            if kind == ("expert", 0):
                pos += -pos % RING
            if not expert and pos % RING + n > RING:
                pos += RING - pos % RING
            slots = [(pos + j) % RING for j in range(n)]
            dense = max([owner[s] for s in slots if not isinstance(owner[s], tuple)], default=0)
            after = max([owner[s][1] for s in slots if isinstance(owner[s], tuple)], default=None)
            if not expert:
                used += 1
            for j, s in enumerate(slots):
                owner[s] = kind if expert else used
                if not expert and j == 0:
                    fills[s] += 1
            items[layer, kind] = (slots, dense, after, [fills[s] for s in slots])
            pos += n
    return items


ITEM = stream_plan()

N_SMALL = DEPTH * (3 + DH + 4 + 12 + 4 + 4)
HT_BANK = (6, 7, 0, 1, 2, 3, 4, 5, 6, 7, 0, 1)
S_BANK = (5, 6, 7, 0)
T_BANK = (3, 4)
O_BANK = (1, 2)
DISP_BANK = (6, 7, 0, 1, 2, 3, 6, 7)
YT_BANK = (0, 1, 2, 3, 6, 7, 0, 1)


class Stage:

    def __init__(self, sem, n):
        self.sem, self.n = sem, n

    def at(self, layer, k=None):
        return self.sem, layer * self.n + (self.n if k is None else k)


def trunk_kernel(nc, x, p, positions, attn_norm, w_in, q_a_norm, w_uq, kv_a_norm, w_ukv, mla_q_norm,
                 mla_k_norm, diff_q_norm, diff_k_norm, lambda_q1, lambda_k1, lambda_q2, lambda_k2,
                 diff_subln, w_out, ffn_norm, w_group, b_group, w_router, b_router, w_gate, w_up,
                 w_down, ple_norm, w_ple_gate, w_ple_proj, const, out):
    with ExitStack() as ctx:
        def sb(name, shape, dt=F32):
            return ctx.enter_context(nc.sbuf_tensor(name, shape, dt))

        def sem(name):
            return ctx.enter_context(nc.semaphore(name))

        def stage(name, n):
            return Stage(sem(name), n)

        ctx.enter_context(nc.allow_non_contiguous_dma(reason="gains with one value per partition"))

        PS = ctx.enter_context(nc.psum_tensor("PS", [P, 8, CB], F32))

        ring = sb("ring", [P, RING * SLOT])
        cst = sb("cst", [P, NCONST])
        ident = cst[:, C_ID:C_ID + P]
        tri = cst[:, C_TRI:C_TRI + P]
        ones = cst[:, C_ONE:C_ONE + P]
        iota_slot = cst[:, C_IOTA:C_IOTA + NSLOT]
        h = sb("h", [P, TT, D])
        hn = sb("hn", [P, TT, D])
        aT = sb("aT", [P, KD, SEQ])
        g_in = sb("g_in", [P, DEPTH, 4, KD])
        g_cq = sb("g_cq", [P, DEPTH, 2])
        g_ckv = sb("g_ckv", [P, DEPTH, 1])
        g_nope = sb("g_nope", [MQK, DEPTH, 2])
        g_k = sb("g_k", [MQK, DEPTH])
        g_rope = sb("g_rope", [P, DEPTH, 2, 2, ROPE])
        g_diff = sb("g_diff", [P, DEPTH, 2, 2, DHD])
        bias = sb("bias", [P, DEPTH, NG + NE])
        w_rt = sb("w_rt", [P, DEPTH, KD, NG + NE])
        lams = sb("lams", [P, DEPTH, 2])
        lame = sb("lame", [P, DEPTH, 2])
        neglam = sb("neglam", [P, DEPTH])
        posi = sb("posi", [P, TT], I32)
        posf = sb("posf", [P, TT])
        NF = HB + HD
        trig_m = sb("trig_m", [P, 2, TT, 2, HB])
        trig_d = sb("trig_d", [P, 2, TT, 2, HD])
        rope_m = sb("rope_m", [P, 2, 2, TT, ROPE])
        rope_d = sb("rope_d", [P, 2, 2, TT, DHD])
        lss = sb("lss", [P, 2 * TT])
        lms = sb("lms", [P, 2 * TT])
        lrs = sb("lrs", [P, 2 * TT])
        ssh = sb("ssh", [P, TT])
        krs = sb("krs", [P, TT, ROPE])
        krr2 = sb("krr2", [P, TT, ROPE])
        ods = sb("ods", [P, TT * DH])
        odr = sb("odr", [P, TT * DH])
        mstat = sb("mstat", [P, TT])
        rstd = sb("rstd", [P, TT])
        expo = sb("expo", [P, 32])
        AREA = 11904
        area = sb("area", [P, AREA])
        used = [0]

        def part(n, **dims):
            v = area[:, used[0]:used[0] + n]
            used[0] += n
            assert used[0] <= AREA, used[0]
            return v

        lat = part(TT * 384).rearrange("p (t n) -> p t n", t=TT)
        kr = part(TT * ROPE).rearrange("p (t n) -> p t n", t=TT)
        krr = part(TT * ROPE).rearrange("p (t n) -> p t n", t=TT)
        cqT = part(2 * SEQ).rearrange("p (k t) -> p k t", k=2)
        ckvT = part(SEQ)
        junk = part(1024)
        rtmp = part(1024)
        dqr = part(TT * 512).rearrange("p (t n) -> p t n", t=TT)
        dkr = part(TT * 512).rearrange("p (t n) -> p t n", t=TT)
        vd = part(TT * 512).rearrange("p (t n) -> p t n", t=TT)
        vm = part(TT * 512).rearrange("p (t n) -> p t n", t=TT)
        qTm = part(MH * SEQ).rearrange("p (h t) -> p h t", h=MH)
        kTm = part(MH * SEQ).rearrange("p (h t) -> p h t", h=MH)
        vmf = vm.rearrange("p t n -> p (t n)")
        lamv = vmf[:, 0:DEPTH * 4 * DHD].rearrange("p (l j n) -> p l j n", l=DEPTH, j=4)
        lamp = vmf[:, DEPTH * 4 * DHD:DEPTH * 4 * DHD + 2 * DHD].rearrange("p (j n) -> p j n", j=2)
        kTf = kTm.rearrange("p h t -> p (h t)")
        nang = TT * 2 * NF
        ang, turns, red, trig_raw = (kTf[:, i * nang:(i + 1) * nang].rearrange("p (t c n) -> p t c n", t=TT, c=2)
                                     for i in range(4))
        hnf = hn[:, :, :].rearrange("p t n -> p (t n)")
        qm = hnf[:, 0:TT * MH * MQK].rearrange("p (t n) -> p t n", t=TT)
        ocat = sb("ocat", [P, TT, D])
        ocf = ocat[:, :, :].rearrange("p t n -> p (t n)")
        km = ocf[:, 0:TT * MH * MQK].rearrange("p (t n) -> p t n", t=TT)
        actjunk = ocf[:, 0:TT * D].rearrange("p (t n) -> p t n", t=TT)
        aTf = aT[:, :, :].rearrange("p k t -> p (k t)")
        qTd = aTf[:, 0:DH * SEQ].rearrange("p (h t) -> p h t", h=DH)
        kTd = aTf[:, DH * SEQ:2 * DH * SEQ].rearrange("p (h t) -> p h t", h=DH)
        prb = sb("prb", [P, 2, 384])
        prT = rtmp[:, 256:1024].rearrange("p (b n) -> p b n", b=2)
        ssq = sb("ssq", [P, 4, TT, 8])
        rsq = sb("rsq", [P, 4, TT, 8])
        sskr = sb("sskr", [P, TT])
        qsc = sb("qsc", [P, 2, 2, TT, 8])
        mx = sb("mx", [P, 16, TT])
        nbias = sb("nbias", [P, 16, TT])
        sums = sb("sums", [P, 16, TT])
        rinv = sb("rinv", [P, 16, TT])
        used[0] = 0
        mTs = part(KD * (NSLOT + BLK)).rearrange("p (k s) -> p k s", k=KD)
        yTs = part(KD * (NSLOT + BLK)).rearrange("p (k s) -> p k s", k=KD)
        ys = area[:, 0:4 * D].rearrange("p (s d) -> p s d", s=4)
        pdis = part(TT * NSLOT).rearrange("p (t s) -> p t s", t=TT)
        GT = part(TT * NSLOT).rearrange("p (t s) -> p t s", t=TT)
        G = pdis.rearrange("p t s -> p (t s)").rearrange("p (s t) -> p s t", s=4)
        GTf = GT.rearrange("p t s -> p (t s)")
        pin = GTf[:, 0:TT * PLE].rearrange("p (t n) -> p t n", t=TT)
        pT = GTf[:, TT * PLE:2 * TT * PLE].rearrange("p (k t) -> p k t", k=2)
        gtmp = ocat[:, :, 0:NSLOT]
        gur = ocf[:, 0:CB]
        yraw = ocf[:, CB:CB + D]
        sg = ocf[:, CB + D:CB + D + KF * BLK].rearrange("p (k s) -> p k s", k=KF)
        hb = ocf[:, CB + D + KF * BLK:CB + D + 2 * KF * BLK].rearrange("p (k s) -> p k s", k=KF)
        w_hi = sb("w_hi", [P, NBUF, CH], F32R)
        w_lo = sb("w_lo", [P, NBUF, CH], F32R)
        x_hl = sb("x_hl", [P, KD, 2 * BLK], F32R)
        h_hl = sb("h_hl", [P, KF, 2 * BLK], F32R)
        raw = ring[:, :].rearrange("p (r s n) -> p r s n", r=REGIONS, s=3)
        rt = {}
        for name, shape in dict(lg=NG + NE, gmax=1, geq=NG, gc=NG, gi=1, goh=NG, gd=NG, ge=NG, gs=1, gw=1, pen=NG,
                                ml=NE, m1=1, eq=NE, c1=NE, i1=1, oh1=NE, ml2=NE, m2=1, c2=NE, i2=1, oh2=NE,
                                dm=1, e2=1, w2=1, w1=1, den=1, M=NE, Mpre=NE, s1=1, s2=1, t1=NE, t2=NE).items():
            rt[name] = sb("rt_" + name, [P, TT, shape])
        Mp = sb("Mp", [P, NE])
        cnt = sb("cnt", [P, 4, NE])
        pfx = sb("pfx", [P, 4, NE])
        boh = sb("boh", [P, 4, NE])
        blk4 = sb("blk4", [P, 4])
        carry = sb("carry", [1, 1])
        ctl = sb("ctl", [4, 1 + P], I32)
        ctle = sb("ctle", [1, NE + 2], I32)
        ctlef = sb("ctlef", [1, NE + 2])
        sig = area[:, 4 * D:4 * D + 4 * CB].rearrange("p (j n) -> p j n", j=4)
        prod = area[:, 6 * D:6 * D + 4 * CB].rearrange("p (j n) -> p j n", j=4)

        arrived = [sem(f"arrived{s}") for s in range(RING)]
        expert_arrived = [sem(f"expert_arrived{r}") for r in range(REGIONS)]
        weights_used = sem("weights_used")
        loaded = {k: sem("loaded_" + k) for k in ("x", "const", "p", "small")}
        sem_pool, sem_dve = sem("pool_order"), sem("dve_order")
        one = {k: sem("one_" + k) for k in ("pow", "posf", "pTc0", "lamp", "lame", "ang", "sin", "trig", "gains")}
        s_sq = stage("sq", 3 * TT)
        s_ms = stage("ms", 3)
        s_rs = stage("rs", 3)
        s_hn0 = stage("hn0", 3)
        s_hn1 = stage("hn1", 3)
        s_tr = stage("tr", 4 * 4)
        s_aTv = stage("aTv", 4 * 2)
        s_aTs = stage("aTs", 4 * 2)
        s_z = stage("z", 4)
        s_lsq = stage("lsq", 1)
        s_lms = stage("lms", 1)
        s_lrs = stage("lrs", 1)
        s_lat = stage("lat", 1)
        s_lT = stage("lT", 1)
        s_lTc = stage("lTc", 1)
        s_junk = stage("junk", 6)
        s_sum = stage("sum", 6)
        s_vd = stage("vd", 1)
        s_uq = stage("uq", TT)
        s_ukv = stage("ukv", TT)
        s_qn = stage("qn", TT)
        s_vm = stage("vm", TT)
        s_kn = stage("kn", TT)
        s_hms = stage("hms", 5)
        s_hrs = stage("hrs", 5)
        s_kr = stage("kr", 1)
        s_krr = stage("krr", 1)
        s_kpe = stage("kpe", TT)
        s_tab = stage("tab", 1)
        s_dq = stage("dq", 1)
        s_dk = stage("dk", 1)
        s_qr = stage("qr", TT)
        s_hT = stage("hT", 12)
        s_hTv = stage("hTv", 6)
        s_hTs = stage("hTs", 6)
        s_S = stage("S", 16)
        s_nb = stage("nb", 16)
        s_exp = stage("exp", 16)
        s_T = stage("T", 16)
        s_Tv = stage("Tv", 8)
        s_Ts = stage("Ts", 8)
        s_O = stage("O", 16)
        s_Oe = stage("Oe", 16)
        s_od = stage("od", 1)
        s_oc = stage("oc", 1)
        s_out = stage("out", 4)
        s_h = stage("hready", 3)
        s_rl = stage("rl", 1)
        s_ra = stage("ra", 2)
        s_re = stage("re", 2)
        s_M = stage("M", 1)
        s_pos = stage("pos", 1)
        s_ctl = stage("ctl", 1)
        s_P = stage("P", 1)
        s_GT = stage("GT", 1)
        s_GTt = stage("GTt", 1)
        s_Gc = stage("Gc", 1)
        s_disp = stage("disp", KD)
        s_dv = stage("dv", KD // 2)
        s_da = stage("da", KD // 2)
        s_pad = stage("pad", 1)
        s_Gl = stage("Gl", 1)
        s_pTt = stage("pTt", 1)
        s_pTc = stage("pTc", 1)
        s_blkT = stage("blkT", 1)
        s_blk = stage("blk", 1)
        s_used = stage("moe_used", 1)
        expert_ready = sem("expert_ready")
        region_free = sem("region_free")
        s_xh = sem("x_hi")
        s_xl = sem("x_lo")
        s_hi = sem("w_hi_ready")
        s_lod = sem("w_lo_dve")
        s_lop = sem("w_lo_pool")
        s_ch = sem("chunk_used")
        s_gue = sem("gu_copied")
        s_B = sem("gu_turned")
        s_silu = sem("silu")
        s_hs = sem("h_steps")
        s_hl = sem("h_ready")
        s_C = sem("down")
        s_ye = sem("y_copied")
        s_D = sem("y_turned")
        s_yc = sem("y_placed")
        s_yT = stage("yT", 8)
        s_yv = stage("yv", 4)
        s_ya = stage("ya", 4)
        s_cmb = stage("cmb", 4)
        s_pp = stage("pp", 4)
        s_gt = stage("gt", 4)
        s_sg = stage("sg", 4)
        s_fin = stage("fin", 4)
        stored = sem("stored")

        def bank(b, n=1):
            return PS[:, b, :] if n == 1 else PS[:, b:b + n, :]

        def slots(item, k, n):
            s = item[0][0]
            return ring[:, s * SLOT:s * SLOT + k * n].rearrange("p (k n) -> p k n", k=k)

        def arrival(eng, item):
            eng.wait_ge(arrived[item[0][0]], 16 * item[3][0])

        def s_sq_at(l, k):
            return s_sq.at(l, TT * (k + 1))

        def hT_dest(l, idx):
            if idx < 4:
                a = 2 * (idx % 2)
                return P, (qTd if idx < 2 else kTd)[:, a:a + 2, :], None
            a = 2 * ((idx - 4) % 4)
            return MQK, (qTm if idx < 8 else kTm)[0:MQK, a:a + 2, :], None if idx < 8 else g_k[:, l:l + 1]

        def block_column(eng, j):
            return eng.value_load(ctl[0:1, ds(j, 1)], min_val=0, max_val=NSLOT)

        def block_counts(eng):
            blocks = eng.value_load(ctle[0:1, NE:NE + 1], min_val=NE, max_val=MAXBLK)
            before = eng.value_load(ctle[0:1, NE + 1:NE + 2], min_val=0, max_val=DEPTH * MAXBLK)
            return blocks, before

        def raw_chunk(region, c):
            if c < 4:
                return raw[:, ds(region, 1), 0:2, c * 512:(c + 1) * 512].rearrange("p o s n -> p (o s) n")
            return raw[:, ds(region, 1), 2:3, (c - 4) * CH:(c - 3) * CH].rearrange("p o s n -> p (o s) n")

        def part_chunk(t, c):
            v = t[:, c % NBUF, :]
            return v.rearrange("p (s n) -> p s n", s=2 if c < 4 else 1)

        block = ctx.enter_context(nc.Block())

        @block.sync
        def _(sp):
            for t in range(TT):
                sp.dma_start(h[:, t, :], x[0, t * P:(t + 1) * P, :]).then_inc(loaded["x"], 16)
            sp.dma_start(cst[:, :], const).then_inc(loaded["const"], 16)

            def load(layer, kind):
                item = ITEM[layer, kind]
                slot, dense, after, _ = item
                if dense:
                    sp.wait_ge(weights_used, dense)
                if after is not None:
                    sp.wait_ge(s_C, sp.value_load(ctle[0:1, after:after + 1], min_val=1, max_val=999) + 1)
                    sp.sem_inc(region_free, 1)
                s = slot[0]
                if kind[0] == "z":
                    a, b = SPLITS[int(kind[1])]
                    src = w_in[layer].rearrange("(p k) n -> p k n", k=KD)[:, :, a:b]
                    dst = slots(item, KD, b - a)
                elif kind == "uq":
                    src = w_uq[layer].rearrange("(p k) n -> p k n", k=2)
                    dst = slots(item, 2, MH * MQK)
                elif kind == "ukv":
                    src = w_ukv[layer]
                    dst = ring[:, s * SLOT:s * SLOT + 1024]
                elif kind[:3] == "out" or kind[:4] == "gate":
                    c = int(kind[-1])
                    w = w_out if kind[:3] == "out" else w_ple_gate
                    src = w[layer].rearrange("(p k) n -> p k n", k=KD)[:, :, c * CB:(c + 1) * CB]
                    dst = slots(item, KD, CB)
                else:
                    src = w_ple_proj[layer].rearrange("(p k) n -> p k n", k=2)
                    dst = slots(item, 2, D)
                sp.dma_start(dst, src).then_inc(arrived[s], 16)

            def load_expert(layer, e, region):
                for part_, w in enumerate((w_gate, w_up, w_down)):
                    s = 3 * region + part_
                    if part_ < 2:
                        src = w[layer].rearrange("g e (p k) f -> (g e) p (k f)", k=KD)[ds(e, 1)]
                        src = src.rearrange("o p n -> (o p) n")
                        dst = ring[:, s * SLOT:(s + 1) * SLOT]
                    else:
                        src = w[layer].rearrange("g e (k p) d -> (g e) p k d", p=P)[ds(e, 1)]
                        src = src.rearrange("o p k d -> (o p) k d")
                        dst = ring[:, s * SLOT:(s + 1) * SLOT].rearrange("p (k d) -> p k d", k=KF)
                    sp.dma_start(dst, src).then_inc(expert_arrived[region], 16)

            def ready(layer, region, turn):
                fills = layer * len(range(region, NE, REGIONS)) + 1
                sp.wait_ge(expert_arrived[region], (turn + fills) * (3 * 16))
                sp.sem_inc(expert_ready, 1)

            def next_expert(layer, e, region, turn):
                over = sp.value_load(ctle[0:1, ds(e - REGIONS, 1)], min_val=1, max_val=999)
                sp.wait_ge(s_C, over + 1)
                sp.sem_inc(region_free, 1)
                load_expert(layer, e, region)
                before = (region - 1) % REGIONS
                ready(layer, before, turn - (1 if region == 0 else 0))

            for layer in range(DEPTH):
                for kind in ("z0", "z1", "z2", "z3", "uq", "ukv", "out0", "out1"):
                    load(layer, kind)
                for e in range(REGIONS):
                    dense = ITEM[layer, ("expert", e)][1]
                    if dense:
                        sp.wait_ge(weights_used, dense)
                    load_expert(layer, e, e)
                for e in range(REGIONS - 1):
                    ready(layer, e, 0)
                sp.wait_ge(*s_ctl.at(layer))
                with sp.Fori(1, NE // REGIONS) as i:
                    for r in range(REGIONS):
                        next_expert(layer, i * REGIONS + r, r, i)
                for e in range(NE // REGIONS * REGIONS, NE):
                    next_expert(layer, e, e % REGIONS, e // REGIONS)
                ready(layer, (NE - 1) % REGIONS, (NE - 1) // REGIONS)
                sp.wait_ge(*s_Gc.at(layer))
                sp.dma_start(pin, p[layer, 0].rearrange("(t p) n -> p t n", p=P)).then_inc(s_Gl.sem, 16)
                for kind in ("proj", "gate0", "gate1"):
                    load(layer, kind)
            for t in range(TT):
                for c in range(2):
                    sp.wait_ge(*s_fin.at(DEPTH - 1, 2 * t + c + 1))
                    sp.dma_start(out[0, t * P:(t + 1) * P, c * CB:(c + 1) * CB],
                                 h[:, t, c * CB:(c + 1) * CB]).then_inc(stored, 16)
            sp.wait_ge(stored, 16 * 2 * TT)

        @block.gpsimd
        def _(pool):
            chain = [0]
            s_chain = sem_pool

            def link(ins):
                chain[0] += 1
                ins.then_inc(s_chain, 1)
                pool.wait_ge(s_chain, chain[0])

            nc.gpsimd.memset(expo[:, :], -0.5).then_inc(one["pow"], 1)
            pool.wait_ge(one["pow"], 1)
            def root(dst, src, n, wait, done):
                pool.wait_ge(*wait)
                nc.gpsimd.tensor_tensor(dst, src, expo[:, 0:n], ALU.pow).then_inc(done.sem, 1)

            for l in range(DEPTH):
                root(rstd[:, :], mstat[:, :], TT, s_ms.at(l, 1), s_rs)
                pool.wait_ge(one["trig"], 6)
                pool.wait_ge(loaded["small"], 16 * N_SMALL)
                if l:
                    pool.wait_ge(*s_qr.at(l - 1))
                    pool.wait_ge(*s_krr.at(l - 1))
                for qk in range(2):
                    for cs in range(2):
                        g = g_rope[:, l, qk, cs, :].unsqueeze(1).broadcast_to([P, TT, ROPE])
                        link(nc.gpsimd.tensor_tensor(rope_m[:, qk, cs], trig_m[:, cs].rearrange("p t a n -> p t (a n)"),
                                                     g, ALU.mult))
                        g = g_diff[:, l, qk, cs, :].unsqueeze(1).broadcast_to([P, TT, DHD])
                        ins = nc.gpsimd.tensor_tensor(rope_d[:, qk, cs], trig_d[:, cs].rearrange("p t a n -> p t (a n)"),
                                                      g, ALU.mult)
                        if qk == 1 and cs == 1:
                            ins.then_inc(s_tab.sem, 1)
                        else:
                            link(ins)

                root(lrs[:, :], lms[:, :], 4, s_lms.at(l), s_lrs)

                def head_root(w):
                    root(rsq[:, w].rearrange("p t h -> p (t h)"), ssq[:, w].rearrange("p t h -> p (t h)"), 16,
                         s_hms.at(l, w + 1), s_hrs)

                head_root(0)
                pool.wait_ge(*s_kr.at(l))
                pool.wait_ge(*s_tab.at(l))
                c_, s_ = rope_m[:, 1, 0], rope_m[:, 1, 1]
                t_ = krs[:, :, :]
                link(nc.gpsimd.tensor_tensor(krr, kr, c_, ALU.mult))
                link(nc.gpsimd.tensor_tensor(t_[:, :, 0:HB], kr[:, :, HB:ROPE], s_[:, :, 0:HB], ALU.mult))
                link(nc.gpsimd.tensor_tensor(t_[:, :, HB:ROPE], kr[:, :, 0:HB], s_[:, :, HB:ROPE], ALU.mult))
                link(nc.gpsimd.tensor_tensor(krr, krr, t_, ALU.add))
                nc.gpsimd.tensor_copy(krr2[:, :, :], krr).then_inc(s_krr.sem, 1)
                head_root(1)
                head_root(2)
                head_root(3)
                pool.wait_ge(*s_hrs.at(l, 4))
                pool.wait_ge(*s_krr.at(l))
                for t in range(TT):
                    kv = km[:, t, :].rearrange("p (h n) -> p h n", h=MH)[:, :, NOPE:MQK]
                    nc.gpsimd.tensor_tensor(kv, krr2[:, t, :].unsqueeze(1).broadcast_to([P, MH, ROPE]),
                                            rsq[:, 3, t, :].unsqueeze(2).broadcast_to([P, MH, ROPE]),
                                            ALU.mult).then_inc(s_kpe.sem, 1)
                pool.wait_ge(*s_hms.at(l, 5))
                nc.gpsimd.tensor_tensor(odr[:, :], ods[:, :], expo[:, 0:TT * DH], ALU.pow).then_inc(s_hrs.sem, 1)
                root(rstd[:, :], mstat[:, :], TT, s_ms.at(l, 2), s_rs)
                nc.gpsimd.memset(mTs[:, :, NSLOT:NSLOT + BLK], 0.0).then_inc(s_pad.sem, 1)
                pool.wait_ge(*s_ctl.at(l))
                blocks, before = block_counts(pool)
                with pool.Fori(0, blocks) as j:
                    region = pool.value_load(ctl[1:2, ds(j + 1, 1)], min_val=0, max_val=REGIONS - 1)
                    for n, c in enumerate(POOL_CHUNKS):
                        pool.wait_ge(s_hi, (before + j) * CHUNKS + (c + 1))
                        nc.gpsimd.tensor_tensor(part_chunk(w_lo, c), raw_chunk(region, c),
                                                part_chunk(w_hi, c).bitcast(F32), ALU.subtract).then_inc(s_lop, 1)
                root(rstd[:, :], mstat[:, :], TT, s_ms.at(l, 3), s_rs)

        @block.scalar
        def _(act):
            act.dma_start(posi[:, :], positions.rearrange("b (t p) -> p (b t)", p=P)).then_inc(loaded["p"], 16)
            n = [0]

            def small_load(dst, src):
                n[0] += 1
                act.dma_start(dst, src).then_inc(loaded["small"], 16)

            for l in range(DEPTH):
                small_load(g_in[:, l, 0, :], attn_norm[l].rearrange("(p k) -> p k", k=KD))
                small_load(g_in[:, l, 2, :], ffn_norm[l].rearrange("(p k) -> p k", k=KD))
                small_load(g_in[:, l, 3, :], ple_norm[l].rearrange("(p k) -> p k", k=KD))
                for hd in range(DH):
                    small_load(g_in[64 + 16 * hd:80 + 16 * hd, l, 1, :], diff_subln[l].rearrange("(p k) -> p k", k=KD))
                small_load(g_cq[:, l, :], q_a_norm[l].rearrange("(p k) -> p k", k=2))
                small_load(g_ckv[:, l, :], kv_a_norm[l].rearrange("(p k) -> p k", k=1))
                small_load(g_nope[0:NOPE, l, 0:1], mla_q_norm[l, 0:NOPE].rearrange("(p k) -> p k", k=1))
                small_load(g_nope[0:NOPE, l, 1:2], mla_k_norm[l, 0:NOPE].rearrange("(p k) -> p k", k=1))
                for qk, (gm, gd) in enumerate(((mla_q_norm, diff_q_norm), (mla_k_norm, diff_k_norm))):
                    small_load(g_rope[:, l, qk, 0, :], gm[l, NOPE:MQK].partition_broadcast(P))
                    small_load(g_rope[:, l, qk, 1, 0:HB], gm[l, NOPE + HB:MQK].partition_broadcast(P))
                    small_load(g_rope[:, l, qk, 1, HB:ROPE], gm[l, NOPE:NOPE + HB].partition_broadcast(P))
                    small_load(g_diff[:, l, qk, 0, :], gd[l].partition_broadcast(P))
                    small_load(g_diff[:, l, qk, 1, 0:HD], gd[l, HD:DHD].partition_broadcast(P))
                    small_load(g_diff[:, l, qk, 1, HD:DHD], gd[l, 0:HD].partition_broadcast(P))
                small_load(bias[:, l, 0:NG], b_group[l].partition_broadcast(P))
                small_load(bias[:, l, NG:NG + NE], b_router[l].partition_broadcast(P))
                small_load(w_rt[:, l, :, 0:NG], w_group[l].rearrange("(p k) n -> p k n", k=KD))
                small_load(w_rt[:, l, :, NG:NG + NE], w_router[l].rearrange("(p k) n -> p k n", k=KD))
                for j, v in enumerate((lambda_q1, lambda_k1, lambda_q2, lambda_k2)):
                    small_load(lamv[:, l, j, :], v[l].partition_broadcast(P))
            assert n[0] == N_SMALL
            def square_tiles(l, k):
                for t in range(TT):
                    if t == 0:
                        if k == 0 and l == 0:
                            act.wait_ge(loaded["x"], 32)
                        elif k == 0:
                            act.wait_ge(*s_h.at(l - 1, 3))
                        else:
                            act.wait_ge(*s_h.at(l, k))
                    act.activation(actjunk[:, t, :], h[:, t, :], ACT.Square, accum_out=ssh[:, t:t + 1]).then_inc(s_sq.sem, 1)

            def norm_tile(l, k):
                act.wait_ge(*s_rs.at(l, k + 1))
                act.activation(hn[:, 0, :], h[:, 0, :], ACT.Copy, scale=rstd[:, 0:1]).then_inc(s_hn0.sem, 1)

            def evac_pass(l, n_):
                for b in (2, 3):
                    act.wait_ge(*s_tr.at(l, 4 * n_ + b + 1))
                    for k in (2 * b, 2 * b + 1):
                        ins = act.activation(aT[:, k, :], PS[:, b, (k % 2) * SEQ:(k % 2 + 1) * SEQ], ACT.Copy,
                                             scale=g_in[:, l, n_, k:k + 1])
                    ins.then_inc(s_aTs.sem, 1)

            for l in range(DEPTH):
                square_tiles(l, 0)
                norm_tile(l, 0)
                if l == 0:
                    act.wait_ge(one["ang"], 1)
                    for cs in range(2):
                        act.activation(trig_raw[:, :, cs, :], red[:, :, cs, :], ACT.Sin).then_inc(one["sin"], 1)
                    act.wait_ge(one["lamp"], 2 * DEPTH)
                    act.activation(lame[:, :, :], lams[:, :, :], ACT.Exp).then_inc(one["lame"], 1)
                    act.wait_ge(one["gains"], 1)
                evac_pass(l, 0)
                act.wait_ge(*s_z.at(l, 1))
                for t in range(TT):
                    act.activation(actjunk[:, t, 0:QR], PS[:, 4 + t, 0:QR], ACT.Square, accum_out=lss[:, t:t + 1])
                    ins = act.activation(actjunk[:, t, QR:QR + KVR], PS[:, 4 + t, QR:QR + KVR], ACT.Square,
                                         accum_out=lss[:, 2 + t:3 + t])
                ins.then_inc(s_lsq.sem, 1)
                act.wait_ge(*s_z.at(l, 2))
                act.activation(junk, bank(6, 2).rearrange("p t n -> p (t n)"), ACT.Square).then_inc(s_junk.sem, 1)
                act.wait_ge(*s_z.at(l, 3))
                act.wait_ge(*s_sum.at(l, 1))
                act.activation(junk, bank(0, 2).rearrange("p t n -> p (t n)"), ACT.Square).then_inc(s_junk.sem, 1)
                act.wait_ge(*s_z.at(l, 4))
                act.activation(vd.rearrange("p t n -> p (t n)"), bank(2, 2).rearrange("p t n -> p (t n)"),
                               ACT.Copy).then_inc(s_vd.sem, 1)
                for t, b in enumerate((6, 0)):
                    act.wait_ge(*s_uq.at(l, t + 1))
                    act.wait_ge(*s_sum.at(l, 2 + t))
                    src = bank(b, 2)[:, :, 0:4 * MQK]
                    act.activation(junk[:, 0:MH * MQK].rearrange("p (b n) -> p b n", b=2), src,
                                   ACT.Square).then_inc(s_junk.sem, 1)
                    dst = qm[:, t, :].rearrange("p (b h n) -> p b h n", b=2, h=4)[:, :, :, 0:NOPE]
                    srcn = src.rearrange("p b (h n) -> p b h n", h=4)[:, :, :, 0:NOPE]
                    act.activation(dst, srcn, ACT.Copy).then_inc(s_qn.sem, 1)
                for t, b in enumerate((2, 4)):
                    act.wait_ge(*s_ukv.at(l, t + 1))
                    src = bank(b, 2).rearrange("p b (h n) -> p b h n", h=4)
                    if t == 0:
                        act.wait_ge(*s_sum.at(l, 4))
                    dst = junk.rearrange("p (t b h n) -> p t b h n", t=2, b=2, h=4)[:, t]
                    ins = act.activation(dst, src[:, :, :, 0:NOPE], ACT.Square)
                    if t == 1:
                        ins.then_inc(s_junk.sem, 1)
                    act.activation(vm[:, t, :].rearrange("p (b h n) -> p b h n", b=2, h=4), src[:, :, :, NOPE:],
                                   ACT.Copy).then_inc(s_vm.sem, 1)
                for j in range(6):
                    idx = 2 * j + 1
                    act.wait_ge(*s_hT.at(l, idx + 1))
                    rows, dst, gain = hT_dest(l, idx)
                    src = PS[0:rows, HT_BANK[idx], :].rearrange("p (h t) -> p h t", h=2)
                    if gain is None:
                        act.activation(dst, src, ACT.Copy).then_inc(s_hTs.sem, 1)
                    else:
                        act.activation(dst, src, ACT.Copy, scale=gain).then_inc(s_hTs.sem, 1)
                for m in range(16 + 1):
                    if m < 16:
                        act.wait_ge(*s_nb.at(l, m + 1))
                        if m >= 2:
                            act.wait_ge(*s_T.at(l, m - 1))
                        kind, hd = (0, m) if m < MAPS else (1, m - MAPS)
                        b = S_BANK[m % 4]
                        act.activation(prb[:, m % 2, 0:P], PS[:, b, 0:P], ACT.Exp, bias=nbias[:, m, 0:1],
                                       scale=qsc[:, kind, 0, 0, hd:hd + 1], accum_out=sums[:, m, 0:1])
                        act.activation(prb[:, m % 2, P:3 * P], PS[:, b, P:3 * P], ACT.Exp, bias=nbias[:, m, 1:2],
                                       scale=qsc[:, kind, 0, 1, hd:hd + 1],
                                       accum_out=sums[:, m, 1:2]).then_inc(s_exp.sem, 1)
                    if m >= 1 and (m - 1) % 2 == 1:
                        j = m - 1
                        act.wait_ge(*s_T.at(l, j + 1))
                        if j >= 2:
                            act.wait_ge(*s_O.at(l, j - 1))
                        act.activation(prT[:, 1, :], PS[:, 4, 0:384], ACT.Copy).then_inc(s_Ts.sem, 1)
                    if m == MAPS + 3:
                        act.wait_ge(*s_od.at(l))
                        act.activation(junk.rearrange("p (t n) -> p t n", t=TT), ocat[:, :, 512:1024],
                                       ACT.Square).then_inc(s_junk.sem, 1)
                evac_pass(l, 1)
                square_tiles(l, 1)
                norm_tile(l, 1)
                evac_pass(l, 2)
                act.wait_ge(*s_ra.at(l, 1))
                act.activation(rt["ge"][:, :, :], rt["gd"][:, :, :], ACT.Exp).then_inc(s_re.sem, 1)
                act.wait_ge(*s_ra.at(l, 2))
                act.activation(rt["e2"][:, :, :], rt["dm"][:, :, :], ACT.Exp).then_inc(s_re.sem, 1)
                for k in range(1, KD, 2):
                    act.wait_ge(*s_disp.at(l, k + 1))
                    act.activation(mTs[:, k, 0:NSLOT], PS[:, DISP_BANK[k], :], ACT.Copy,
                                   scale=g_in[:, l, 2, k:k + 1]).then_inc(s_da.sem, 1)
                act.wait_ge(*s_ctl.at(l))
                act.wait_ge(*s_dv.at(l))
                act.wait_ge(*s_da.at(l))
                act.wait_ge(*s_pad.at(l))
                blocks, before = block_counts(act)
                with act.Fori(0, blocks) as j:
                    first = block_column(act, j + 1)
                    region = act.value_load(ctl[1:2, ds(j + 1, 1)], min_val=0, max_val=REGIONS - 1)
                    expert = act.value_load(ctl[2:3, ds(j + 1, 1)], min_val=1, max_val=NE)
                    act.wait_ge(s_ch, (before + j) * CHUNKS + 1)
                    act.activation(x_hl[:, :, 0:BLK], mTs[:, :, ds(first, BLK)], ACT.Copy).then_inc(s_xh, 1)
                    act.wait_ge(expert_ready, expert + l * NE)
                    for c in range(CHUNKS):
                        act.wait_ge(s_ch, (before + j) * CHUNKS + (c + 1))
                        act.activation(part_chunk(w_hi, c), raw_chunk(region, c), ACT.Copy).then_inc(s_hi, 1)
                    act.wait_ge(s_ch, (before + j) * CHUNKS + (4 + NBUF))
                    act.activation(gur, PS[:, 4, :], ACT.Copy).then_inc(s_gue, 1)
                    act.wait_ge(s_B, before + j + 1)
                    act.activation(sg, PS[:, 5, :].rearrange("p (q s) -> p q s", q=4)[:, 0:KF, 0:BLK],
                                   ACT.Silu).then_inc(s_silu, 1)
                for j in range(4):
                    act.wait_ge(*s_yT.at(l, 2 * j + 2))
                    act.activation(ys[:, j, CB:2 * CB], PS[:, YT_BANK[2 * j + 1], :], ACT.Copy).then_inc(s_ya.sem, 1)
                square_tiles(l, 2)
                norm_tile(l, 2)
                evac_pass(l, 3)
                for j in range(4):
                    act.wait_ge(*s_gt.at(l, j + 1))
                    act.activation(sig[:, j, :], PS[:, j, :], ACT.Sigmoid).then_inc(s_sg.sem, 1)

        @block.vector
        def _(dve):
            chain = [0]

            def link(ins):
                chain[0] += 1
                ins.then_inc(sem_dve, 1)
                dve.wait_ge(sem_dve, chain[0])

            tt, ts, stt = nc.vector.tensor_tensor, nc.vector.tensor_scalar, nc.vector.scalar_tensor_tensor
            cp, red_ = nc.vector.tensor_copy, nc.vector.tensor_reduce

            dve.sem_inc(s_ch, NBUF)
            dve.sem_inc(s_C, 1)
            dve.sem_inc(s_D, 1)
            dve.sem_inc(s_yc, 1)
            nc.vector.memset(g_in[0:64, :, 1, :], 1.0)
            nc.vector.memset(g_k[:, :], 1.0)
            link(nc.vector.memset(carry[:, :], 0.0))

            def rotary_angles():
                dve.wait_ge(loaded["const"], 16)
                dve.wait_ge(loaded["p"], 16)
                link(cp(posf[:, :], posi[:, :]))
                freq = cst[:, C_FM:C_FM + NF]
                for t in range(TT):
                    for cs in range(2):
                        ins = ts(ang[:, t, cs, :], freq, posf[:, t:t + 1], None, ALU.mult)
                link(ins)
                for cs in range(2):
                    ins = ts(turns[:, :, cs, :], ang[:, :, cs, :], INV_2PI, 0.25 * (1 - cs), ALU.mult, ALU.add)
                link(ins)
                link(ts(turns[:, :, :, :], turns[:, :, :, :], ROUND, None, ALU.add))
                link(ts(turns[:, :, :, :], turns[:, :, :, :], -ROUND, None, ALU.add))
                link(stt(out=red[:, :, :, :], in0=turns[:, :, :, :], scalar=-TWO_PI_1, in1=ang[:, :, :, :],
                         op0=ALU.mult, op1=ALU.add))
                link(stt(out=red[:, :, :, :], in0=turns[:, :, :, :], scalar=-TWO_PI_2, in1=red[:, :, :, :],
                         op0=ALU.mult, op1=ALU.add))
                link(stt(out=red[:, :, :, :], in0=turns[:, :, :, :], scalar=-TWO_PI_3, in1=red[:, :, :, :],
                         op0=ALU.mult, op1=ALU.add))
                link(ts(red[:, :, 0, :], red[:, :, 0, :], math.pi / 2, None, ALU.add))
                ts(red[:, :, :, :], red[:, :, :, :], PI, -PI, ALU.min, ALU.max).then_inc(one["ang"], 1)

            def rotary_tables():
                dve.wait_ge(one["sin"], 2)
                for dst, a, n in ((trig_m, 0, HB), (trig_d, HB, HD)):
                    cos, sin = trig_raw[:, :, 0, a:a + n], trig_raw[:, :, 1, a:a + n]
                    cp(dst[:, 0], cos.unsqueeze(2).broadcast_to([P, TT, 2, n])).then_inc(one["trig"], 1)
                    ts(dst[:, 1, :, 0, :], sin, -1.0, None, ALU.mult).then_inc(one["trig"], 1)
                    cp(dst[:, 1, :, 1, :], sin).then_inc(one["trig"], 1)

            def gains():
                dve.wait_ge(loaded["small"], 16 * N_SMALL)
                for l in range(DEPTH):
                    init = 0.8 - 0.6 * math.exp(-0.3 * l)
                    ts(g_in[64:P, l, 1, :], g_in[64:P, l, 1, :], 1.0 - init, None, ALU.mult)
                    tt(g_k[0:NOPE, l:l + 1], g_nope[0:NOPE, l, 0:1], g_nope[0:NOPE, l, 1:2], ALU.mult)
                    for j in range(2):
                        link(tt(lamp[:, j, :], lamv[:, l, 2 * j, :], lamv[:, l, 2 * j + 1, :], ALU.mult))
                        red_(lams[:, l, j:j + 1], lamp[:, j, :], AX.X, ALU.add).then_inc(one["lamp"], 1)
                dve.wait_ge(one["lame"], 1)
                for l in range(DEPTH):
                    init = 0.8 - 0.6 * math.exp(-0.3 * l)
                    link(tt(neglam[:, l:l + 1], lame[:, l, 1:2], lame[:, l, 0:1], ALU.subtract))
                    link(ts(neglam[:, l:l + 1], neglam[:, l:l + 1], -init, None, ALU.add))

            def norm(l, k):
                dve.wait_ge(*s_sq_at(l, k))
                ts(mstat[:, :], ssh[:, :], 1.0 / D, EPS, ALU.mult, ALU.add).then_inc(s_ms.sem, 1)
                dve.wait_ge(*s_rs.at(l, k + 1))
                ts(hn[:, 1, :], h[:, 1, :], rstd[:, 1:2], None, ALU.mult).then_inc(s_hn1.sem, 1)

            def evac_pass(l, n_):
                for b in (0, 1):
                    dve.wait_ge(*s_tr.at(l, 4 * n_ + b + 1))
                    g = g_in[:, l, n_, 2 * b:2 * b + 2].unsqueeze(2).broadcast_to([P, 2, SEQ])
                    tt(aT[:, 2 * b:2 * b + 2, :], bank(b).rearrange("p (k t) -> p k t", k=2), g,
                       ALU.mult).then_inc(s_aTv.sem, 1)

            def head_ms(w, n):
                ts(ssq[:, w], ssq[:, w], 1.0 / n, EPS, ALU.mult, ALU.add).then_inc(s_hms.sem, 1)

            def rotate(dst, src, tab, scratch, half):
                c, s = tab
                link(tt(dst, src, c, ALU.mult))
                tt(scratch[:, :, :, 0:half], src[:, :, :, half:2 * half], s[:, :, :, 0:half], ALU.mult)
                link(tt(scratch[:, :, :, half:2 * half], src[:, :, :, 0:half], s[:, :, :, half:2 * half], ALU.mult))
                return tt(dst, dst, scratch, ALU.add)

            def table(t, n, heads, token=None):
                v = t if token is None else t[:, token:token + 1].broadcast_to([P, 2, n])
                return v.unsqueeze(2).broadcast_to([P, 2, heads, n])

            rotary_angles()
            for l in range(DEPTH):
                norm(l, 0)
                if l == 0:
                    rotary_tables()
                    gains()
                    dve.sem_inc(one["gains"], 1)
                evac_pass(l, 0)
                dve.wait_ge(*s_lsq.at(l))
                ts(lms[:, 0:TT], lss[:, 0:TT], 1.0 / QR, EPS, ALU.mult, ALU.add)
                ts(lms[:, TT:2 * TT], lss[:, TT:2 * TT], 1.0 / KVR, EPS, ALU.mult, ALU.add).then_inc(s_lms.sem, 1)
                link(cp(kr, bank(4, 2)[:, :, QR + KVR:QR + KVR + ROPE]))
                link(tt(krs[:, :, :], kr, kr, ALU.mult))
                red_(sskr[:, :], krs[:, :, :], AX.X, ALU.add).then_inc(s_kr.sem, 1)
                dve.wait_ge(*s_lrs.at(l))
                for t in range(TT):
                    ts(lat[:, t, 0:QR], PS[:, 4 + t, 0:QR], lrs[:, t:t + 1], None, ALU.mult)
                    ins = ts(lat[:, t, QR:QR + KVR], PS[:, 4 + t, QR:QR + KVR], lrs[:, TT + t:TT + t + 1], None, ALU.mult)
                ins.then_inc(s_lat.sem, 1)
                dve.wait_ge(*s_junk.at(l, 1))
                red_(ssq[:, 0].rearrange("p t h -> p (t h)"), junk.rearrange("p (h n) -> p h n", n=DHD), AX.X,
                     ALU.add).then_inc(s_sum.sem, 1)
                dve.wait_ge(*s_sum.at(l, 1))
                head_ms(0, DHD)
                dve.wait_ge(*s_tab.at(l))
                src = bank(6, 2).rearrange("p t (h n) -> p t h n", h=8)
                scratch = rtmp.rearrange("p (t h n) -> p t h n", t=TT, h=8)
                rotate(dqr.rearrange("p t (h n) -> p t h n", h=8), src,
                       [table(rope_d[:, 0, cs], DHD, 8) for cs in range(2)], scratch, HD).then_inc(s_dq.sem, 1)
                dve.wait_ge(*s_lT.at(l))
                tt(cqT, bank(4).rearrange("p (k t) -> p k t", k=2), g_cq[:, l, :].unsqueeze(2).broadcast_to([P, 2, SEQ]),
                   ALU.mult)
                ts(ckvT, PS[:, 5, 0:SEQ], g_ckv[:, l, 0:1], None, ALU.mult).then_inc(s_lTc.sem, 1)
                dve.wait_ge(*s_junk.at(l, 2))
                red_(ssq[:, 1].rearrange("p t h -> p (t h)"), junk.rearrange("p (h n) -> p h n", n=DHD), AX.X,
                     ALU.add).then_inc(s_sum.sem, 1)
                dve.wait_ge(*s_sum.at(l, 2))
                head_ms(1, DHD)
                dk4 = dkr.rearrange("p t (h n) -> p t h n", h=8)
                dve.wait_ge(*s_dq.at(l))
                link(rotate(dk4, bank(0, 2).rearrange("p t (h n) -> p t h n", h=8),
                            [table(rope_d[:, 1, cs], DHD, 8) for cs in range(2)], scratch, HD))
                dve.wait_ge(*s_hrs.at(l, 2))
                tt(dk4, dk4, rsq[:, 1].unsqueeze(3).broadcast_to([P, TT, 8, DHD]), ALU.mult).then_inc(s_dk.sem, 1)
                for sign in range(2):
                    ts(qsc[:, 0, sign], rsq[:, 0], (1 - 2 * sign) * DHD ** -0.5, None, ALU.mult)
                dve.wait_ge(*s_dk.at(l))
                for t, b in enumerate((6, 0)):
                    dve.wait_ge(*s_junk.at(l, 3 + t))
                    red_(ssq[:, 2, t], junk[:, 0:MH * MQK].rearrange("p (h n) -> p h n", n=MQK), AX.X,
                         ALU.add).then_inc(s_sum.sem, 1)
                    dve.wait_ge(*s_qn.at(l, t + 1))
                    src = bank(b, 2)[:, :, 0:4 * MQK].rearrange("p b (h n) -> p b h n", h=4)[:, :, :, NOPE:MQK]
                    dst = qm[:, t, :].rearrange("p (b h n) -> p b h n", b=2, h=4)[:, :, :, NOPE:MQK]
                    scr = rtmp[:, 256 * t:256 * t + 256].rearrange("p (b h n) -> p b h n", b=2, h=4)
                    rotate(dst, src, [table(rope_m[:, 0, cs], ROPE, 4, t) for cs in range(2)], scr,
                           HB).then_inc(s_qr.sem, 1)
                dve.wait_ge(*s_sum.at(l, 4))
                head_ms(2, MQK)
                dve.wait_ge(*s_junk.at(l, 5))
                red_(ssq[:, 3].rearrange("p t h -> p (t h)"), junk.rearrange("p (h n) -> p h n", n=NOPE), AX.X,
                     ALU.add).then_inc(s_sum.sem, 1)
                dve.wait_ge(*s_sum.at(l, 5))
                link(tt(ssq[:, 3], ssq[:, 3], sskr[:, :].unsqueeze(2).broadcast_to([P, TT, 8]), ALU.add))
                head_ms(3, MQK)
                dve.wait_ge(*s_hrs.at(l, 4))
                dve.wait_ge(*s_vm.at(l))
                for t, b in enumerate((2, 4)):
                    src = bank(b, 2).rearrange("p b (h n) -> p b h n", h=4)[:, :, :, 0:NOPE]
                    dst = km[:, t, :].rearrange("p (b h n) -> p b h n", b=2, h=4)[:, :, :, 0:NOPE]
                    r = rsq[:, 3, t, :].rearrange("p (b h) -> p b h", b=2).unsqueeze(3).broadcast_to([P, 2, 4, NOPE])
                    tt(dst, src, r, ALU.mult).then_inc(s_kn.sem, 1)
                for sign in range(2):
                    ins = ts(qsc[:, 1, sign], rsq[:, 2], (1 - 2 * sign) * MQK ** -0.5, None, ALU.mult)
                link(ins)
                for j in range(6):
                    idx = 2 * j
                    dve.wait_ge(*s_hT.at(l, idx + 1))
                    rows, dst, gain = hT_dest(l, idx)
                    src = PS[0:rows, HT_BANK[idx], :].rearrange("p (h t) -> p h t", h=2)
                    if gain is None:
                        cp(dst, src).then_inc(s_hTv.sem, 1)
                    else:
                        ts(dst, src, gain, None, ALU.mult).then_inc(s_hTv.sem, 1)

                def maximum(m):
                    kind, hd = (0, m) if m < MAPS else (1, m - MAPS)
                    dve.wait_ge(*s_S.at(l, m + 1))
                    b = S_BANK[m % 4]
                    red_(mx[:, m, 0:1], PS[:, b, 0:P], AX.X, ALU.max)
                    link(red_(mx[:, m, 1:2], PS[:, b, P:3 * P], AX.X, ALU.max))
                    tt(nbias[:, m, :], mx[:, m, :], qsc[:, kind, 1, :, hd], ALU.mult).then_inc(s_nb.sem, 1)

                def output(m):
                    dve.wait_ge(*s_O.at(l, m + 1))
                    link(nc.vector.reciprocal(rinv[:, m, :], sums[:, m, :]))
                    b = O_BANK[m % 2]
                    if m < MAPS:
                        src = bank(b).rearrange("p (t n) -> p t n", t=TT)[:, :, 0:DV]
                        dst = ocat[:, :, 512 + DV * (m // 2):512 + DV * (m // 2 + 1)]
                        w = rinv[:, m, :].unsqueeze(2).broadcast_to([P, TT, DV])
                        if m % 2 == 0:
                            tt(dst, src, w, ALU.mult).then_inc(s_Oe.sem, 1)
                        else:
                            link(ts(rinv[:, m, :], rinv[:, m, :], neglam[:, l:l + 1], None, ALU.mult))
                            tmp = rtmp[:, 0:TT * DV].rearrange("p (t n) -> p t n", t=TT)
                            tt(tmp, src, w, ALU.mult).then_inc(s_Oe.sem, 1)
                            dve.wait_ge(*s_Oe.at(l, m + 1))
                            ins = tt(dst, dst, tmp, ALU.add)
                            if m == MAPS - 1:
                                ins.then_inc(s_od.sem, 1)
                            else:
                                link(ins)
                    else:
                        hd = m - MAPS
                        src = bank(b).rearrange("p (t n) -> p t n", t=TT)[:, :, 0:MV]
                        tt(ocat[:, :, MV * hd:MV * (hd + 1)], src, rinv[:, m, :].unsqueeze(2).broadcast_to([P, TT, MV]),
                           ALU.mult).then_inc(s_Oe.sem, 1)

                def sub_norm():
                    dve.wait_ge(*s_junk.at(l, 6))
                    red_(ods[:, :], junk.rearrange("p (h n) -> p h n", n=DV), AX.X, ALU.add).then_inc(s_sum.sem, 1)
                    dve.wait_ge(*s_sum.at(l, 6))
                    ts(ods[:, :], ods[:, :], 1.0 / DV, EPS, ALU.mult, ALU.add).then_inc(s_hms.sem, 1)

                def sub_scale():
                    dve.wait_ge(*s_hrs.at(l, 5))
                    o4 = ocat[:, :, 512:1024].rearrange("p t (h n) -> p t h n", h=DH)
                    r = odr[:, :].rearrange("p (t h) -> p t h", t=TT).unsqueeze(3).broadcast_to([P, TT, DH, DV])
                    return tt(o4, o4, r, ALU.mult)

                for i in range(16 + 2):
                    if i < 16:
                        maximum(i)
                    if 1 <= i <= 16 and (i - 1) % 2 == 0:
                        j = i - 1
                        dve.wait_ge(*s_T.at(l, j + 1))
                        if j >= 2:
                            dve.wait_ge(*s_O.at(l, j - 1))
                        cp(prT[:, 0, :], PS[:, 3, 0:384]).then_inc(s_Tv.sem, 1)
                    if i >= 2:
                        output(i - 2)
                    if i == MAPS + 5:
                        sub_norm()
                sub_scale().then_inc(s_oc.sem, 1)
                evac_pass(l, 1)
                for c in range(2):
                    for t in range(TT):
                        j = 2 * c + t
                        dve.wait_ge(*s_out.at(l, j + 1))
                        v = h[:, t, c * CB:(c + 1) * CB]
                        ins = tt(v, v, bank(4 + j), ALU.add)
                ins.then_inc(s_h.sem, 1)
                norm(l, 1)
                evac_pass(l, 2)

                R = {k: v[:, :, :] for k, v in rt.items()}
                g4 = cst[:, C_G4:C_G4 + NG].unsqueeze(1).broadcast_to([P, TT, NG])
                e32 = cst[:, C_E32:C_E32 + NE].unsqueeze(1).broadcast_to([P, TT, NE])

                def wide(v, n):
                    return v.broadcast_to([P, TT, n])

                dve.wait_ge(*s_rl.at(l))
                link(tt(R["lg"], PS[:, 4, 0:TT * (NG + NE)].rearrange("p (t n) -> p t n", t=TT),
                        bias[:, l, :].unsqueeze(1).broadcast_to([P, TT, NG + NE]), ALU.add))
                lgg, lge = rt["lg"][:, :, 0:NG], rt["lg"][:, :, NG:NG + NE]
                link(red_(R["gmax"], lgg, AX.X, ALU.max))
                tt(R["gd"], lgg, wide(R["gmax"], NG), ALU.subtract).then_inc(s_ra.sem, 1)
                link(tt(R["geq"], lgg, wide(R["gmax"], NG), ALU.is_equal))
                link(stt(out=R["gc"], in0=R["geq"], scalar=-1000.0, in1=g4, op0=ALU.mult, op1=ALU.add))
                link(red_(R["gi"], R["gc"], AX.X, ALU.min))
                link(tt(R["goh"], R["gc"], wide(R["gi"], NG), ALU.is_equal))
                link(ts(R["pen"], R["goh"], 1e30, -1e30, ALU.mult, ALU.add))
                ml4 = R["ml"].rearrange("p t (g e) -> p t g e", g=NG)
                link(tt(ml4, lge.rearrange("p t (g e) -> p t g e", g=NG),
                        rt["pen"][:, :, :].unsqueeze(3).broadcast_to([P, TT, NG, NEG]), ALU.add))

                def top(src, m, eq, c, i, oh):
                    link(red_(R[m], src, AX.X, ALU.max))
                    link(tt(R[eq], src, wide(R[m], NE), ALU.is_equal))
                    link(stt(out=R[c], in0=R[eq], scalar=-1000.0, in1=e32, op0=ALU.mult, op1=ALU.add))
                    link(red_(R[i], R[c], AX.X, ALU.min))
                    link(tt(R[oh], R[c], wide(R[i], NE), ALU.is_equal))

                top(R["ml"], "m1", "eq", "c1", "i1", "oh1")
                link(stt(out=R["ml2"], in0=R["oh1"], scalar=-2e30, in1=R["ml"], op0=ALU.mult, op1=ALU.add))
                top(R["ml2"], "m2", "eq", "c2", "i2", "oh2")
                tt(R["dm"], R["m2"], R["m1"], ALU.subtract).then_inc(s_ra.sem, 1)
                for i, a in (("i1", "t1"), ("i2", "t2")):
                    link(ts(R[i], R[i], 1000.0, None, ALU.add))
                    link(tt(R[a], e32, wide(R[i], NE), ALU.is_gt))
                link(tt(R["Mpre"], R["t1"], R["t2"], ALU.add))
                tt(Mp[:, :], rt["Mpre"][:, 0, :], rt["Mpre"][:, 1, :], ALU.add)
                tt(R["M"], R["oh1"], R["oh2"], ALU.add).then_inc(s_M.sem, 1)
                dve.wait_ge(*s_re.at(l, 2))
                link(red_(R["gs"], R["ge"], AX.X, ALU.add))
                link(ts(R["den"], R["e2"], 1.0, None, ALU.add))
                link(tt(R["den"], R["den"], R["gs"], ALU.mult))
                link(nc.vector.reciprocal(R["w1"], R["den"]))
                link(tt(R["w2"], R["w1"], R["e2"], ALU.mult))
                dve.wait_ge(*s_pos.at(l))
                pos = PS[:, 5, 0:TT * NE].rearrange("p (t n) -> p t n", t=TT)
                for oh, t_, s in (("oh1", "t1", "s1"), ("oh2", "t2", "s2")):
                    link(tt(R[t_], R[oh], pos, ALU.mult))
                    link(red_(R[s], R[t_], AX.X, ALU.add))
                for t in range(TT):
                    link(ts(pdis[:, t, :], iota_slot, rt["s1"][:, t, :], None, ALU.is_equal))
                    ins = stt(out=pdis[:, t, :], in0=iota_slot, scalar=rt["s2"][:, t, :], in1=pdis[:, t, :],
                              op0=ALU.is_equal, op1=ALU.add)
                ins.then_inc(s_P.sem, 1)
                off, cnts = PS[:, 5, 2 * NE:3 * NE], PS[:, 5, 3 * NE:4 * NE]
                link(ts(cnt[:, 0, :], cnts, BLK + 0.5, 1.0, ALU.is_gt, ALU.add))
                link(stt(out=cnt[:, 1, :], in0=cnts, scalar=2 * BLK + 0.5, in1=cnt[:, 0, :], op0=ALU.is_gt, op1=ALU.add))
                link(stt(out=cnt[:, 2, :], in0=cnts, scalar=3 * BLK + 0.5, in1=cnt[:, 1, :], op0=ALU.is_gt, op1=ALU.add))
                per = cnt[:, 2, :]
                link(nc.vector.memset(pfx[:, :, :], 0.0))
                link(cp(pfx[:, 1, :], per))
                flat = pfx[:, :, :].rearrange("p a n -> p (a n)")
                at = NE
                for j in range(5):
                    to = NE + 2 * NE * ((j + 1) % 2)
                    link(tt(flat[:, to:to + NE], flat[:, at:at + NE], flat[:, at - 2 ** j:at + NE - 2 ** j], ALU.add))
                    at = to
                run = flat[:, at:at + NE]
                jcol = cst[:, C_J:C_J + 1]
                link(ts(boh[:, 0, :], run, jcol, None, ALU.is_le))
                link(red_(blk4[:, 3:4], boh[:, 0, :], AX.X, ALU.add))
                link(ts(boh[:, 1, :], cst[:, C_E32:C_E32 + NE], blk4[:, 3:4], None, ALU.is_equal))
                link(tt(boh[:, 2, :], run, per, ALU.subtract))
                link(stt(out=boh[:, 2, :], in0=boh[:, 2, :], scalar=-float(BLK), in1=off, op0=ALU.mult, op1=ALU.add))
                link(tt(boh[:, 2, :], boh[:, 2, :], boh[:, 1, :], ALU.mult))
                link(red_(blk4[:, 0:1], boh[:, 2, :], AX.X, ALU.add))
                link(stt(out=blk4[:, 0:1], in0=jcol, scalar=float(BLK), in1=blk4[:, 0:1], op0=ALU.mult, op1=ALU.add))
                link(tt(boh[:, 3, :], boh[:, 1, :], cst[:, C_MOD:C_MOD + NE], ALU.mult))
                link(red_(blk4[:, 1:2], boh[:, 3, :], AX.X, ALU.add))
                ts(blk4[:, 2:3], blk4[:, 3:4], 1.0, None, ALU.add).then_inc(s_blk.sem, 1)
                link(ts(ctlef[:, 0:NE], run[0:1], carry[:, 0:1], None, ALU.add))
                cp(ctlef[:, NE:NE + 1], run[0:1, NE - 1:NE])
                link(cp(ctlef[:, NE + 1:NE + 2], carry[:, :]))
                link(ts(carry[:, :], run[0:1, NE - 1:NE], carry[:, 0:1], None, ALU.add))
                cp(ctle[:, :], ctlef[:, :])
                nc.vector.memset(ctl[:, 0:1], 0)
                for k in range(0, KD, 2):
                    dve.wait_ge(*s_disp.at(l, k + 1))
                    ts(mTs[:, k, 0:NSLOT], PS[:, DISP_BANK[k], :], g_in[:, l, 2, k:k + 1], None,
                       ALU.mult).then_inc(s_dv.sem, 1)
                dve.wait_ge(*s_blkT.at(l))
                cp(ctl[:, 1:1 + P], PS[0:4, 5, 4 * NE:4 * NE + P]).then_inc(s_ctl.sem, 1)
                for t in range(TT):
                    ts(GT[:, t, :], iota_slot, rt["s1"][:, t, :], rt["w1"][:, t, :], ALU.is_equal, ALU.mult)
                    link(ts(gtmp[:, t, :], iota_slot, rt["s2"][:, t, :], rt["w2"][:, t, :], ALU.is_equal, ALU.mult))
                tt(GT, GT, gtmp, ALU.add).then_inc(s_GT.sem, 1)
                dve.wait_ge(*s_GTt.at(l))
                cp(G.rearrange("p s t -> p (s t)"), bank(0, 2).rearrange("p b n -> p (b n)")).then_inc(s_Gc.sem, 1)
                dve.wait_ge(*s_ctl.at(l))
                dve.wait_ge(*s_da.at(l))
                blocks, before = block_counts(dve)

                def copy_y(at):
                    dve.wait_ge(s_C, at + 1)
                    dve.wait_ge(s_D, at + (l + 1))
                    cp(yraw, bank(6, 2).rearrange("p b n -> p (b n)")).then_inc(s_ye, 1)

                def place_y(at, j):
                    col = block_column(dve, j)
                    dve.wait_ge(s_D, at + (l + 2))
                    cp(yTs[:, :, ds(col, BLK)],
                       bank(0, 2).rearrange("p b (k s) -> p (b k) s", s=2 * BLK)[:, :, 0:BLK]).then_inc(s_yc, 1)

                def low_part(at, region, c):
                    dve.wait_ge(s_hi, at * CHUNKS + (c + 1))
                    tt(part_chunk(w_lo, c), raw_chunk(region, c), part_chunk(w_hi, c).bitcast(F32),
                       ALU.subtract).then_inc(s_lod, 1)

                with dve.Fori(0, blocks) as j:
                    at = before + j
                    first = block_column(dve, j + 1)
                    region = dve.value_load(ctl[1:2, ds(j + 1, 1)], min_val=0, max_val=REGIONS - 1)
                    dve.wait_ge(s_xh, at + 1)
                    tt(x_hl[:, :, BLK:2 * BLK], mTs[:, :, ds(first, BLK)], x_hl[:, :, 0:BLK].bitcast(F32),
                       ALU.subtract).then_inc(s_xl, 1)
                    for c in DVE_CHUNKS[0:2]:
                        low_part(at, region, c)
                    copy_y(at)
                    for c in DVE_CHUNKS[2:]:
                        low_part(at, region, c)
                    dve.wait_ge(s_silu, at + 1)
                    tt(hb, sg, PS[:, 5, :].rearrange("p (q s) -> p q s", q=4)[:, KF:2 * KF, 0:BLK],
                       ALU.mult).then_inc(s_hs, 1)
                    dve.wait_ge(s_hs, at * 2 + 1)
                    cp(h_hl[:, :, 0:BLK], hb).then_inc(s_hs, 1)
                    dve.wait_ge(s_hs, at * 2 + 2)
                    tt(h_hl[:, :, BLK:2 * BLK], hb, h_hl[:, :, 0:BLK].bitcast(F32), ALU.subtract).then_inc(s_hl, 1)
                    place_y(at, j)
                copy_y(before + blocks)
                place_y(before + blocks, blocks)
                dve.wait_ge(*s_pTt.at(l))
                cp(pT.rearrange("p k t -> p (k t)"), PS[:, 5, :]).then_inc(s_pTc.sem, 1)
                for j in range(4):
                    dve.wait_ge(*s_yT.at(l, 2 * j + 1))
                    cp(ys[:, j, 0:CB], PS[:, YT_BANK[2 * j], :]).then_inc(s_yv.sem, 1)
                for c in range(2):
                    for t in range(TT):
                        j = 2 * c + t
                        dve.wait_ge(*s_cmb.at(l, j + 1))
                        v = h[:, t, c * CB:(c + 1) * CB]
                        ins = tt(v, v, bank(4 + j), ALU.add)
                ins.then_inc(s_h.sem, 1)
                norm(l, 2)
                evac_pass(l, 3)
                for t in range(TT):
                    for c in range(2):
                        j = 2 * t + c
                        dve.wait_ge(*s_sg.at(l, j + 1))
                        link(tt(prod[:, j, :], sig[:, j, :], bank(4 + j), ALU.mult))
                        v = h[:, t, c * CB:(c + 1) * CB]
                        tt(v, v, prod[:, j, :], ALU.add).then_inc(s_fin.sem, 1)
                dve.wait_ge(*s_fin.at(l))
                dve.sem_inc(s_h.sem, 1)

        @block.tensor
        def _(pe):
            mm = nc.tensor.matmul

            def used():
                pe.drain().then_inc(weights_used, 1)

            def tr(dst, src, rows=P):
                return pe.transpose(dst, src, ident[0:rows, 0:rows] if rows < P else ident)

            def transposed_pass(l, n_, src):
                for t in range(TT):
                    for k in range(KD):
                        b = k // 2
                        c = (k % 2) * SEQ + t * P
                        ins = tr(PS[:, b, c:c + P], src[:, t, k::KD])
                        if t == TT - 1 and k % 2 == 1:
                            ins.then_inc(s_tr.sem, 1)

            def aT_ready(l, n_):
                pe.wait_ge(*s_aTv.at(l, 2 * n_ + 2))
                pe.wait_ge(*s_aTs.at(l, 2 * n_ + 2))

            pe.wait_ge(loaded["const"], 16)
            for l in range(DEPTH):
                pe.wait_ge(*s_hn0.at(l, 1))
                pe.wait_ge(*s_hn1.at(l, 1))
                transposed_pass(l, 0, hn)
                aT_ready(l, 0)
                for c, b in enumerate((4, 6, 0, 2)):
                    item = ITEM[l, f"z{c}"]
                    n = SPLITS[c][1] - SPLITS[c][0]
                    w = slots(item, KD, n)
                    arrival(pe, item)
                    for t in range(TT):
                        for k in range(KD):
                            ins = mm(PS[:, b + t, 0:n], aT[:, k, t * P:(t + 1) * P], w[:, k, :], start=(k == 0),
                                     stop=(k == KD - 1))
                    ins.then_inc(s_z.sem, 1)
                    used()
                    if c == 2:
                        pe.wait_ge(*s_lat.at(l))
                        pe.wait_ge(*s_kr.at(l))
                        for t in range(TT):
                            for k in range(2):
                                tr(PS[:, 4, k * SEQ + t * P:k * SEQ + (t + 1) * P], lat[:, t, k:QR:2])
                            ins = tr(PS[:, 5, t * P:(t + 1) * P], lat[:, t, QR:QR + KVR])
                        ins.then_inc(s_lT.sem, 1)
                item = ITEM[l, "uq"]
                w = slots(item, 2, MH * MQK)
                arrival(pe, item)
                pe.wait_ge(*s_lTc.at(l))
                for t, b in enumerate((6, 0)):
                    pe.wait_ge(*(s_dq if t == 0 else s_dk).at(l))
                    for half in range(2):
                        for k in range(2):
                            ins = mm(PS[:, b + half, 0:4 * MQK], cqT[:, k, t * P:(t + 1) * P],
                                     w[:, k, half * 4 * MQK:(half + 1) * 4 * MQK], start=(k == 0), stop=(k == 1))
                    ins.then_inc(s_uq.sem, 1)
                used()
                item = ITEM[l, "ukv"]
                w = slots(item, 2, CB)
                arrival(pe, item)
                for t, b in enumerate((2, 4)):
                    if t == 0:
                        pe.wait_ge(*s_vd.at(l))
                    for half in range(2):
                        ins = mm(PS[:, b + half, :], ckvT[:, t * P:(t + 1) * P], w[:, half, :], start=True, stop=True)
                    ins.then_inc(s_ukv.sem, 1)
                used()
                for idx in range(12):
                    b = HT_BANK[idx]
                    if idx == 0:
                        pe.wait_ge(*s_qr.at(l, 1))
                        pe.wait_ge(*s_qn.at(l, 1))
                    if idx == 2:
                        pe.wait_ge(*s_qr.at(l, 2))
                        pe.wait_ge(*s_qn.at(l, 2))
                    if idx == 4:
                        pe.wait_ge(*s_kn.at(l, 2))
                        pe.wait_ge(*s_vm.at(l, 2))
                    if idx == 8:
                        pe.wait_ge(*s_kpe.at(l, 2))
                        pe.wait_ge(*s_hTv.at(l, 2))
                        pe.wait_ge(*s_hTs.at(l, 2))
                    for j in range(2):
                        for t in range(TT):
                            c = j * SEQ + t * P
                            if idx < 4:
                                hd = 2 * (idx % 2) + j
                                src = (dqr if idx < 2 else dkr)[:, t, hd * P:(hd + 1) * P]
                                ins = tr(PS[:, b, c:c + P], src)
                            else:
                                hd = 2 * ((idx - 4) % 4) + j
                                src = (qm if idx < 8 else km)[:, t, hd * MQK:(hd + 1) * MQK]
                                ins = tr(PS[0:MQK, b, c:c + P], src)
                    ins.then_inc(s_hT.sem, 1)
                pe.wait_ge(*s_hTv.at(l))
                pe.wait_ge(*s_hTs.at(l))

                def scores(m):
                    if m >= 4:
                        pe.wait_ge(*s_exp.at(l, m - 3))
                    b = S_BANK[m % 4]
                    if m < MAPS:
                        r = slice((m % 2) * DHD, (m % 2 + 1) * DHD)
                        q, k = qTd[r, m // 2, :], kTd[r, m // 2, :]
                        rows = r
                    else:
                        rows = slice(0, MQK)
                        q, k = qTm[rows, m - MAPS, :], kTm[rows, m - MAPS, :]
                    mu, mv = cst[rows, C_MU:C_MU + P], cst[rows, C_MV:C_MV + CHUNK]
                    for t in range(TT):
                        a = t * P
                        n = (t + 1) * P
                        mm(PS[:, b, a:a + n], q[:, t * P:(t + 1) * P], k[:, 0:n], start=True, stop=False)
                        ins = mm(PS[:, b, a + n - CHUNK:a + n], mu, mv, start=False, stop=True)
                    ins.then_inc(s_S.sem, 1)

                def turn(m):
                    pe.wait_ge(*s_exp.at(l, m + 1))
                    if m >= 2:
                        pe.wait_ge(*(s_Tv if m % 2 == 0 else s_Ts).at(l, m // 2))
                    for j in range(3):
                        ins = tr(PS[:, T_BANK[m % 2], j * P:(j + 1) * P], prb[:, m % 2, j * P:(j + 1) * P])
                    ins.then_inc(s_T.sem, 1)

                def values(m):
                    pe.wait_ge(*(s_Tv if m % 2 == 0 else s_Ts).at(l, m // 2 + 1))
                    if m >= 2:
                        pe.wait_ge(*s_Oe.at(l, m - 1))
                    b = O_BANK[m % 2]
                    if m < MAPS:
                        n = DV
                        v = [vd[:, t, (m // 2) * DV:(m // 2 + 1) * DV] for t in range(TT)]
                    else:
                        n = MV
                        v = [vm[:, t, (m - MAPS) * MV:(m - MAPS + 1) * MV] for t in range(TT)]
                    w = prT[:, m % 2, :]
                    mm(PS[:, b, 0:n], w[:, 0:P], v[0], start=True, stop=True)
                    mm(PS[:, b, SEQ:SEQ + n], w[:, P:2 * P], v[0], start=True, stop=False)
                    mm(PS[:, b, SEQ:SEQ + n], w[:, 2 * P:3 * P], v[1], start=False, stop=True).then_inc(s_O.sem, 1)

                for i in range(16 + 2):
                    if i < 16:
                        scores(i)
                    if 1 <= i <= 16:
                        turn(i - 1)
                    if i >= 2:
                        values(i - 2)
                pe.wait_ge(*s_oc.at(l))
                transposed_pass(l, 1, ocat)
                aT_ready(l, 1)
                for c in range(2):
                    item = ITEM[l, f"out{c}"]
                    w = slots(item, KD, CB)
                    arrival(pe, item)
                    for t in range(TT):
                        for k in range(KD):
                            ins = mm(bank(4 + 2 * c + t), aT[:, k, t * P:(t + 1) * P], w[:, k, :], start=(k == 0),
                                     stop=(k == KD - 1))
                        ins.then_inc(s_out.sem, 1)
                    used()
                pe.wait_ge(*s_hn0.at(l, 2))
                pe.wait_ge(*s_hn1.at(l, 2))
                transposed_pass(l, 2, hn)
                aT_ready(l, 2)
                for t in range(TT):
                    for k in range(KD):
                        ins = mm(PS[:, 4, t * (NG + NE):(t + 1) * (NG + NE)], aT[:, k, t * P:(t + 1) * P], w_rt[:, l, k, :],
                                 start=(k == 0), stop=(k == KD - 1))
                ins.then_inc(s_rl.sem, 1)
                pe.wait_ge(*s_M.at(l))
                M0, M1 = rt["M"][:, 0, :], rt["M"][:, 1, :]
                mm(PS[:, 5, 0:NE], ones, Mp[:, :], start=True, stop=False)
                mm(PS[:, 5, 0:NE], tri, M0, start=False, stop=True)
                mm(PS[:, 5, NE:2 * NE], ones, Mp[:, :], start=True, stop=False)
                mm(PS[:, 5, NE:2 * NE], ones, M0, start=False, stop=False)
                mm(PS[:, 5, NE:2 * NE], tri, M1, start=False, stop=True)
                mm(PS[:, 5, 2 * NE:3 * NE], ones, Mp[:, :], start=True, stop=True)
                mm(PS[:, 5, 3 * NE:4 * NE], ones, M0, start=True, stop=False)
                mm(PS[:, 5, 3 * NE:4 * NE], ones, M1, start=False, stop=True).then_inc(s_pos.sem, 1)
                pe.wait_ge(*s_P.at(l))
                for k in range(KD):
                    if k >= 6:
                        pe.wait_ge(*(s_dv if k == 6 else s_da).at(l, 1))
                    for t in range(TT):
                        ins = mm(bank(DISP_BANK[k]), hn[:, t, k::KD], pdis[:, t, :], start=(t == 0), stop=(t == TT - 1))
                    ins.then_inc(s_disp.sem, 1)
                pe.wait_ge(*s_blk.at(l))
                tr(PS[0:4, 5, 4 * NE:4 * NE + P], blk4[:, :]).then_inc(s_blkT.sem, 1)
                pe.wait_ge(*s_GT.at(l))
                pe.wait_ge(*s_dv.at(l))
                pe.wait_ge(*s_da.at(l))
                for s in range(4):
                    for t in range(TT):
                        c = (s % 2) * SEQ + t * P
                        ins = tr(PS[:, s // 2, c:c + P], GT[:, t, s * P:(s + 1) * P])
                ins.then_inc(s_GTt.sem, 1)
                pe.wait_ge(*s_ctl.at(l))
                pe.wait_ge(*s_Gc.at(l))
                blocks, before = block_counts(pe)

                def chunk(at, c):
                    if c in POOL_CHUNKS:
                        pe.wait_ge(s_lop, at * len(POOL_CHUNKS) + (POOL_CHUNKS.index(c) + 1))
                    else:
                        pe.wait_ge(s_lod, at * len(DVE_CHUNKS) + (DVE_CHUNKS.index(c) + 1))
                    for n in range(2):
                        for half, w in enumerate((w_hi, w_lo)):
                            if c < 4:
                                v = w[:, c % NBUF, :].rearrange("p (s k f) -> p s k f", s=2, k=2)[:, :, n, :]
                                ins = mm(PS[:, 4, :], x_hl[:, 2 * c + n, :], v, start=(c == 0 and n == 0 and half == 0),
                                         stop=(c == 3 and n == 1 and half == 1))
                            else:
                                v = w[:, c % NBUF, n * CB:(n + 1) * CB]
                                ins = mm(PS[:, 6 + n, :], h_hl[:, c - 4, :], v, start=(c == 4 and half == 0),
                                         stop=(c == 5 and half == 1))
                    ins.then_inc(s_ch, 1)
                    return ins

                pair = cst[:, C_II:C_II + P]

                def turn_y(at):
                    pe.wait_ge(s_ye, at + (l + 1))
                    pe.wait_ge(s_yc, at + (l + 1))
                    for d in range(KD):
                        ins = mm(PS[:, d // 4, d % 4 * P:(d % 4 + 1) * P], yraw[:, d * P:(d + 1) * P], pair,
                                 start=True, stop=True)
                    ins.then_inc(s_D, 1)

                with pe.Fori(0, blocks) as j:
                    at = before + j
                    pe.wait_ge(s_xl, at + 1)
                    for c in range(4):
                        chunk(at, c)
                    pe.wait_ge(s_gue, at + 1)
                    for q in range(2 * KF):
                        ins = mm(PS[:, 5, q * P:(q + 1) * P], gur[:, q * P:(q + 1) * P], pair, start=True, stop=True)
                    ins.then_inc(s_B, 1)
                    turn_y(at)
                    pe.wait_ge(s_hl, at + 1)
                    for c in range(4, 6):
                        ins = chunk(at, c)
                    pe.drain().then_inc(s_C, 1)
                turn_y(before + blocks)
                pe.wait_ge(s_Gl.sem, 16 * (l + 1))
                for k in range(2):
                    for t in range(TT):
                        ins = tr(PS[:, 5, k * SEQ + t * P:k * SEQ + (t + 1) * P], pin[:, t, k::2])
                ins.then_inc(s_pTt.sem, 1)
                pe.wait_ge(s_yc, before + blocks + (l + 2))
                for j in range(8):
                    if j >= 6:
                        pe.wait_ge(*(s_yv if j == 6 else s_ya).at(l, 1))
                    s, half = j // 2, j % 2
                    for d in range(4):
                        ins = tr(PS[:, YT_BANK[j], d * P:(d + 1) * P], yTs[:, half * 4 + d, s * P:(s + 1) * P])
                    ins.then_inc(s_yT.sem, 1)
                pe.wait_ge(*s_yv.at(l))
                pe.wait_ge(*s_ya.at(l))
                pe.wait_ge(*s_pTc.at(l))
                for c in range(2):
                    for t in range(TT):
                        for s in range(4):
                            ins = mm(bank(4 + 2 * c + t), G[:, s, t * P:(t + 1) * P], ys[:, s, c * CB:(c + 1) * CB],
                                     start=(s == 0), stop=(s == 3))
                        ins.then_inc(s_cmb.sem, 1)
                pe.wait_ge(*s_hn0.at(l, 3))
                pe.wait_ge(*s_hn1.at(l, 3))
                transposed_pass(l, 3, hn)
                item = ITEM[l, "proj"]
                w = slots(item, 2, D)
                arrival(pe, item)
                for t in range(TT):
                    for c in range(2):
                        for k in range(2):
                            ins = mm(bank(4 + 2 * t + c), pT[:, k, t * P:(t + 1) * P], w[:, k, c * CB:(c + 1) * CB],
                                     start=(k == 0), stop=(k == 1))
                        ins.then_inc(s_pp.sem, 1)
                used()
                aT_ready(l, 3)
                for c in range(2):
                    arrival(pe, ITEM[l, f"gate{c}"])
                for t in range(TT):
                    for c in range(2):
                        w = slots(ITEM[l, f"gate{c}"], KD, CB)
                        for k in range(KD):
                            ins = mm(bank(2 * t + c), aT[:, k, t * P:(t + 1) * P], w[:, k, :], start=(k == 0),
                                     stop=(k == KD - 1))
                        ins.then_inc(s_gt.sem, 1)
                used()
                used()


_INS = ["x", "p", "positions", "attn_norm", "w_in", "q_a_norm", "w_uq", "kv_a_norm", "w_ukv", "mla_q_norm",
        "mla_k_norm", "diff_q_norm", "diff_k_norm", "lambda_q1", "lambda_k1", "lambda_q2", "lambda_k2", "diff_subln",
        "w_out", "ffn_norm", "w_group", "b_group", "w_router", "b_router", "w_gate", "w_up", "w_down", "ple_norm",
        "w_ple_gate", "w_ple_proj"]


def kernel(**inputs):
    import numpy as _np
    import concourse.bacc as _bacc
    from concourse import mybir as _mybir
    from concourse.bass_utils import run_bass_kernel_spmd as _run

    nc = _bacc.Bacc("TRN2", target_bir_lowering=False, num_devices=1)
    arrays, args = {}, []
    for name in _INS:
        a = _np.ascontiguousarray(inputs[name])
        arrays[f"in_{name}"] = a
        args.append(nc.dram_tensor(f"in_{name}", a.shape, _mybir.dt.from_np(a.dtype), kind="ExternalInput").ap())
    const = constants()
    arrays["in_const"] = const
    args.append(nc.dram_tensor("in_const", const.shape, _mybir.dt.float32, kind="ExternalInput").ap())
    args.append(nc.dram_tensor("out_0", (1, SEQ, D), _mybir.dt.float32, kind="ExternalOutput").ap())
    trunk_kernel(nc, *args)
    r = _run(nc, [arrays], core_ids=[0])
    return r.results[0]["out_0"]
```

```python
import math
from contextlib import ExitStack

import concourse.bass as bass
from concourse import mybir

F32 = mybir.dt.float32
F32R = mybir.dt.float32r
I32 = mybir.dt.int32
ALU = mybir.AluOpType
ACT = mybir.ActivationFunctionType
AX = mybir.AxisListType
ds = bass.ds

P = 128
D = 1024
SEQ = 256
DEPTH = 2
TT = SEQ // P
KD = D // P
CHUNK = 64
EPS = 1e-6
PLE = 256
MH, NOPE, ROPE, MV = 8, 64, 32, 64
MQK = NOPE + ROPE
QR, KVR = 256, 128
DH, DHD = 4, 64
DV = 2 * DHD
MAPS = 2 * DH
SPLITS = [(0, 416), (416, 928), (928, 1440), (1440, 1952)]
NG, NEG, FF = 4, 8, 256
NE = NG * NEG
KF = FF // P
BLK = 64
NSLOT = 2 * SEQ
CB = 512

SLOT = 2048
REGIONS = 3
RING = 3 * REGIONS
CHUNKS = 6
GU = 4
CH = 3 * SLOT // CHUNKS
NBUF = 3
DVE_SHARE = 9 / 16
MAXBLK = NE + NSLOT // BLK

HB = ROPE // 2
HD = DHD // 2
C_ID, C_TRI, C_ONE, C_MU, C_MV = 0, 128, 256, 384, 512
C_IOTA = C_MV + CHUNK
C_FM = C_IOTA + NSLOT
C_FD = C_FM + HB
C_E32 = C_FD + HD
C_G4 = C_E32 + NE
C_MOD = C_G4 + NG
C_J = C_MOD + NE
C_II = C_J + 1
NCONST = C_II + P

INV_2PI = 1.0 / (2.0 * math.pi)
TWO_PI_1 = 6.28125
TWO_PI_2 = 2029 / 2.0 ** 20
TWO_PI_3 = 2.0 * math.pi - TWO_PI_1 - TWO_PI_2
ROUND = 12582912.0
PI = 3.1415925


def constants():
    import numpy as np
    c = np.zeros((P, NCONST), np.float32)
    c[:, C_ID:C_ID + P] = np.eye(P)
    c[:, C_TRI:C_TRI + P] = np.triu(np.ones((P, P)), 1)
    c[:, C_ONE:C_ONE + P] = 1.0
    c[0, C_MU:C_MU + CHUNK] = 1.0
    c[CHUNK, C_MU:C_MU + CHUNK] = 1.0
    c[0, C_MV:C_MV + CHUNK] = -1e30
    c[CHUNK, C_MV:C_MV + CHUNK] = -1e30
    c[:, C_IOTA:C_IOTA + NSLOT] = np.arange(NSLOT)
    c[:, C_FM:C_FM + HB] = np.float32(10000.0) ** (-np.arange(0, ROPE, 2, dtype=np.float32) / ROPE)
    c[:, C_FD:C_FD + HD] = np.float32(10000.0) ** (-np.arange(0, DHD, 2, dtype=np.float32) / DHD)
    c[:, C_E32:C_E32 + NE] = np.arange(NE)
    c[:, C_G4:C_G4 + NG] = np.arange(NG)
    c[:, C_MOD:C_MOD + NE] = np.arange(NE) % REGIONS
    c[:, C_J] = np.arange(P)
    c[:, C_II:C_II + P] = np.tile(np.eye(BLK), (2, 2))
    return c


def stream_plan():
    items, pos, used = {}, 0, 0
    owner = [0] * RING
    fills = [0] * RING
    for layer in range(DEPTH):
        kinds = [("z0", 2), ("z1", 2), ("z2", 2), ("z3", 2), ("uq", 1), ("ukv", 1), ("out0", 2), ("out1", 2)]
        kinds += [(("expert", e), 3) for e in range(NE)]
        kinds += [("proj", 1), ("gate0", 2), ("gate1", 2)]
        for kind, n in kinds:
            expert = isinstance(kind, tuple)
            if kind == ("expert", 0):
                pos += -pos % RING
            if not expert and pos % RING + n > RING:
                pos += RING - pos % RING
            slots = [(pos + j) % RING for j in range(n)]
            dense = max([owner[s] for s in slots if not isinstance(owner[s], tuple)], default=0)
            after = max([owner[s][1] for s in slots if isinstance(owner[s], tuple)], default=None)
            if not expert:
                used += 1
            for j, s in enumerate(slots):
                owner[s] = kind if expert else used
                if not expert and j == 0:
                    fills[s] += 1
            items[layer, kind] = (slots, dense, after, [fills[s] for s in slots])
            pos += n
    return items


ITEM = stream_plan()

N_SMALL = 2 + DH + 4 + 12 + 4 + 2 + 2 * DEPTH
HT_BANK = (6, 7, 0, 1, 2, 3, 4, 5, 6, 7, 0, 1)
S_BANK = (5, 6, 7, 0)
T_BANK = (3, 4)
O_BANK = (1, 2)
DISP_BANK = (6, 7, 0, 1, 2, 3, 4, 6)
YT_BANK = (0, 1, 2, 3, 6, 7, 0, 1)


class Turn:

    FIRST, INNER, LAST = range(3)

    def __init__(self, at, kind):
        self.at, self.kind = at, kind
        self.shift = -(0, CHUNKS - GU, CHUNKS)[kind] % NBUF

    def count(self, c):
        less = (0, CHUNKS - GU, CHUNKS)[self.kind]
        return self.at * CHUNKS + (CHUNKS + c + 1 - less)


class Stage:

    def __init__(self, sem, n):
        self.sem, self.n = sem, n

    def at(self, layer, k=None):
        return self.sem, layer * self.n + (self.n if k is None else k)


def trunk_kernel(nc, x, p, positions, attn_norm, w_in, q_a_norm, w_uq, kv_a_norm, w_ukv, mla_q_norm,
                 mla_k_norm, diff_q_norm, diff_k_norm, lambda_q1, lambda_k1, lambda_q2, lambda_k2,
                 diff_subln, w_out, ffn_norm, w_group, b_group, w_router, b_router, w_gate, w_up,
                 w_down, ple_norm, w_ple_gate, w_ple_proj, const, out):
    with ExitStack() as ctx:
        def sb(name, shape, dt=F32):
            return ctx.enter_context(nc.sbuf_tensor(name, shape, dt))

        def sem(name):
            return ctx.enter_context(nc.semaphore(name))

        def stage(name, n):
            return Stage(sem(name), n)

        ctx.enter_context(nc.allow_non_contiguous_dma(reason="gains with one value per partition"))

        PS = ctx.enter_context(nc.psum_tensor("PS", [P, 8, CB], F32))

        ring = sb("ring", [P, RING * SLOT])
        cst = sb("cst", [P, NCONST])
        ident = cst[:, C_ID:C_ID + P]
        tri = cst[:, C_TRI:C_TRI + P]
        ones = cst[:, C_ONE:C_ONE + P]
        iota_slot = cst[:, C_IOTA:C_IOTA + NSLOT]
        h = sb("h", [P, TT, D])
        hn = sb("hn", [P, TT, D])
        aT = sb("aT", [P, KD, SEQ])
        g_in = sb("g_in", [P, DEPTH, 4, KD])
        g_cq = sb("g_cq", [P, DEPTH, 2])
        g_ckv = sb("g_ckv", [P, DEPTH, 1])
        g_nope = sb("g_nope", [MQK, DEPTH, 2])
        g_k = sb("g_k", [MQK, DEPTH])
        g_rope = sb("g_rope", [P, DEPTH, 2, 2, ROPE])
        g_diff = sb("g_diff", [P, DEPTH, 2, 2, DHD])
        bias = sb("bias", [P, DEPTH, NG + NE])
        w_rt = sb("w_rt", [P, DEPTH, KD, NG + NE])
        lams = sb("lams", [P, DEPTH, 2])
        lame = sb("lame", [P, DEPTH, 2])
        neglam = sb("neglam", [P, DEPTH])
        posi = sb("posi", [P, TT], I32)
        posf = sb("posf", [P, TT])
        NF = HB + HD
        trig_m = sb("trig_m", [P, 2, TT, 2, HB])
        trig_d = sb("trig_d", [P, 2, TT, 2, HD])
        rope_m = sb("rope_m", [P, 2, 2, TT, ROPE])
        rope_d = sb("rope_d", [P, 2, 2, TT, DHD])
        lss = sb("lss", [P, 2 * TT])
        lms = sb("lms", [P, 2 * TT])
        lrs = sb("lrs", [P, 2 * TT])
        ssh = sb("ssh", [P, TT])
        krs = sb("krs", [P, TT, ROPE])
        krr2 = sb("krr2", [P, TT, ROPE])
        ods = sb("ods", [P, TT * DH])
        odr = sb("odr", [P, TT * DH])
        mstat = sb("mstat", [P, TT])
        rstd = sb("rstd", [P, TT])
        expo = sb("expo", [P, 32])
        AREA = 11904
        area = sb("area", [P, AREA])
        used = [0]

        def part(n, **dims):
            v = area[:, used[0]:used[0] + n]
            used[0] += n
            assert used[0] <= AREA, used[0]
            return v

        lat = part(TT * 384).rearrange("p (t n) -> p t n", t=TT)
        kr = part(TT * ROPE).rearrange("p (t n) -> p t n", t=TT)
        krr = part(TT * ROPE).rearrange("p (t n) -> p t n", t=TT)
        cqT = part(2 * SEQ).rearrange("p (k t) -> p k t", k=2)
        ckvT = part(SEQ)
        junk = part(1024)
        rtmp = part(1024)
        dqr = part(TT * 512).rearrange("p (t n) -> p t n", t=TT)
        dkr = part(TT * 512).rearrange("p (t n) -> p t n", t=TT)
        vd = part(TT * 512).rearrange("p (t n) -> p t n", t=TT)
        vm = part(TT * 512).rearrange("p (t n) -> p t n", t=TT)
        qTm = part(MH * SEQ).rearrange("p (h t) -> p h t", h=MH)
        kTm = part(MH * SEQ).rearrange("p (h t) -> p h t", h=MH)
        vmf = vm.rearrange("p t n -> p (t n)")
        lamv = vmf[:, 0:DEPTH * 4 * DHD].rearrange("p (l j n) -> p l j n", l=DEPTH, j=4)
        lamp = vmf[:, DEPTH * 4 * DHD:DEPTH * 4 * DHD + 2 * DHD].rearrange("p (j n) -> p j n", j=2)
        kTf = kTm.rearrange("p h t -> p (h t)")
        nang = TT * 2 * NF
        ang, turns, red, trig_raw = (kTf[:, i * nang:(i + 1) * nang].rearrange("p (t c n) -> p t c n", t=TT, c=2)
                                     for i in range(4))
        hnf = hn[:, :, :].rearrange("p t n -> p (t n)")
        qm = hnf[:, 0:TT * MH * MQK].rearrange("p (t n) -> p t n", t=TT)
        ocat = sb("ocat", [P, TT, D])
        ocf = ocat[:, :, :].rearrange("p t n -> p (t n)")
        km = ocf[:, 0:TT * MH * MQK].rearrange("p (t n) -> p t n", t=TT)
        actjunk = ocf[:, 0:TT * D].rearrange("p (t n) -> p t n", t=TT)
        aTf = aT[:, :, :].rearrange("p k t -> p (k t)")
        qTd = aTf[:, 0:DH * SEQ].rearrange("p (h t) -> p h t", h=DH)
        kTd = aTf[:, DH * SEQ:2 * DH * SEQ].rearrange("p (h t) -> p h t", h=DH)
        prb = sb("prb", [P, 2, 384])
        prT = rtmp[:, 256:1024].rearrange("p (b n) -> p b n", b=2)
        ssq = sb("ssq", [P, 4, TT, 8])
        rsq = sb("rsq", [P, 4, TT, 8])
        sskr = sb("sskr", [P, TT])
        qsc = sb("qsc", [P, 2, 2, TT, 8])
        mx = sb("mx", [P, 16, TT])
        nbias = sb("nbias", [P, 16, TT])
        sums = sb("sums", [P, 16, TT])
        rinv = sb("rinv", [P, 16, TT])
        used[0] = 0
        mTs = part(KD * (NSLOT + BLK)).rearrange("p (k s) -> p k s", k=KD)
        yTs = part(KD * (NSLOT + BLK)).rearrange("p (k s) -> p k s", k=KD)
        ys = area[:, 0:4 * D].rearrange("p (s d) -> p s d", s=4)
        G = part(4 * SEQ).rearrange("p (s t) -> p s t", s=4)
        GT = part(TT * NSLOT).rearrange("p (t s) -> p t s", t=TT)
        GTf = GT.rearrange("p t s -> p (t s)")
        pin = GTf[:, 0:TT * PLE].rearrange("p (t n) -> p t n", t=TT)
        pT = GTf[:, TT * PLE:2 * TT * PLE].rearrange("p (k t) -> p k t", k=2)
        gtmp = ocat[:, :, 0:NSLOT]
        gur = ocf[:, 0:CB]
        yraw = ocf[:, CB:CB + D]
        sg = ocf[:, CB + D:CB + D + KF * BLK].rearrange("p (k s) -> p k s", k=KF)
        hb = ocf[:, CB + D + KF * BLK:CB + D + 2 * KF * BLK].rearrange("p (k s) -> p k s", k=KF)
        w_hi = sb("w_hi", [P, NBUF, CH], F32R)
        w_lo = sb("w_lo", [P, NBUF, CH], F32R)
        table = sb("table", [P, 1])
        w_hif, w_lof = (w[:, :, :].rearrange("p b n -> p (b n)") for w in (w_hi, w_lo))
        tok_hl = [w[:, 0:TT * D].rearrange("p (t n) -> p t n", t=TT) for w in (w_hif, w_lof)]
        pdis = w_hif[:, TT * D:TT * (D + NSLOT)].rearrange("p (t s) -> p t s", t=TT)
        x_hl = sb("x_hl", [P, KD, 2 * BLK], F32R)
        h_hl = sb("h_hl", [P, KF, 2 * BLK], F32R)
        raw = ring[:, :].rearrange("p (r s n) -> p r s n", r=REGIONS, s=3)
        rt = {}
        for name, shape in dict(lg=NG + NE, gmax=1, geq=NG, gc=NG, gi=1, goh=NG, gd=NG, ge=NG, gs=1, pen=NG,
                                ml=NE, m1=1, eq=NE, c1=NE, i1=1, oh1=NE, ml2=NE, m2=1, c2=NE, i2=1, oh2=NE,
                                dm=1, e2=1, w2=1, w1=1, den=1, M=NE, Mpre=NE, s1=1, s2=1, t1=NE, t2=NE).items():
            rt[name] = sb("rt_" + name, [P, TT, shape])
        Mp = sb("Mp", [P, NE])
        cnt = sb("cnt", [P, 4, NE])
        pfx = sb("pfx", [P, 4, NE])
        boh = sb("boh", [P, 4, NE])
        blk4 = sb("blk4", [P, 4])
        carry = sb("carry", [1, 1])
        ctl = sb("ctl", [4, 1 + P], I32)
        ctle = sb("ctle", [1, NE + 2], I32)
        ctlef = sb("ctlef", [1, NE + 2])
        sig = area[:, 4 * D:4 * D + 4 * CB].rearrange("p (j n) -> p j n", j=4)
        prod = area[:, 6 * D:6 * D + 4 * CB].rearrange("p (j n) -> p j n", j=4)

        arrived = [sem(f"arrived{s}") for s in range(RING)]
        gu_arrived = [sem(f"gu_arrived{r}") for r in range(REGIONS)]
        down_arrived = [sem(f"down_arrived{r}") for r in range(REGIONS)]
        weights_used = sem("weights_used")
        loaded = {k: sem("loaded_" + k) for k in ("x", "const", "p", "gain", "small")}
        sem_pool, sem_dve = sem("pool_order"), sem("dve_order")
        one = {k: sem("one_" + k) for k in ("pow", "lamp", "lame", "ang", "sin", "trig", "gains")}
        s_sq = stage("sq", 3 * TT)
        s_ms = stage("ms", 3)
        s_rs = stage("rs", 3)
        s_hn0 = stage("hn0", 3)
        s_hn1 = stage("hn1", 3)
        s_tr = stage("tr", 4 * 4)
        s_aTv = stage("aTv", 4 * 2)
        s_aTs = stage("aTs", 4 * 2)
        s_z = stage("z", 4)
        s_lsq = stage("lsq", 1)
        s_lms = stage("lms", 1)
        s_lrs = stage("lrs", 1)
        s_lat = stage("lat", 1)
        s_lT = stage("lT", 1)
        s_lTc = stage("lTc", 1)
        s_junk = stage("junk", 6)
        s_sum = stage("sum", 6)
        s_vd = stage("vd", 1)
        s_uq = stage("uq", TT)
        s_ukv = stage("ukv", TT)
        s_qn = stage("qn", TT)
        s_vm = stage("vm", TT)
        s_kn = stage("kn", TT)
        s_hms = stage("hms", 5)
        s_hrs = stage("hrs", 5)
        s_kr = stage("kr", 1)
        s_krr = stage("krr", 1)
        s_kpe = stage("kpe", TT)
        s_tab = stage("tab", 1)
        s_dq = stage("dq", 1)
        s_dk = stage("dk", 1)
        s_qr = stage("qr", TT)
        s_hT = stage("hT", 12)
        s_hTv = stage("hTv", 6)
        s_hTs = stage("hTs", 6)
        s_S = stage("S", 16)
        s_nb = stage("nb", 16)
        s_exp = stage("exp", 16)
        s_T = stage("T", 16)
        s_Tv = stage("Tv", 8)
        s_Ts = stage("Ts", 8)
        s_O = stage("O", 16)
        s_Oe = stage("Oe", 16)
        s_od = stage("od", 1)
        s_oc = stage("oc", 1)
        s_out = stage("out", 4)
        s_h0 = stage("h_tile0", 2)
        s_h = stage("hready", 3)
        s_rl = stage("rl", 1)
        s_ra = stage("ra", 2)
        s_re = stage("re", 2)
        s_M = stage("M", 1)
        s_pos = stage("pos", 1)
        s_ctl = stage("ctl", 1)
        s_th = stage("tok_hi", 1)
        s_tl = stage("tok_lo", 1)
        s_P = stage("P", 1)
        s_GT = stage("GT", 1)
        s_GTt = stage("GTt", 1)
        s_Gc = stage("Gc", 1)
        s_disp = stage("disp", KD)
        s_dv = stage("dv", KD // 2)
        s_da = stage("da", KD // 2)
        s_pad = stage("pad", 1)
        s_Gl = stage("Gl", 1)
        s_pTt = stage("pTt", 1)
        s_pTc = stage("pTc", 1)
        s_blkT = stage("blkT", 1)
        s_blk = stage("blk", 1)
        gu_ready = sem("gu_ready")
        down_ready = sem("down_ready")
        region_free = sem("region_free")
        s_xh = sem("x_hi")
        s_xl = sem("x_lo")
        s_hi = sem("w_hi_ready")
        s_lod = sem("w_lo_dve")
        s_lop = sem("w_lo_pool")
        s_ch = sem("chunk_used")
        s_gue = sem("gu_copied")
        s_B = sem("gu_turned")
        s_silu = sem("silu")
        s_hs = sem("h_steps")
        s_hl = sem("h_ready")
        s_ye = sem("y_copied")
        s_D = sem("y_turned")
        s_yc = sem("y_placed")
        s_yT = stage("yT", 8)
        s_yv = stage("yv", 4)
        s_ya = stage("ya", 4)
        s_cmb = stage("cmb", 4)
        s_gt = stage("gt", 4)
        s_sg = stage("sg", 4)
        s_fin = stage("fin", 4)
        stored = sem("stored")

        def bank(b, n=1):
            return PS[:, b, :] if n == 1 else PS[:, b:b + n, :]

        def slots(item, k, n):
            s = item[0][0]
            return ring[:, s * SLOT:s * SLOT + k * n].rearrange("p (k n) -> p k n", k=k)

        def arrival(eng, item):
            eng.wait_ge(arrived[item[0][0]], 16 * item[3][0])

        def s_sq_at(l, k):
            return s_sq.at(l, TT * (k + 1))

        def hT_dest(l, idx):
            if idx < 4:
                a = 2 * (idx % 2)
                return P, (qTd if idx < 2 else kTd)[:, a:a + 2, :], None
            a = 2 * ((idx - 4) % 4)
            return MQK, (qTm if idx < 8 else kTm)[0:MQK, a:a + 2, :], None if idx < 8 else g_k[:, l:l + 1]

        def block_column(eng, j):
            return eng.value_load(ctl[0:1, ds(j, 1)], min_val=0, max_val=NSLOT)

        def region_of(eng, j):
            return eng.value_load(ctl[1:2, ds(j + 1, 1)], min_val=0, max_val=REGIONS - 1)

        def expert_of(eng, j):
            return eng.value_load(ctl[2:3, ds(j + 1, 1)], min_val=1, max_val=NE)

        def block_counts(eng):
            blocks = eng.value_load(ctle[0:1, NE:NE + 1], min_val=NE, max_val=MAXBLK)
            before = eng.value_load(ctle[0:1, NE + 1:NE + 2], min_val=0, max_val=DEPTH * MAXBLK)
            return blocks, before

        def raw_chunk(region, c):
            if c < GU:
                return raw[:, ds(region, 1), 0:2, c * 512:(c + 1) * 512].rearrange("p o s n -> p (o s) n")
            return raw[:, ds(region, 1), 2:3, (c - GU) * CH:(c - GU + 1) * CH].rearrange("p o s n -> p (o s) n")

        def shares(v):
            n = v.shape[2]
            cut = int(n * DVE_SHARE)
            return v[:, :, 0:cut], v[:, :, cut:n]

        def low_part(eng, share, turn, c, region):
            return eng.tensor_tensor(shares(part_chunk(turn, w_lo, c))[share], shares(raw_chunk(region, c))[share],
                                     shares(part_chunk(turn, w_hi, c))[share].bitcast(F32), ALU.subtract)

        def part_chunk(turn, t, c):
            v = t[:, (c + turn.shift) % NBUF, :]
            return v.rearrange("p (s n) -> p s n", s=2 if c < GU else 1)

        block = ctx.enter_context(nc.Block())

        @block.sync
        def _(sp):
            for t in range(TT):
                sp.dma_start(h[:, t, :], x[0, t * P:(t + 1) * P, :]).then_inc(loaded["x"], 16)
            sp.dma_start(cst[:, :], const).then_inc(loaded["const"], 16)

            def load(layer, kind):
                item = ITEM[layer, kind]
                slot, dense, after, _ = item
                if dense:
                    sp.wait_ge(weights_used, dense)
                if after is not None:
                    down_over(after)
                s = slot[0]
                if kind[0] == "z":
                    a, b = SPLITS[int(kind[1])]
                    src = w_in[layer].rearrange("(p k) n -> p k n", k=KD)[:, :, a:b]
                    dst = slots(item, KD, b - a)
                elif kind == "uq":
                    src = w_uq[layer].rearrange("(p k) n -> p k n", k=2)
                    dst = slots(item, 2, MH * MQK)
                elif kind == "ukv":
                    src = w_ukv[layer]
                    dst = ring[:, s * SLOT:s * SLOT + 1024]
                elif kind[:3] == "out" or kind[:4] == "gate":
                    c = int(kind[-1])
                    w = w_out if kind[:3] == "out" else w_ple_gate
                    src = w[layer].rearrange("(p k) n -> p k n", k=KD)[:, :, c * CB:(c + 1) * CB]
                    dst = slots(item, KD, CB)
                else:
                    src = w_ple_proj[layer].rearrange("(p k) n -> p k n", k=2)
                    dst = slots(item, 2, D)
                sp.dma_start(dst, src).then_inc(arrived[s], 16)

            def chunks_used(e, more):
                over = sp.value_load(ctle[0:1, ds(e, 1)], min_val=1, max_val=DEPTH * MAXBLK)
                sp.wait_ge(s_ch, over * CHUNKS + (CHUNKS + NBUF + more))
                sp.sem_inc(region_free, 1)

            def gu_over(e):
                chunks_used(e, -2 if isinstance(e, int) and e == 0 else -(CHUNKS - GU + CHUNKS) + GU)

            def down_over(e):
                chunks_used(e, 0 if isinstance(e, int) and e == NE - 1 else GU)

            def load_gu(layer, e, region):
                for part_, w in enumerate((w_gate, w_up)):
                    src = w[layer].rearrange("g e (p k) f -> (g e) p (k f)", k=KD)[ds(e, 1)]
                    s = 3 * region + part_
                    sp.dma_start(ring[:, s * SLOT:(s + 1) * SLOT],
                                 src.rearrange("o p n -> (o p) n")).then_inc(gu_arrived[region], 16)

            def load_down(layer, e, region):
                src = w_down[layer].rearrange("g e (k p) d -> (g e) p k d", p=P)[ds(e, 1)]
                s = 3 * region + 2
                sp.dma_start(ring[:, s * SLOT:(s + 1) * SLOT].rearrange("p (k d) -> p k d", k=KF),
                             src.rearrange("o p k d -> (o p) k d")).then_inc(down_arrived[region], 16)

            def ready(layer, e, region, arrivals, done, each):
                turn = (e - region) // REGIONS if isinstance(e, int) else e
                fills = layer * len(range(region, NE, REGIONS)) + 1
                sp.wait_ge(arrivals[region], (turn + fills) * (each * 16))
                sp.sem_inc(done, 1)

            def gu_is_ready(layer, e):
                ready(layer, e, e % REGIONS, gu_arrived, gu_ready, 2)

            def down_is_ready(layer, e):
                ready(layer, e, e % REGIONS, down_arrived, down_ready, 1)

            for layer in range(DEPTH):
                for kind in ("z0", "z1", "z2", "z3", "uq", "ukv", "out0", "out1"):
                    load(layer, kind)
                for e in range(REGIONS):
                    dense = ITEM[layer, ("expert", e)][1]
                    if dense:
                        sp.wait_ge(weights_used, dense)
                    load_gu(layer, e, e)
                    load_down(layer, e, e)
                gu_is_ready(layer, 0)
                gu_is_ready(layer, 1)
                down_is_ready(layer, 0)
                sp.wait_ge(*s_ctl.at(layer))
                gu_over(0)
                load_gu(layer, REGIONS, 0)
                with sp.Fori(1, 1 + (NE - REGIONS - 1) // REGIONS) as i:
                    for r in range(1, REGIONS + 1):
                        e = i * REGIONS + r
                        ready(layer, i + (r - 2) // REGIONS, (r - 2) % REGIONS, gu_arrived, gu_ready, 2)
                        ready(layer, i + (r - 3) // REGIONS, (r - 3) % REGIONS, down_arrived, down_ready, 1)
                        gu_over(e - REGIONS)
                        load_gu(layer, e, r % REGIONS)
                        down_over(e - 1 - REGIONS)
                        load_down(layer, e - 1, r - 1)
                for e in range(1 + (NE - 1) // REGIONS * REGIONS, NE):
                    gu_is_ready(layer, e - 2)
                    down_is_ready(layer, e - 3)
                    gu_over(e - REGIONS)
                    load_gu(layer, e, e % REGIONS)
                    down_over(e - 1 - REGIONS)
                    load_down(layer, e - 1, (e - 1) % REGIONS)
                gu_is_ready(layer, NE - 2)
                down_is_ready(layer, NE - 3)
                down_over(NE - 1 - REGIONS)
                load_down(layer, NE - 1, (NE - 1) % REGIONS)
                gu_is_ready(layer, NE - 1)
                down_is_ready(layer, NE - 2)
                sp.wait_ge(*s_Gc.at(layer))
                sp.dma_start(pin, p[layer, 0].rearrange("(t p) n -> p t n", p=P)).then_inc(s_Gl.sem, 16)
                load(layer, "proj")
                load(layer, "gate0")
                down_is_ready(layer, NE - 1)
                load(layer, "gate1")
            for t in range(TT):
                for c in range(2):
                    sp.wait_ge(*s_fin.at(DEPTH - 1, 2 * t + c + 1))
                    sp.dma_start(out[0, t * P:(t + 1) * P, c * CB:(c + 1) * CB],
                                 h[:, t, c * CB:(c + 1) * CB]).then_inc(stored, 16)
            sp.wait_ge(stored, 16 * 2 * TT)

        @block.gpsimd
        def _(pool):
            chain = [0]
            s_chain = sem_pool

            def link(ins):
                chain[0] += 1
                ins.then_inc(s_chain, 1)
                pool.wait_ge(s_chain, chain[0])

            nc.gpsimd.memset(expo[:, :], -0.5).then_inc(one["pow"], 1)
            pool.wait_ge(one["pow"], 1)
            def root(dst, src, n, wait, done):
                pool.wait_ge(*wait)
                nc.gpsimd.tensor_tensor(dst, src, expo[:, 0:n], ALU.pow).then_inc(done.sem, 1)

            for l in range(DEPTH):
                root(rstd[:, :], mstat[:, :], TT, s_ms.at(l, 1), s_rs)
                pool.wait_ge(one["trig"], 6)
                pool.wait_ge(loaded["small"], 16 * N_SMALL)
                if l:
                    pool.wait_ge(*s_qr.at(l - 1))
                    pool.wait_ge(*s_krr.at(l - 1))
                for qk in range(2):
                    for cs in range(2):
                        g = g_rope[:, l, qk, cs, :].unsqueeze(1).broadcast_to([P, TT, ROPE])
                        link(nc.gpsimd.tensor_tensor(rope_m[:, qk, cs], trig_m[:, cs].rearrange("p t a n -> p t (a n)"),
                                                     g, ALU.mult))
                        g = g_diff[:, l, qk, cs, :].unsqueeze(1).broadcast_to([P, TT, DHD])
                        ins = nc.gpsimd.tensor_tensor(rope_d[:, qk, cs], trig_d[:, cs].rearrange("p t a n -> p t (a n)"),
                                                      g, ALU.mult)
                        if qk == 1 and cs == 1:
                            ins.then_inc(s_tab.sem, 1)
                        else:
                            link(ins)

                root(lrs[:, :], lms[:, :], 4, s_lms.at(l), s_lrs)

                def head_root(w):
                    root(rsq[:, w].rearrange("p t h -> p (t h)"), ssq[:, w].rearrange("p t h -> p (t h)"), 16,
                         s_hms.at(l, w + 1), s_hrs)

                head_root(0)
                pool.wait_ge(*s_kr.at(l))
                pool.wait_ge(*s_tab.at(l))
                c_, s_ = rope_m[:, 1, 0], rope_m[:, 1, 1]
                t_ = krs[:, :, :]
                link(nc.gpsimd.tensor_tensor(krr, kr, c_, ALU.mult))
                link(nc.gpsimd.tensor_tensor(t_[:, :, 0:HB], kr[:, :, HB:ROPE], s_[:, :, 0:HB], ALU.mult))
                link(nc.gpsimd.tensor_tensor(t_[:, :, HB:ROPE], kr[:, :, 0:HB], s_[:, :, HB:ROPE], ALU.mult))
                link(nc.gpsimd.tensor_tensor(krr, krr, t_, ALU.add))
                nc.gpsimd.tensor_copy(krr2[:, :, :], krr).then_inc(s_krr.sem, 1)
                head_root(1)
                head_root(2)
                head_root(3)
                pool.wait_ge(*s_hrs.at(l, 4))
                pool.wait_ge(*s_krr.at(l))
                for t in range(TT):
                    kv = km[:, t, :].rearrange("p (h n) -> p h n", h=MH)[:, :, NOPE:MQK]
                    nc.gpsimd.tensor_tensor(kv, krr2[:, t, :].unsqueeze(1).broadcast_to([P, MH, ROPE]),
                                            rsq[:, 3, t, :].unsqueeze(2).broadcast_to([P, MH, ROPE]),
                                            ALU.mult).then_inc(s_kpe.sem, 1)
                pool.wait_ge(*s_hms.at(l, 5))
                nc.gpsimd.tensor_tensor(odr[:, :], ods[:, :], expo[:, 0:TT * DH], ALU.pow).then_inc(s_hrs.sem, 1)
                root(rstd[:, :], mstat[:, :], TT, s_ms.at(l, 2), s_rs)
                nc.gpsimd.memset(mTs[:, :, NSLOT:NSLOT + BLK], 0.0).then_inc(s_pad.sem, 1)
                pool.wait_ge(*s_th.at(l))
                nc.gpsimd.tensor_tensor(tok_hl[1], hn[:, :, :], tok_hl[0].bitcast(F32), ALU.subtract).then_inc(s_tl.sem, 1)
                pool.wait_ge(*s_ctl.at(l))
                blocks, before = block_counts(pool)

                def low(turn, chunks, region):
                    for c in chunks:
                        pool.wait_ge(s_hi, turn.count(c))
                        low_part(nc.gpsimd, 1, turn, c, region).then_inc(s_lop, 1)

                def x_low(m, j):
                    first = block_column(pool, j + 1)
                    pool.wait_ge(s_xh, m + 1)
                    nc.gpsimd.tensor_tensor(x_hl[:, :, BLK:2 * BLK], mTs[:, :, ds(first, BLK)],
                                            x_hl[:, :, 0:BLK].bitcast(F32), ALU.subtract).then_inc(s_xl, 1)

                pool.wait_ge(*s_dv.at(l))
                pool.wait_ge(*s_da.at(l))
                pool.wait_ge(*s_pad.at(l))
                x_low(before + l, 0)
                low(Turn(before, Turn.FIRST), range(GU), region_of(pool, 0))
                x_low(before + (l + 1), 1)
                with pool.Fori(1, blocks) as j:
                    turn = Turn(before + j, Turn.INNER)
                    region, last_region = region_of(pool, j), region_of(pool, j - 1)
                    low(turn, range(GU), region)
                    low(turn, range(GU, CHUNKS), last_region)
                    x_low(before + j + (l + 1), j + 1)
                low(Turn(before + blocks, Turn.LAST), range(GU, CHUNKS), region_of(pool, blocks - 1))
                root(rstd[:, :], mstat[:, :], TT, s_ms.at(l, 3), s_rs)

        @block.scalar
        def _(act):
            act.dma_start(posi[:, :], positions.rearrange("b (t p) -> p (b t)", p=P)).then_inc(loaded["p"], 16)
            act.dma_start(g_in[:, :, 0, :], attn_norm.rearrange("l (p k) -> p l k", k=KD)).then_inc(loaded["gain"], 16)

            def small_loads():
                by_row = lambda v, k: v.rearrange("l (p k) -> p l k", k=k)
                loads = [(g_in[:, :, 2, :], by_row(ffn_norm, KD)), (g_in[:, :, 3, :], by_row(ple_norm, KD))]
                for qk, (gm, gd) in enumerate(((mla_q_norm, diff_q_norm), (mla_k_norm, diff_k_norm))):
                    for cs, at, v in ((0, 0, gd[:, :]), (1, 0, gd[:, HD:DHD]), (1, HD, gd[:, 0:HD])):
                        loads.append((g_diff[:, :, qk, cs, at:at + v.shape[1]], v.partition_broadcast(P)))
                    for cs, at, v in ((0, 0, gm[:, NOPE:MQK]), (1, 0, gm[:, NOPE + HB:MQK]),
                                      (1, HB, gm[:, NOPE:NOPE + HB])):
                        loads.append((g_rope[:, :, qk, cs, at:at + v.shape[1]], v.partition_broadcast(P)))
                for j, v in enumerate((lambda_q1, lambda_k1, lambda_q2, lambda_k2)):
                    loads.append((lamv[:, :, j, :], v.partition_broadcast(P)))
                for hd in range(DH):
                    loads.append((g_in[64 + 16 * hd:80 + 16 * hd, :, 1, :], by_row(diff_subln, KD)))
                loads += [(g_cq[:, :, :], by_row(q_a_norm, 2)), (g_ckv[:, :, :], by_row(kv_a_norm, 1)),
                          (g_nope[0:NOPE, :, 0:1], by_row(mla_q_norm[:, 0:NOPE], 1)),
                          (g_nope[0:NOPE, :, 1:2], by_row(mla_k_norm[:, 0:NOPE], 1)),
                          (bias[:, :, 0:NG], b_group.partition_broadcast(P)),
                          (bias[:, :, NG:NG + NE], b_router.partition_broadcast(P))]
                for l in range(DEPTH):
                    loads += [(w_rt[:, l, :, 0:NG], w_group[l].rearrange("(p k) n -> p k n", k=KD)),
                              (w_rt[:, l, :, NG:NG + NE], w_router[l].rearrange("(p k) n -> p k n", k=KD))]
                assert len(loads) == N_SMALL
                for dst, src in loads:
                    act.dma_start(dst, src).then_inc(loaded["small"], 16)

            def square_tiles(l, k):
                for t in range(TT):
                    if k == 0 and l == 0:
                        act.wait_ge(loaded["x"], 32)
                    elif k == 0:
                        act.wait_ge(*s_h.at(l - 1, 3))
                    else:
                        act.wait_ge(*(s_h0 if t == 0 else s_h).at(l, k))
                    act.activation(actjunk[:, t, :], h[:, t, :], ACT.Square,
                                   accum_out=ssh[:, t:t + 1]).then_inc(s_sq.sem, 1)

            def norm_tile(l, k):
                act.wait_ge(*s_rs.at(l, k + 1))
                act.activation(hn[:, 0, :], h[:, 0, :], ACT.Copy, scale=rstd[:, 0:1]).then_inc(s_hn0.sem, 1)

            def evac_pass(l, n_):
                for b in (2, 3):
                    act.wait_ge(*s_tr.at(l, 4 * n_ + b + 1))
                    for k in (2 * b, 2 * b + 1):
                        ins = act.activation(aT[:, k, :], PS[:, b, (k % 2) * SEQ:(k % 2 + 1) * SEQ], ACT.Copy,
                                             scale=g_in[:, l, n_, k:k + 1])
                    ins.then_inc(s_aTs.sem, 1)

            for l in range(DEPTH):
                square_tiles(l, 0)
                norm_tile(l, 0)
                if l == 0:
                    act.wait_ge(loaded["gain"], 16)
                evac_pass(l, 0)
                if l == 0:
                    act.wait_ge(one["ang"], 1)
                    for cs in range(2):
                        act.activation(trig_raw[:, :, cs, :], red[:, :, cs, :], ACT.Sin).then_inc(one["sin"], 1)
                    small_loads()
                    act.wait_ge(one["lamp"], 2 * DEPTH)
                    act.activation(lame[:, :, :], lams[:, :, :], ACT.Exp).then_inc(one["lame"], 1)
                    act.wait_ge(one["gains"], 1)
                act.wait_ge(*s_z.at(l, 1))
                for t in range(TT):
                    act.activation(actjunk[:, t, 0:QR], PS[:, 4 + t, 0:QR], ACT.Square, accum_out=lss[:, t:t + 1])
                    ins = act.activation(actjunk[:, t, QR:QR + KVR], PS[:, 4 + t, QR:QR + KVR], ACT.Square,
                                         accum_out=lss[:, 2 + t:3 + t])
                ins.then_inc(s_lsq.sem, 1)
                act.wait_ge(*s_z.at(l, 2))
                act.activation(junk, bank(6, 2).rearrange("p t n -> p (t n)"), ACT.Square).then_inc(s_junk.sem, 1)
                act.wait_ge(*s_z.at(l, 3))
                act.wait_ge(*s_sum.at(l, 1))
                act.activation(junk, bank(0, 2).rearrange("p t n -> p (t n)"), ACT.Square).then_inc(s_junk.sem, 1)
                act.wait_ge(*s_z.at(l, 4))
                act.activation(vd.rearrange("p t n -> p (t n)"), bank(2, 2).rearrange("p t n -> p (t n)"),
                               ACT.Copy).then_inc(s_vd.sem, 1)
                for t, b in enumerate((6, 0)):
                    act.wait_ge(*s_uq.at(l, t + 1))
                    act.wait_ge(*s_sum.at(l, 2 + t))
                    src = bank(b, 2)[:, :, 0:4 * MQK]
                    act.activation(junk[:, 0:MH * MQK].rearrange("p (b n) -> p b n", b=2), src,
                                   ACT.Square).then_inc(s_junk.sem, 1)
                    dst = qm[:, t, :].rearrange("p (b h n) -> p b h n", b=2, h=4)[:, :, :, 0:NOPE]
                    srcn = src.rearrange("p b (h n) -> p b h n", h=4)[:, :, :, 0:NOPE]
                    act.activation(dst, srcn, ACT.Copy).then_inc(s_qn.sem, 1)
                for t, b in enumerate((2, 4)):
                    act.wait_ge(*s_ukv.at(l, t + 1))
                    src = bank(b, 2).rearrange("p b (h n) -> p b h n", h=4)
                    if t == 0:
                        act.wait_ge(*s_sum.at(l, 4))
                    dst = junk.rearrange("p (t b h n) -> p t b h n", t=2, b=2, h=4)[:, t]
                    ins = act.activation(dst, src[:, :, :, 0:NOPE], ACT.Square)
                    if t == 1:
                        ins.then_inc(s_junk.sem, 1)
                    act.activation(vm[:, t, :].rearrange("p (b h n) -> p b h n", b=2, h=4), src[:, :, :, NOPE:],
                                   ACT.Copy).then_inc(s_vm.sem, 1)
                for j in range(6):
                    idx = 2 * j + 1
                    act.wait_ge(*s_hT.at(l, idx + 1))
                    rows, dst, gain = hT_dest(l, idx)
                    src = PS[0:rows, HT_BANK[idx], :].rearrange("p (h t) -> p h t", h=2)
                    if gain is None:
                        act.activation(dst, src, ACT.Copy).then_inc(s_hTs.sem, 1)
                    else:
                        act.activation(dst, src, ACT.Copy, scale=gain).then_inc(s_hTs.sem, 1)
                for m in range(16 + 1):
                    if m < 16:
                        act.wait_ge(*s_nb.at(l, m + 1))
                        if m >= 2:
                            act.wait_ge(*s_T.at(l, m - 1))
                        kind, hd = (0, m) if m < MAPS else (1, m - MAPS)
                        b = S_BANK[m % 4]
                        act.activation(prb[:, m % 2, 0:P], PS[:, b, 0:P], ACT.Exp, bias=nbias[:, m, 0:1],
                                       scale=qsc[:, kind, 0, 0, hd:hd + 1], accum_out=sums[:, m, 0:1])
                        act.activation(prb[:, m % 2, P:3 * P], PS[:, b, P:3 * P], ACT.Exp, bias=nbias[:, m, 1:2],
                                       scale=qsc[:, kind, 0, 1, hd:hd + 1],
                                       accum_out=sums[:, m, 1:2]).then_inc(s_exp.sem, 1)
                    if m >= 1 and (m - 1) % 2 == 1:
                        j = m - 1
                        act.wait_ge(*s_T.at(l, j + 1))
                        if j >= 2:
                            act.wait_ge(*s_O.at(l, j - 1))
                        act.activation(prT[:, 1, :], PS[:, 4, 0:384], ACT.Copy).then_inc(s_Ts.sem, 1)
                    if m == MAPS + 3:
                        act.wait_ge(*s_od.at(l))
                        act.activation(junk.rearrange("p (t n) -> p t n", t=TT), ocat[:, :, 512:1024],
                                       ACT.Square).then_inc(s_junk.sem, 1)
                evac_pass(l, 1)
                square_tiles(l, 1)
                norm_tile(l, 1)
                evac_pass(l, 2)
                act.wait_ge(*s_hn1.at(l, 2))
                act.activation(tok_hl[0], hn[:, :, :], ACT.Copy).then_inc(s_th.sem, 1)
                act.wait_ge(*s_ra.at(l, 1))
                act.activation(rt["ge"][:, :, :], rt["gd"][:, :, :], ACT.Exp).then_inc(s_re.sem, 1)
                act.wait_ge(*s_ra.at(l, 2))
                act.activation(rt["e2"][:, :, :], rt["dm"][:, :, :], ACT.Exp).then_inc(s_re.sem, 1)
                act.activation(table[:, :], cst[:, C_G4:C_G4 + 1], ACT.Silu)
                for k in range(1, KD, 2):
                    act.wait_ge(*s_disp.at(l, k + 1))
                    act.activation(mTs[:, k, 0:NSLOT], PS[:, DISP_BANK[k], :], ACT.Copy,
                                   scale=g_in[:, l, 2, k:k + 1]).then_inc(s_da.sem, 1)
                act.wait_ge(*s_ctl.at(l))
                act.wait_ge(*s_dv.at(l))
                act.wait_ge(*s_da.at(l))
                act.wait_ge(*s_pad.at(l))
                blocks, before = block_counts(act)

                def high(turn, c, region):
                    act.wait_ge(s_ch, turn.count(c))
                    act.activation(part_chunk(turn, w_hi, c), raw_chunk(region, c), ACT.Copy).then_inc(s_hi, 1)

                def silu(at):
                    act.wait_ge(s_B, at)
                    act.activation(sg, PS[:, 5, :].rearrange("p (q s) -> p q s", q=4)[:, 0:KF, 0:BLK],
                                   ACT.Silu).then_inc(s_silu, 1)

                def copy_gu(turn, j):
                    first = block_column(act, j + 2)
                    act.wait_ge(s_ch, turn.count(GU - 1) + NBUF)
                    act.activation(gur, PS[:, 4, :], ACT.Copy).then_inc(s_gue, 1)
                    act.activation(x_hl[:, :, 0:BLK], mTs[:, :, ds(first, BLK)], ACT.Copy).then_inc(s_xh, 1)

                def high_down(turn, j):
                    region, expert = region_of(act, j), expert_of(act, j)
                    act.wait_ge(down_ready, expert + l * NE)
                    for c in range(GU, CHUNKS):
                        high(turn, c, region)

                turn = Turn(before, Turn.FIRST)
                region = region_of(act, 0)
                act.activation(x_hl[:, :, 0:BLK], mTs[:, :, 0:BLK], ACT.Copy).then_inc(s_xh, 1)
                act.wait_ge(gu_ready, 1 + l * NE)
                for c in range(GU):
                    high(turn, c, region)
                copy_gu(turn, 0)
                with act.Fori(1, blocks) as j:
                    turn = Turn(before + j, Turn.INNER)
                    region, expert = region_of(act, j), expert_of(act, j)
                    act.wait_ge(gu_ready, expert + l * NE)
                    for c in range(GU):
                        high(turn, c, region)
                        if c == 1:
                            silu(before + j)
                    high_down(turn, j - 1)
                    copy_gu(turn, j)
                silu(before + blocks)
                high_down(Turn(before + blocks, Turn.LAST), blocks - 1)
                for j in range(4):
                    act.wait_ge(*s_yT.at(l, 2 * j + 2))
                    act.activation(ys[:, j, CB:2 * CB], PS[:, YT_BANK[2 * j + 1], :], ACT.Copy).then_inc(s_ya.sem, 1)
                square_tiles(l, 2)
                norm_tile(l, 2)
                evac_pass(l, 3)
                for j in range(4):
                    act.wait_ge(*s_gt.at(l, j + 1))
                    act.activation(sig[:, j, :], PS[:, j, :], ACT.Sigmoid).then_inc(s_sg.sem, 1)

        @block.vector
        def _(dve):
            chain = [0]

            def link(ins):
                chain[0] += 1
                ins.then_inc(sem_dve, 1)
                dve.wait_ge(sem_dve, chain[0])

            tt, ts, stt = nc.vector.tensor_tensor, nc.vector.tensor_scalar, nc.vector.scalar_tensor_tensor
            cp, red_ = nc.vector.tensor_copy, nc.vector.tensor_reduce

            dve.sem_inc(s_ch, CHUNKS + NBUF)
            dve.sem_inc(s_hi, CHUNKS)
            dve.sem_inc(s_lod, CHUNKS)
            dve.sem_inc(s_lop, CHUNKS)
            dve.sem_inc(s_hs, 2)
            dve.sem_inc(s_D, 1)
            dve.sem_inc(s_yc, 1)
            nc.vector.memset(g_in[0:64, :, 1, :], 1.0)
            nc.vector.memset(g_k[:, :], 1.0)
            link(nc.vector.memset(carry[:, :], 0.0))

            def rotary_angles():
                dve.wait_ge(loaded["const"], 16)
                dve.wait_ge(loaded["p"], 16)
                link(cp(posf[:, :], posi[:, :]))
                freq = cst[:, C_FM:C_FM + NF]
                for t in range(TT):
                    for cs in range(2):
                        ins = ts(ang[:, t, cs, :], freq, posf[:, t:t + 1], None, ALU.mult)
                link(ins)
                for cs in range(2):
                    ins = ts(turns[:, :, cs, :], ang[:, :, cs, :], INV_2PI, 0.25 * (1 - cs), ALU.mult, ALU.add)
                link(ins)
                link(ts(turns[:, :, :, :], turns[:, :, :, :], ROUND, None, ALU.add))
                link(ts(turns[:, :, :, :], turns[:, :, :, :], -ROUND, None, ALU.add))
                link(stt(out=red[:, :, :, :], in0=turns[:, :, :, :], scalar=-TWO_PI_1, in1=ang[:, :, :, :],
                         op0=ALU.mult, op1=ALU.add))
                link(stt(out=red[:, :, :, :], in0=turns[:, :, :, :], scalar=-TWO_PI_2, in1=red[:, :, :, :],
                         op0=ALU.mult, op1=ALU.add))
                link(stt(out=red[:, :, :, :], in0=turns[:, :, :, :], scalar=-TWO_PI_3, in1=red[:, :, :, :],
                         op0=ALU.mult, op1=ALU.add))
                link(ts(red[:, :, 0, :], red[:, :, 0, :], math.pi / 2, None, ALU.add))
                ts(red[:, :, :, :], red[:, :, :, :], PI, -PI, ALU.min, ALU.max).then_inc(one["ang"], 1)

            def rotary_tables():
                dve.wait_ge(one["sin"], 2)
                for dst, a, n in ((trig_m, 0, HB), (trig_d, HB, HD)):
                    cos, sin = trig_raw[:, :, 0, a:a + n], trig_raw[:, :, 1, a:a + n]
                    cp(dst[:, 0], cos.unsqueeze(2).broadcast_to([P, TT, 2, n])).then_inc(one["trig"], 1)
                    ts(dst[:, 1, :, 0, :], sin, -1.0, None, ALU.mult).then_inc(one["trig"], 1)
                    cp(dst[:, 1, :, 1, :], sin).then_inc(one["trig"], 1)

            def gains():
                dve.wait_ge(loaded["small"], 16 * N_SMALL)
                for l in range(DEPTH):
                    init = 0.8 - 0.6 * math.exp(-0.3 * l)
                    ts(g_in[64:P, l, 1, :], g_in[64:P, l, 1, :], 1.0 - init, None, ALU.mult)
                    tt(g_k[0:NOPE, l:l + 1], g_nope[0:NOPE, l, 0:1], g_nope[0:NOPE, l, 1:2], ALU.mult)
                    for j in range(2):
                        link(tt(lamp[:, j, :], lamv[:, l, 2 * j, :], lamv[:, l, 2 * j + 1, :], ALU.mult))
                        red_(lams[:, l, j:j + 1], lamp[:, j, :], AX.X, ALU.add).then_inc(one["lamp"], 1)
                dve.wait_ge(one["lame"], 1)
                for l in range(DEPTH):
                    init = 0.8 - 0.6 * math.exp(-0.3 * l)
                    link(tt(neglam[:, l:l + 1], lame[:, l, 1:2], lame[:, l, 0:1], ALU.subtract))
                    link(ts(neglam[:, l:l + 1], neglam[:, l:l + 1], -init, None, ALU.add))

            def norm(l, k):
                dve.wait_ge(*s_sq_at(l, k))
                ts(mstat[:, :], ssh[:, :], 1.0 / D, EPS, ALU.mult, ALU.add).then_inc(s_ms.sem, 1)
                dve.wait_ge(*s_rs.at(l, k + 1))
                ts(hn[:, 1, :], h[:, 1, :], rstd[:, 1:2], None, ALU.mult).then_inc(s_hn1.sem, 1)

            def evac_pass(l, n_):
                for b in (0, 1):
                    dve.wait_ge(*s_tr.at(l, 4 * n_ + b + 1))
                    g = g_in[:, l, n_, 2 * b:2 * b + 2].unsqueeze(2).broadcast_to([P, 2, SEQ])
                    tt(aT[:, 2 * b:2 * b + 2, :], bank(b).rearrange("p (k t) -> p k t", k=2), g,
                       ALU.mult).then_inc(s_aTv.sem, 1)

            def head_ms(w, n):
                ts(ssq[:, w], ssq[:, w], 1.0 / n, EPS, ALU.mult, ALU.add).then_inc(s_hms.sem, 1)

            def rotate(dst, src, tab, scratch, half):
                c, s = tab
                link(tt(dst, src, c, ALU.mult))
                tt(scratch[:, :, :, 0:half], src[:, :, :, half:2 * half], s[:, :, :, 0:half], ALU.mult)
                link(tt(scratch[:, :, :, half:2 * half], src[:, :, :, 0:half], s[:, :, :, half:2 * half], ALU.mult))
                return tt(dst, dst, scratch, ALU.add)

            def table(t, n, heads, token=None):
                v = t if token is None else t[:, token:token + 1].broadcast_to([P, 2, n])
                return v.unsqueeze(2).broadcast_to([P, 2, heads, n])

            for l in range(DEPTH):
                norm(l, 0)
                if l == 0:
                    rotary_angles()
                    dve.wait_ge(loaded["gain"], 16)
                evac_pass(l, 0)
                if l == 0:
                    rotary_tables()
                    gains()
                    dve.sem_inc(one["gains"], 1)
                dve.wait_ge(*s_lsq.at(l))
                ts(lms[:, 0:TT], lss[:, 0:TT], 1.0 / QR, EPS, ALU.mult, ALU.add)
                ts(lms[:, TT:2 * TT], lss[:, TT:2 * TT], 1.0 / KVR, EPS, ALU.mult, ALU.add).then_inc(s_lms.sem, 1)
                link(cp(kr, bank(4, 2)[:, :, QR + KVR:QR + KVR + ROPE]))
                link(tt(krs[:, :, :], kr, kr, ALU.mult))
                red_(sskr[:, :], krs[:, :, :], AX.X, ALU.add).then_inc(s_kr.sem, 1)
                dve.wait_ge(*s_lrs.at(l))
                for t in range(TT):
                    ts(lat[:, t, 0:QR], PS[:, 4 + t, 0:QR], lrs[:, t:t + 1], None, ALU.mult)
                    ins = ts(lat[:, t, QR:QR + KVR], PS[:, 4 + t, QR:QR + KVR], lrs[:, TT + t:TT + t + 1], None, ALU.mult)
                ins.then_inc(s_lat.sem, 1)
                dve.wait_ge(*s_junk.at(l, 1))
                red_(ssq[:, 0].rearrange("p t h -> p (t h)"), junk.rearrange("p (h n) -> p h n", n=DHD), AX.X,
                     ALU.add).then_inc(s_sum.sem, 1)
                dve.wait_ge(*s_sum.at(l, 1))
                head_ms(0, DHD)
                dve.wait_ge(*s_tab.at(l))
                src = bank(6, 2).rearrange("p t (h n) -> p t h n", h=8)
                scratch = rtmp.rearrange("p (t h n) -> p t h n", t=TT, h=8)
                rotate(dqr.rearrange("p t (h n) -> p t h n", h=8), src,
                       [table(rope_d[:, 0, cs], DHD, 8) for cs in range(2)], scratch, HD).then_inc(s_dq.sem, 1)
                dve.wait_ge(*s_lT.at(l))
                tt(cqT, bank(4).rearrange("p (k t) -> p k t", k=2), g_cq[:, l, :].unsqueeze(2).broadcast_to([P, 2, SEQ]),
                   ALU.mult)
                ts(ckvT, PS[:, 5, 0:SEQ], g_ckv[:, l, 0:1], None, ALU.mult).then_inc(s_lTc.sem, 1)
                dve.wait_ge(*s_junk.at(l, 2))
                red_(ssq[:, 1].rearrange("p t h -> p (t h)"), junk.rearrange("p (h n) -> p h n", n=DHD), AX.X,
                     ALU.add).then_inc(s_sum.sem, 1)
                dve.wait_ge(*s_sum.at(l, 2))
                head_ms(1, DHD)
                dk4 = dkr.rearrange("p t (h n) -> p t h n", h=8)
                dve.wait_ge(*s_dq.at(l))
                link(rotate(dk4, bank(0, 2).rearrange("p t (h n) -> p t h n", h=8),
                            [table(rope_d[:, 1, cs], DHD, 8) for cs in range(2)], scratch, HD))
                dve.wait_ge(*s_hrs.at(l, 2))
                tt(dk4, dk4, rsq[:, 1].unsqueeze(3).broadcast_to([P, TT, 8, DHD]), ALU.mult).then_inc(s_dk.sem, 1)
                for sign in range(2):
                    ts(qsc[:, 0, sign], rsq[:, 0], (1 - 2 * sign) * DHD ** -0.5, None, ALU.mult)
                dve.wait_ge(*s_dk.at(l))
                for t, b in enumerate((6, 0)):
                    dve.wait_ge(*s_junk.at(l, 3 + t))
                    red_(ssq[:, 2, t], junk[:, 0:MH * MQK].rearrange("p (h n) -> p h n", n=MQK), AX.X,
                         ALU.add).then_inc(s_sum.sem, 1)
                    dve.wait_ge(*s_qn.at(l, t + 1))
                    src = bank(b, 2)[:, :, 0:4 * MQK].rearrange("p b (h n) -> p b h n", h=4)[:, :, :, NOPE:MQK]
                    dst = qm[:, t, :].rearrange("p (b h n) -> p b h n", b=2, h=4)[:, :, :, NOPE:MQK]
                    scr = rtmp[:, 256 * t:256 * t + 256].rearrange("p (b h n) -> p b h n", b=2, h=4)
                    rotate(dst, src, [table(rope_m[:, 0, cs], ROPE, 4, t) for cs in range(2)], scr,
                           HB).then_inc(s_qr.sem, 1)
                dve.wait_ge(*s_sum.at(l, 4))
                head_ms(2, MQK)
                dve.wait_ge(*s_junk.at(l, 5))
                red_(ssq[:, 3].rearrange("p t h -> p (t h)"), junk.rearrange("p (h n) -> p h n", n=NOPE), AX.X,
                     ALU.add).then_inc(s_sum.sem, 1)
                dve.wait_ge(*s_sum.at(l, 5))
                link(tt(ssq[:, 3], ssq[:, 3], sskr[:, :].unsqueeze(2).broadcast_to([P, TT, 8]), ALU.add))
                head_ms(3, MQK)
                dve.wait_ge(*s_hrs.at(l, 4))
                dve.wait_ge(*s_vm.at(l))
                for t, b in enumerate((2, 4)):
                    src = bank(b, 2).rearrange("p b (h n) -> p b h n", h=4)[:, :, :, 0:NOPE]
                    dst = km[:, t, :].rearrange("p (b h n) -> p b h n", b=2, h=4)[:, :, :, 0:NOPE]
                    r = rsq[:, 3, t, :].rearrange("p (b h) -> p b h", b=2).unsqueeze(3).broadcast_to([P, 2, 4, NOPE])
                    tt(dst, src, r, ALU.mult).then_inc(s_kn.sem, 1)
                for sign in range(2):
                    ins = ts(qsc[:, 1, sign], rsq[:, 2], (1 - 2 * sign) * MQK ** -0.5, None, ALU.mult)
                link(ins)
                for j in range(6):
                    idx = 2 * j
                    dve.wait_ge(*s_hT.at(l, idx + 1))
                    rows, dst, gain = hT_dest(l, idx)
                    src = PS[0:rows, HT_BANK[idx], :].rearrange("p (h t) -> p h t", h=2)
                    if gain is None:
                        cp(dst, src).then_inc(s_hTv.sem, 1)
                    else:
                        ts(dst, src, gain, None, ALU.mult).then_inc(s_hTv.sem, 1)

                def maximum(m):
                    kind, hd = (0, m) if m < MAPS else (1, m - MAPS)
                    dve.wait_ge(*s_S.at(l, m + 1))
                    b = S_BANK[m % 4]
                    red_(mx[:, m, 0:1], PS[:, b, 0:P], AX.X, ALU.max)
                    link(red_(mx[:, m, 1:2], PS[:, b, P:3 * P], AX.X, ALU.max))
                    tt(nbias[:, m, :], mx[:, m, :], qsc[:, kind, 1, :, hd], ALU.mult).then_inc(s_nb.sem, 1)

                def output(m):
                    dve.wait_ge(*s_O.at(l, m + 1))
                    link(nc.vector.reciprocal(rinv[:, m, :], sums[:, m, :]))
                    b = O_BANK[m % 2]
                    if m < MAPS:
                        src = bank(b).rearrange("p (t n) -> p t n", t=TT)[:, :, 0:DV]
                        dst = ocat[:, :, 512 + DV * (m // 2):512 + DV * (m // 2 + 1)]
                        w = rinv[:, m, :].unsqueeze(2).broadcast_to([P, TT, DV])
                        if m % 2 == 0:
                            tt(dst, src, w, ALU.mult).then_inc(s_Oe.sem, 1)
                        else:
                            link(ts(rinv[:, m, :], rinv[:, m, :], neglam[:, l:l + 1], None, ALU.mult))
                            tmp = rtmp[:, 0:TT * DV].rearrange("p (t n) -> p t n", t=TT)
                            tt(tmp, src, w, ALU.mult).then_inc(s_Oe.sem, 1)
                            dve.wait_ge(*s_Oe.at(l, m + 1))
                            ins = tt(dst, dst, tmp, ALU.add)
                            if m == MAPS - 1:
                                ins.then_inc(s_od.sem, 1)
                            else:
                                link(ins)
                    else:
                        hd = m - MAPS
                        src = bank(b).rearrange("p (t n) -> p t n", t=TT)[:, :, 0:MV]
                        tt(ocat[:, :, MV * hd:MV * (hd + 1)], src, rinv[:, m, :].unsqueeze(2).broadcast_to([P, TT, MV]),
                           ALU.mult).then_inc(s_Oe.sem, 1)

                def sub_norm():
                    dve.wait_ge(*s_junk.at(l, 6))
                    red_(ods[:, :], junk.rearrange("p (h n) -> p h n", n=DV), AX.X, ALU.add).then_inc(s_sum.sem, 1)
                    dve.wait_ge(*s_sum.at(l, 6))
                    ts(ods[:, :], ods[:, :], 1.0 / DV, EPS, ALU.mult, ALU.add).then_inc(s_hms.sem, 1)

                def sub_scale():
                    dve.wait_ge(*s_hrs.at(l, 5))
                    o4 = ocat[:, :, 512:1024].rearrange("p t (h n) -> p t h n", h=DH)
                    r = odr[:, :].rearrange("p (t h) -> p t h", t=TT).unsqueeze(3).broadcast_to([P, TT, DH, DV])
                    return tt(o4, o4, r, ALU.mult)

                for i in range(16 + 2):
                    if i < 16:
                        maximum(i)
                    if 1 <= i <= 16 and (i - 1) % 2 == 0:
                        j = i - 1
                        dve.wait_ge(*s_T.at(l, j + 1))
                        if j >= 2:
                            dve.wait_ge(*s_O.at(l, j - 1))
                        cp(prT[:, 0, :], PS[:, 3, 0:384]).then_inc(s_Tv.sem, 1)
                    if i >= 2:
                        output(i - 2)
                    if i == MAPS + 5:
                        sub_norm()
                sub_scale().then_inc(s_oc.sem, 1)
                evac_pass(l, 1)
                for t in range(TT):
                    for c in range(2):
                        j = 2 * t + c
                        dve.wait_ge(*s_out.at(l, j + 1))
                        v = h[:, t, c * CB:(c + 1) * CB]
                        ins = tt(v, v, bank(4 + j), ALU.add)
                    ins.then_inc((s_h0 if t == 0 else s_h).sem, 1)
                norm(l, 1)
                evac_pass(l, 2)

                R = {k: v[:, :, :] for k, v in rt.items()}
                g4 = cst[:, C_G4:C_G4 + NG].unsqueeze(1).broadcast_to([P, TT, NG])
                e32 = cst[:, C_E32:C_E32 + NE].unsqueeze(1).broadcast_to([P, TT, NE])

                def wide(v, n):
                    return v.broadcast_to([P, TT, n])

                dve.wait_ge(*s_rl.at(l))
                link(tt(R["lg"], PS[:, 4, 0:TT * (NG + NE)].rearrange("p (t n) -> p t n", t=TT),
                        bias[:, l, :].unsqueeze(1).broadcast_to([P, TT, NG + NE]), ALU.add))
                lgg, lge = rt["lg"][:, :, 0:NG], rt["lg"][:, :, NG:NG + NE]
                link(red_(R["gmax"], lgg, AX.X, ALU.max))
                tt(R["gd"], lgg, wide(R["gmax"], NG), ALU.subtract).then_inc(s_ra.sem, 1)
                link(tt(R["geq"], lgg, wide(R["gmax"], NG), ALU.is_equal))
                link(stt(out=R["gc"], in0=R["geq"], scalar=-1000.0, in1=g4, op0=ALU.mult, op1=ALU.add))
                link(red_(R["gi"], R["gc"], AX.X, ALU.min))
                link(tt(R["goh"], R["gc"], wide(R["gi"], NG), ALU.is_equal))
                link(ts(R["pen"], R["goh"], 1e30, -1e30, ALU.mult, ALU.add))
                ml4 = R["ml"].rearrange("p t (g e) -> p t g e", g=NG)
                link(tt(ml4, lge.rearrange("p t (g e) -> p t g e", g=NG),
                        rt["pen"][:, :, :].unsqueeze(3).broadcast_to([P, TT, NG, NEG]), ALU.add))

                def top(src, m, eq, c, i, oh):
                    link(red_(R[m], src, AX.X, ALU.max))
                    link(tt(R[eq], src, wide(R[m], NE), ALU.is_equal))
                    link(stt(out=R[c], in0=R[eq], scalar=-1000.0, in1=e32, op0=ALU.mult, op1=ALU.add))
                    link(red_(R[i], R[c], AX.X, ALU.min))
                    link(tt(R[oh], R[c], wide(R[i], NE), ALU.is_equal))

                top(R["ml"], "m1", "eq", "c1", "i1", "oh1")
                link(stt(out=R["ml2"], in0=R["oh1"], scalar=-2e30, in1=R["ml"], op0=ALU.mult, op1=ALU.add))
                top(R["ml2"], "m2", "eq", "c2", "i2", "oh2")
                tt(R["dm"], R["m2"], R["m1"], ALU.subtract).then_inc(s_ra.sem, 1)
                for i, a in (("i1", "t1"), ("i2", "t2")):
                    link(ts(R[i], R[i], 1000.0, None, ALU.add))
                    link(tt(R[a], e32, wide(R[i], NE), ALU.is_gt))
                link(tt(R["Mpre"], R["t1"], R["t2"], ALU.add))
                tt(Mp[:, :], rt["Mpre"][:, 0, :], rt["Mpre"][:, 1, :], ALU.add)
                tt(R["M"], R["oh1"], R["oh2"], ALU.add).then_inc(s_M.sem, 1)
                dve.wait_ge(*s_re.at(l, 2))
                link(red_(R["gs"], R["ge"], AX.X, ALU.add))
                link(ts(R["den"], R["e2"], 1.0, None, ALU.add))
                link(tt(R["den"], R["den"], R["gs"], ALU.mult))
                link(nc.vector.reciprocal(R["w1"], R["den"]))
                link(tt(R["w2"], R["w1"], R["e2"], ALU.mult))
                dve.wait_ge(*s_pos.at(l))
                pos = PS[:, 5, 0:TT * NE].rearrange("p (t n) -> p t n", t=TT)
                for oh, t_, s in (("oh1", "t1", "s1"), ("oh2", "t2", "s2")):
                    link(tt(R[t_], R[oh], pos, ALU.mult))
                    link(red_(R[s], R[t_], AX.X, ALU.add))
                for t in range(TT):
                    link(ts(pdis[:, t, :], iota_slot, rt["s1"][:, t, :], None, ALU.is_equal))
                    ins = stt(out=pdis[:, t, :], in0=iota_slot, scalar=rt["s2"][:, t, :], in1=pdis[:, t, :].bitcast(F32),
                              op0=ALU.is_equal, op1=ALU.add)
                ins.then_inc(s_P.sem, 1)
                off, cnts = PS[:, 5, 2 * NE:3 * NE], PS[:, 5, 3 * NE:4 * NE]
                link(ts(cnt[:, 0, :], cnts, BLK + 0.5, 1.0, ALU.is_gt, ALU.add))
                link(stt(out=cnt[:, 1, :], in0=cnts, scalar=2 * BLK + 0.5, in1=cnt[:, 0, :], op0=ALU.is_gt, op1=ALU.add))
                link(stt(out=cnt[:, 2, :], in0=cnts, scalar=3 * BLK + 0.5, in1=cnt[:, 1, :], op0=ALU.is_gt, op1=ALU.add))
                per = cnt[:, 2, :]
                link(nc.vector.memset(pfx[:, :, :], 0.0))
                link(cp(pfx[:, 1, :], per))
                flat = pfx[:, :, :].rearrange("p a n -> p (a n)")
                at = NE
                for j in range(5):
                    to = NE + 2 * NE * ((j + 1) % 2)
                    link(tt(flat[:, to:to + NE], flat[:, at:at + NE], flat[:, at - 2 ** j:at + NE - 2 ** j], ALU.add))
                    at = to
                run = flat[:, at:at + NE]
                jcol = cst[:, C_J:C_J + 1]
                link(ts(boh[:, 0, :], run, jcol, None, ALU.is_le))
                link(red_(blk4[:, 3:4], boh[:, 0, :], AX.X, ALU.add))
                link(ts(boh[:, 1, :], cst[:, C_E32:C_E32 + NE], blk4[:, 3:4], None, ALU.is_equal))
                link(tt(boh[:, 2, :], run, per, ALU.subtract))
                link(stt(out=boh[:, 2, :], in0=boh[:, 2, :], scalar=-float(BLK), in1=off, op0=ALU.mult, op1=ALU.add))
                link(tt(boh[:, 2, :], boh[:, 2, :], boh[:, 1, :], ALU.mult))
                link(red_(blk4[:, 0:1], boh[:, 2, :], AX.X, ALU.add))
                link(stt(out=blk4[:, 0:1], in0=jcol, scalar=float(BLK), in1=blk4[:, 0:1], op0=ALU.mult, op1=ALU.add))
                link(ts(blk4[:, 0:1], blk4[:, 0:1], float(NSLOT), None, ALU.min))
                link(tt(boh[:, 3, :], boh[:, 1, :], cst[:, C_MOD:C_MOD + NE], ALU.mult))
                link(red_(blk4[:, 1:2], boh[:, 3, :], AX.X, ALU.add))
                ts(blk4[:, 2:3], blk4[:, 3:4], 1.0, None, ALU.add).then_inc(s_blk.sem, 1)
                link(ts(ctlef[:, 0:NE], run[0:1], carry[:, 0:1], None, ALU.add))
                cp(ctlef[:, NE:NE + 1], run[0:1, NE - 1:NE])
                link(cp(ctlef[:, NE + 1:NE + 2], carry[:, :]))
                link(ts(carry[:, :], run[0:1, NE - 1:NE], carry[:, 0:1], None, ALU.add))
                cp(ctle[:, :], ctlef[:, :])
                nc.vector.memset(ctl[:, 0:1], 0)
                for k in range(0, KD, 2):
                    dve.wait_ge(*s_disp.at(l, k + 1))
                    ts(mTs[:, k, 0:NSLOT], PS[:, DISP_BANK[k], :], g_in[:, l, 2, k:k + 1], None,
                       ALU.mult).then_inc(s_dv.sem, 1)
                dve.wait_ge(*s_blkT.at(l))
                cp(ctl[:, 1:1 + P], PS[0:4, 5, 4 * NE:4 * NE + P]).then_inc(s_ctl.sem, 1)
                for t in range(TT):
                    ts(GT[:, t, :], iota_slot, rt["s1"][:, t, :], rt["w1"][:, t, :], ALU.is_equal, ALU.mult)
                    link(ts(gtmp[:, t, :], iota_slot, rt["s2"][:, t, :], rt["w2"][:, t, :], ALU.is_equal, ALU.mult))
                tt(GT, GT, gtmp, ALU.add).then_inc(s_GT.sem, 1)
                dve.wait_ge(*s_GTt.at(l))
                cp(G.rearrange("p s t -> p (s t)"), bank(0, 2).rearrange("p b n -> p (b n)")).then_inc(s_Gc.sem, 1)
                dve.wait_ge(*s_ctl.at(l))
                dve.wait_ge(*s_da.at(l))
                blocks, before = block_counts(dve)


                def copy_y(m, chunks, more):
                    dve.wait_ge(s_ch, chunks + (CHUNKS + NBUF + more))
                    dve.wait_ge(s_D, m + 1)
                    cp(yraw, bank(6, 2).rearrange("p b n -> p (b n)")).then_inc(s_ye, 1)

                def place_y(m, j):
                    col = block_column(dve, j)
                    dve.wait_ge(s_D, m + 2)
                    cp(yTs[:, :, ds(col, BLK)],
                       bank(0, 2).rearrange("p b (k s) -> p (b k) s", s=2 * BLK)[:, :, 0:BLK]).then_inc(s_yc, 1)

                def low(turn, c, region):
                    dve.wait_ge(s_hi, turn.count(c))
                    low_part(nc.vector, 0, turn, c, region).then_inc(s_lod, 1)

                def hidden(at):
                    dve.wait_ge(s_silu, at)
                    tt(hb, sg, PS[:, 5, :].rearrange("p (q s) -> p q s", q=4)[:, KF:2 * KF, 0:BLK],
                       ALU.mult).then_inc(s_hs, 1)
                    dve.wait_ge(s_hs, at * 2 + 1)
                    cp(h_hl[:, :, 0:BLK], hb).then_inc(s_hs, 1)
                    dve.wait_ge(s_hs, at * 2 + 2)
                    tt(h_hl[:, :, BLK:2 * BLK], hb, h_hl[:, :, 0:BLK].bitcast(F32), ALU.subtract).then_inc(s_hl, 1)

                turn = Turn(before, Turn.FIRST)
                region = region_of(dve, 0)
                for c in range(GU):
                    low(turn, c, region)
                with dve.Fori(1, blocks) as j:
                    at = before + j
                    turn = Turn(at, Turn.INNER)
                    region = region_of(dve, j)
                    low(turn, 0, region)
                    low(turn, 1, region)
                    low(turn, 2, region)
                    copy_y(at + (l - 1), at * CHUNKS, GU - CHUNKS)
                    low(turn, 3, region)
                    hidden(at)
                    last_region = region_of(dve, j - 1)
                    low(turn, 4, last_region)
                    low(turn, 5, last_region)
                    place_y(at + (l - 1), j - 1)
                last = before + blocks
                copy_y(last + (l - 1), last * CHUNKS, GU - CHUNKS)
                hidden(last)
                last_region = region_of(dve, blocks - 1)
                for c in range(GU, CHUNKS):
                    low(Turn(last, Turn.LAST), c, last_region)
                place_y(last + (l - 1), blocks - 1)
                copy_y(last + l, last * CHUNKS, 0)
                place_y(last + l, blocks)
                dve.wait_ge(*s_pTt.at(l))
                cp(pT.rearrange("p k t -> p (k t)"), PS[:, 5, :]).then_inc(s_pTc.sem, 1)
                for j in range(4):
                    dve.wait_ge(*s_yT.at(l, 2 * j + 1))
                    cp(ys[:, j, 0:CB], PS[:, YT_BANK[2 * j], :]).then_inc(s_yv.sem, 1)
                for t in range(TT):
                    for c in range(2):
                        j = 2 * t + c
                        dve.wait_ge(*s_cmb.at(l, j + 1))
                        v = h[:, t, c * CB:(c + 1) * CB]
                        ins = tt(v, v, bank(4 + j), ALU.add)
                    ins.then_inc((s_h0 if t == 0 else s_h).sem, 1)
                norm(l, 2)
                evac_pass(l, 3)
                for t in range(TT):
                    for c in range(2):
                        j = 2 * t + c
                        dve.wait_ge(*s_sg.at(l, j + 1))
                        link(tt(prod[:, j, :], sig[:, j, :], bank(4 + j), ALU.mult))
                        v = h[:, t, c * CB:(c + 1) * CB]
                        tt(v, v, prod[:, j, :], ALU.add).then_inc(s_fin.sem, 1)
                dve.wait_ge(*s_fin.at(l))
                dve.sem_inc(s_h.sem, 1)

        @block.tensor
        def _(pe):
            mm = nc.tensor.matmul

            def used():
                pe.drain().then_inc(weights_used, 1)

            def tr(dst, src, rows=P):
                return pe.transpose(dst, src, ident[0:rows, 0:rows] if rows < P else ident)

            def transposed_pass(l, n_, src):
                for t in range(TT):
                    for k in range(KD):
                        b = k // 2
                        c = (k % 2) * SEQ + t * P
                        ins = tr(PS[:, b, c:c + P], src[:, t, k::KD])
                        if t == TT - 1 and k % 2 == 1:
                            ins.then_inc(s_tr.sem, 1)

            def aT_ready(l, n_):
                pe.wait_ge(*s_aTv.at(l, 2 * n_ + 2))
                pe.wait_ge(*s_aTs.at(l, 2 * n_ + 2))

            pe.wait_ge(loaded["const"], 16)
            for l in range(DEPTH):
                pe.wait_ge(*s_hn0.at(l, 1))
                pe.wait_ge(*s_hn1.at(l, 1))
                transposed_pass(l, 0, hn)
                aT_ready(l, 0)
                for c, b in enumerate((4, 6, 0, 2)):
                    item = ITEM[l, f"z{c}"]
                    n = SPLITS[c][1] - SPLITS[c][0]
                    w = slots(item, KD, n)
                    arrival(pe, item)
                    for t in range(TT):
                        for k in range(KD):
                            ins = mm(PS[:, b + t, 0:n], aT[:, k, t * P:(t + 1) * P], w[:, k, :], start=(k == 0),
                                     stop=(k == KD - 1))
                    ins.then_inc(s_z.sem, 1)
                    used()
                    if c == 2:
                        pe.wait_ge(*s_lat.at(l))
                        pe.wait_ge(*s_kr.at(l))
                        for t in range(TT):
                            for k in range(2):
                                tr(PS[:, 4, k * SEQ + t * P:k * SEQ + (t + 1) * P], lat[:, t, k:QR:2])
                            ins = tr(PS[:, 5, t * P:(t + 1) * P], lat[:, t, QR:QR + KVR])
                        ins.then_inc(s_lT.sem, 1)
                item = ITEM[l, "uq"]
                w = slots(item, 2, MH * MQK)
                arrival(pe, item)
                pe.wait_ge(*s_lTc.at(l))
                for t, b in enumerate((6, 0)):
                    pe.wait_ge(*(s_dq if t == 0 else s_dk).at(l))
                    for half in range(2):
                        for k in range(2):
                            ins = mm(PS[:, b + half, 0:4 * MQK], cqT[:, k, t * P:(t + 1) * P],
                                     w[:, k, half * 4 * MQK:(half + 1) * 4 * MQK], start=(k == 0), stop=(k == 1))
                    ins.then_inc(s_uq.sem, 1)
                used()
                item = ITEM[l, "ukv"]
                w = slots(item, 2, CB)
                arrival(pe, item)
                for t, b in enumerate((2, 4)):
                    if t == 0:
                        pe.wait_ge(*s_vd.at(l))
                    for half in range(2):
                        ins = mm(PS[:, b + half, :], ckvT[:, t * P:(t + 1) * P], w[:, half, :], start=True, stop=True)
                    ins.then_inc(s_ukv.sem, 1)
                used()
                for idx in range(12):
                    b = HT_BANK[idx]
                    if idx == 0:
                        pe.wait_ge(*s_qr.at(l, 1))
                        pe.wait_ge(*s_qn.at(l, 1))
                    if idx == 2:
                        pe.wait_ge(*s_qr.at(l, 2))
                        pe.wait_ge(*s_qn.at(l, 2))
                    if idx == 4:
                        pe.wait_ge(*s_kn.at(l, 2))
                        pe.wait_ge(*s_vm.at(l, 2))
                    if idx == 8:
                        pe.wait_ge(*s_kpe.at(l, 2))
                        pe.wait_ge(*s_hTv.at(l, 2))
                        pe.wait_ge(*s_hTs.at(l, 2))
                    for j in range(2):
                        for t in range(TT):
                            c = j * SEQ + t * P
                            if idx < 4:
                                hd = 2 * (idx % 2) + j
                                src = (dqr if idx < 2 else dkr)[:, t, hd * P:(hd + 1) * P]
                                ins = tr(PS[:, b, c:c + P], src)
                            else:
                                hd = 2 * ((idx - 4) % 4) + j
                                src = (qm if idx < 8 else km)[:, t, hd * MQK:(hd + 1) * MQK]
                                ins = tr(PS[0:MQK, b, c:c + P], src)
                    ins.then_inc(s_hT.sem, 1)
                pe.wait_ge(*s_hTv.at(l))
                pe.wait_ge(*s_hTs.at(l))

                def scores(m):
                    if m >= 4:
                        pe.wait_ge(*s_exp.at(l, m - 3))
                    b = S_BANK[m % 4]
                    if m < MAPS:
                        r = slice((m % 2) * DHD, (m % 2 + 1) * DHD)
                        q, k = qTd[r, m // 2, :], kTd[r, m // 2, :]
                        rows = r
                    else:
                        rows = slice(0, MQK)
                        q, k = qTm[rows, m - MAPS, :], kTm[rows, m - MAPS, :]
                    mu, mv = cst[rows, C_MU:C_MU + P], cst[rows, C_MV:C_MV + CHUNK]
                    for t in range(TT):
                        a = t * P
                        n = (t + 1) * P
                        mm(PS[:, b, a:a + n], q[:, t * P:(t + 1) * P], k[:, 0:n], start=True, stop=False)
                        ins = mm(PS[:, b, a + n - CHUNK:a + n], mu, mv, start=False, stop=True)
                    ins.then_inc(s_S.sem, 1)

                def turn(m):
                    pe.wait_ge(*s_exp.at(l, m + 1))
                    if m >= 2:
                        pe.wait_ge(*(s_Tv if m % 2 == 0 else s_Ts).at(l, m // 2))
                    for j in range(3):
                        ins = tr(PS[:, T_BANK[m % 2], j * P:(j + 1) * P], prb[:, m % 2, j * P:(j + 1) * P])
                    ins.then_inc(s_T.sem, 1)

                def values(m):
                    pe.wait_ge(*(s_Tv if m % 2 == 0 else s_Ts).at(l, m // 2 + 1))
                    if m >= 2:
                        pe.wait_ge(*s_Oe.at(l, m - 1))
                    b = O_BANK[m % 2]
                    if m < MAPS:
                        n = DV
                        v = [vd[:, t, (m // 2) * DV:(m // 2 + 1) * DV] for t in range(TT)]
                    else:
                        n = MV
                        v = [vm[:, t, (m - MAPS) * MV:(m - MAPS + 1) * MV] for t in range(TT)]
                    w = prT[:, m % 2, :]
                    mm(PS[:, b, 0:n], w[:, 0:P], v[0], start=True, stop=True)
                    mm(PS[:, b, SEQ:SEQ + n], w[:, P:2 * P], v[0], start=True, stop=False)
                    mm(PS[:, b, SEQ:SEQ + n], w[:, 2 * P:3 * P], v[1], start=False, stop=True).then_inc(s_O.sem, 1)

                for i in range(16 + 2):
                    if i < 16:
                        scores(i)
                    if 1 <= i <= 16:
                        turn(i - 1)
                    if i >= 2:
                        values(i - 2)
                pe.wait_ge(*s_oc.at(l))
                transposed_pass(l, 1, ocat)
                aT_ready(l, 1)
                for c in range(2):
                    arrival(pe, ITEM[l, f"out{c}"])
                for t in range(TT):
                    for c in range(2):
                        w = slots(ITEM[l, f"out{c}"], KD, CB)
                        for k in range(KD):
                            ins = mm(bank(4 + 2 * t + c), aT[:, k, t * P:(t + 1) * P], w[:, k, :], start=(k == 0),
                                     stop=(k == KD - 1))
                        ins.then_inc(s_out.sem, 1)
                used()
                used()
                pe.wait_ge(*s_hn0.at(l, 2))
                pe.wait_ge(*s_hn1.at(l, 2))
                transposed_pass(l, 2, hn)
                aT_ready(l, 2)
                for t in range(TT):
                    for k in range(KD):
                        ins = mm(PS[:, 4, t * (NG + NE):(t + 1) * (NG + NE)], aT[:, k, t * P:(t + 1) * P], w_rt[:, l, k, :],
                                 start=(k == 0), stop=(k == KD - 1))
                ins.then_inc(s_rl.sem, 1)
                pe.wait_ge(*s_M.at(l))
                M0, M1 = rt["M"][:, 0, :], rt["M"][:, 1, :]
                mm(PS[:, 5, 0:NE], ones, Mp[:, :], start=True, stop=False)
                mm(PS[:, 5, 0:NE], tri, M0, start=False, stop=True)
                mm(PS[:, 5, NE:2 * NE], ones, Mp[:, :], start=True, stop=False)
                mm(PS[:, 5, NE:2 * NE], ones, M0, start=False, stop=False)
                mm(PS[:, 5, NE:2 * NE], tri, M1, start=False, stop=True)
                mm(PS[:, 5, 2 * NE:3 * NE], ones, Mp[:, :], start=True, stop=True)
                mm(PS[:, 5, 3 * NE:4 * NE], ones, M0, start=True, stop=False)
                mm(PS[:, 5, 3 * NE:4 * NE], ones, M1, start=False, stop=True).then_inc(s_pos.sem, 1)
                pe.wait_ge(*s_P.at(l))
                pe.wait_ge(*s_tl.at(l))
                for k in range(KD):
                    if k == 7:
                        pe.wait_ge(*s_dv.at(l, 1))
                    for t in range(TT):
                        for half in range(2):
                            ins = mm(bank(DISP_BANK[k]), tok_hl[half][:, t, k::KD], pdis[:, t, :],
                                     start=(t == 0 and half == 0), stop=(t == TT - 1 and half == 1))
                    ins.then_inc(s_disp.sem, 1)
                pe.wait_ge(*s_blk.at(l))
                tr(PS[0:4, 5, 4 * NE:4 * NE + P], blk4[:, :]).then_inc(s_blkT.sem, 1)
                pe.wait_ge(*s_GT.at(l))
                pe.wait_ge(*s_dv.at(l))
                pe.wait_ge(*s_da.at(l))
                for s in range(4):
                    for t in range(TT):
                        c = (s % 2) * SEQ + t * P
                        ins = tr(PS[:, s // 2, c:c + P], GT[:, t, s * P:(s + 1) * P])
                ins.then_inc(s_GTt.sem, 1)
                pe.wait_ge(*s_ctl.at(l))
                pe.wait_ge(*s_Gc.at(l))
                blocks, before = block_counts(pe)


                def chunk(turn, c):
                    pe.wait_ge(s_lod, turn.count(c))
                    pe.wait_ge(s_lop, turn.count(c))
                    for n in range(2):
                        for half, w in enumerate((w_hi, w_lo)):
                            if c < GU:
                                v = part_chunk(turn, w, c)[:, :, n * FF:(n + 1) * FF]
                                ins = mm(PS[:, 4, :], x_hl[:, 2 * c + n, :], v, start=(c == 0 and n == 0 and half == 0),
                                         stop=(c == GU - 1 and n == 1 and half == 1))
                            else:
                                v = part_chunk(turn, w, c)[:, 0, n * CB:(n + 1) * CB]
                                ins = mm(PS[:, 6 + n, :], h_hl[:, c - GU, :], v, start=(c == GU and half == 0),
                                         stop=(c == CHUNKS - 1 and half == 1))
                    ins.then_inc(s_ch, 1)

                pair = cst[:, C_II:C_II + P]

                def gate_up(turn, m):
                    pe.wait_ge(s_xl, m + 1)
                    for c in range(GU):
                        chunk(turn, c)

                def down(turn):
                    pe.wait_ge(s_hl, turn.at)
                    for c in range(GU, CHUNKS):
                        chunk(turn, c)

                def turn_gu(at):
                    pe.wait_ge(s_gue, at + 1)
                    for q in range(2 * KF):
                        ins = mm(PS[:, 5, q * P:(q + 1) * P], gur[:, q * P:(q + 1) * P], pair, start=True, stop=True)
                    ins.then_inc(s_B, 1)

                def turn_y(m):
                    pe.wait_ge(s_ye, m + 1)
                    pe.wait_ge(s_yc, m + 1)
                    for d in range(KD):
                        ins = mm(PS[:, d // 4, d % 4 * P:(d % 4 + 1) * P], yraw[:, d * P:(d + 1) * P], pair,
                                 start=True, stop=True)
                    ins.then_inc(s_D, 1)

                gate_up(Turn(before, Turn.FIRST), before + l)
                turn_gu(before)
                with pe.Fori(1, blocks) as j:
                    at = before + j
                    turn = Turn(at, Turn.INNER)
                    gate_up(turn, at + l)
                    turn_y(at + (l - 1))
                    down(turn)
                    turn_gu(at)
                last = before + blocks
                turn_y(last + (l - 1))
                down(Turn(last, Turn.LAST))
                turn_y(last + l)
                pe.wait_ge(s_Gl.sem, 16 * (l + 1))
                for k in range(2):
                    for t in range(TT):
                        ins = tr(PS[:, 5, k * SEQ + t * P:k * SEQ + (t + 1) * P], pin[:, t, k::2])
                ins.then_inc(s_pTt.sem, 1)
                pe.wait_ge(s_yc, last + (l + 2))
                for j in range(8):
                    if j >= 6:
                        pe.wait_ge(*(s_yv if j == 6 else s_ya).at(l, 1))
                    s, half = j // 2, j % 2
                    for d in range(4):
                        ins = tr(PS[:, YT_BANK[j], d * P:(d + 1) * P], yTs[:, half * 4 + d, s * P:(s + 1) * P])
                    ins.then_inc(s_yT.sem, 1)
                pe.wait_ge(*s_yv.at(l))
                pe.wait_ge(*s_ya.at(l))
                pe.wait_ge(*s_pTc.at(l))
                for t in range(TT):
                    for c in range(2):
                        for s in range(4):
                            ins = mm(bank(4 + 2 * t + c), G[:, s, t * P:(t + 1) * P], ys[:, s, c * CB:(c + 1) * CB],
                                     start=(s == 0), stop=(s == 3))
                        ins.then_inc(s_cmb.sem, 1)
                pe.wait_ge(*s_h.at(l, 2))
                item = ITEM[l, "proj"]
                w = slots(item, 2, D)
                arrival(pe, item)
                for t in range(TT):
                    for c in range(2):
                        for k in range(2):
                            ins = mm(bank(4 + 2 * t + c), pT[:, k, t * P:(t + 1) * P], w[:, k, c * CB:(c + 1) * CB],
                                     start=(k == 0), stop=(k == 1))
                used()
                pe.wait_ge(*s_hn0.at(l, 3))
                pe.wait_ge(*s_hn1.at(l, 3))
                transposed_pass(l, 3, hn)
                aT_ready(l, 3)
                for c in range(2):
                    arrival(pe, ITEM[l, f"gate{c}"])
                for t in range(TT):
                    for c in range(2):
                        w = slots(ITEM[l, f"gate{c}"], KD, CB)
                        for k in range(KD):
                            ins = mm(bank(2 * t + c), aT[:, k, t * P:(t + 1) * P], w[:, k, :], start=(k == 0),
                                     stop=(k == KD - 1))
                        ins.then_inc(s_gt.sem, 1)
                used()
                used()


_INS = ["x", "p", "positions", "attn_norm", "w_in", "q_a_norm", "w_uq", "kv_a_norm", "w_ukv", "mla_q_norm",
        "mla_k_norm", "diff_q_norm", "diff_k_norm", "lambda_q1", "lambda_k1", "lambda_q2", "lambda_k2", "diff_subln",
        "w_out", "ffn_norm", "w_group", "b_group", "w_router", "b_router", "w_gate", "w_up", "w_down", "ple_norm",
        "w_ple_gate", "w_ple_proj"]


def kernel(**inputs):
    import numpy as _np
    import concourse.bacc as _bacc
    from concourse import mybir as _mybir
    from concourse.bass_utils import run_bass_kernel_spmd as _run

    nc = _bacc.Bacc("TRN2", target_bir_lowering=False, num_devices=1)
    arrays, args = {}, []
    for name in _INS:
        a = _np.ascontiguousarray(inputs[name])
        arrays[f"in_{name}"] = a
        args.append(nc.dram_tensor(f"in_{name}", a.shape, _mybir.dt.from_np(a.dtype), kind="ExternalInput").ap())
    const = constants()
    arrays["in_const"] = const
    args.append(nc.dram_tensor("in_const", const.shape, _mybir.dt.float32, kind="ExternalInput").ap())
    args.append(nc.dram_tensor("out_0", (1, SEQ, D), _mybir.dt.float32, kind="ExternalOutput").ap())
    trunk_kernel(nc, *args)
    r = _run(nc, [arrays], core_ids=[0])
    return r.results[0]["out_0"]
```
